# Optimizing a Trainium2 kernel written in Bass

```python
import jax, jax.numpy as jnp
from jax import lax
import numpy as np

D_MODEL = 1024
BATCH = 1
SEQ = 256
DEPTH = 2
DEC_BATCH = 8
DEC_SEQ = 1
PAST_LEN = 2048
PAGE_SIZE = 128

SSM_HEAD_DIM = 64
SSM_INNER = D_MODEL
SSM_HEADS = SSM_INNER // SSM_HEAD_DIM
SSM_GROUPS = 2
SSM_STATE = 128
CONV_WIDTH = 4
CONV_DIM = SSM_INNER + 2 * SSM_GROUPS * SSM_STATE
SSD_CHUNK = 128
CMLP_WIDTH = D_MODEL
CMLP_GROUPS = 8
CMLP_GROUP_DIM = CMLP_WIDTH // CMLP_GROUPS
CMLP_CHUNK = 128
FFN_DIM = 2816
N_EXPERTS = 8
TOP_K = 2
EPS = 1e-6
IN_SIZES = (SSM_INNER, CONV_DIM, SSM_HEADS, CMLP_WIDTH, CMLP_WIDTH, D_MODEL, D_MODEL)
IN_DIM = SSM_INNER + CONV_DIM + SSM_HEADS + 2 * CMLP_WIDTH + 2 * D_MODEL

kernel_name = 'hybrid_ssd_chunkmlp_moe_step'

def split_cols(a, sizes):
    idx, acc = [], 0
    for s in sizes[:-1]:
        acc += s
        idx.append(acc)
    return jnp.split(a, idx, axis=-1)

def rmsnorm(x, g):
    xf = x.astype(jnp.float32)
    y = xf * lax.rsqrt(jnp.mean(xf * xf, axis=-1, keepdims=True) + EPS)
    return (y * g.astype(jnp.float32)).astype(x.dtype)

def layernorm(x, g, b):
    xf = x.astype(jnp.float32)
    mu = jnp.mean(xf, axis=-1, keepdims=True)
    xc = xf - mu
    y = xc * lax.rsqrt(jnp.mean(xc * xc, axis=-1, keepdims=True) + EPS)
    return (y * g.astype(jnp.float32) + b.astype(jnp.float32)).astype(x.dtype)

def causal_dwconv(x, conv_state, w, b):
    L = x.shape[1]
    xp = jnp.concatenate([conv_state.astype(x.dtype), x], axis=1)
    y = b + sum(xp[:, k:k + L] * w[k] for k in range(CONV_WIDTH))
    return y, xp[:, L:]

def ssd_scan(x, dt, a, bm, cm, h0):
    Bsz, L = x.shape[:2]
    G, N, P = SSM_GROUPS, SSM_STATE, SSM_HEAD_DIM
    R = SSM_HEADS // G
    Q = SSD_CHUNK if L % SSD_CHUNK == 0 else L
    nc = L // Q
    f32 = jnp.float32
    xs = x.astype(f32).reshape(Bsz, nc, Q, G, R, P).transpose(1, 0, 2, 3, 4, 5)
    dts = dt.astype(f32).reshape(Bsz, nc, Q, G, R).transpose(1, 0, 2, 3, 4)
    bs = bm.astype(f32).reshape(Bsz, nc, Q, G, N).transpose(1, 0, 2, 3, 4)
    cs = cm.astype(f32).reshape(Bsz, nc, Q, G, N).transpose(1, 0, 2, 3, 4)
    ar = a.astype(f32).reshape(G, R)
    causal = jnp.tril(jnp.ones((Q, Q), bool))[None, :, :, None, None]

    def step(h, inp):
        xc, dtc, bc, cc = inp
        cum = jnp.cumsum(dtc * ar, axis=1)
        seg = cum[:, :, None] - cum[:, None, :]
        decay = jnp.exp(jnp.where(causal, seg, -jnp.inf))
        cb = jnp.einsum('btgn,bsgn->btsg', cc, bc)
        mix = cb[..., None] * decay * dtc[:, None]
        y_in = jnp.einsum('btsgr,bsgrp->btgrp', mix, xc)
        y_st = jnp.einsum('btgn,bgrpn->btgrp', cc, h) * jnp.exp(cum)[..., None]
        last = cum[:, -1]
        w_end = jnp.exp(last[:, None] - cum) * dtc
        h_new = h * jnp.exp(last)[..., None, None] + jnp.einsum('bsgn,bsgr,bsgrp->bgrpn', bc, w_end, xc)
        return h_new, y_in + y_st

    h0g = h0.astype(f32).reshape(Bsz, G, R, P, N)
    hT, ys = lax.scan(step, h0g, (xs, dts, bs, cs))
    y = ys.transpose(1, 0, 2, 3, 4, 5).reshape(Bsz, L, SSM_HEADS, P)
    return y, hT.reshape(Bsz, SSM_HEADS, P, N)

def ssd_branch(z, xbc, dt_raw, conv_state, h0, conv_w, conv_b, dt_bias, a_log, d_skip, norm_g):
    Bsz, L = z.shape[:2]
    xbc_c, conv_new = causal_dwconv(xbc, conv_state, conv_w, conv_b)
    xbc_c = jax.nn.silu(xbc_c)
    xs, bm, cm = jnp.split(xbc_c, [SSM_INNER, SSM_INNER + SSM_GROUPS * SSM_STATE], axis=-1)
    xs = xs.reshape(Bsz, L, SSM_HEADS, SSM_HEAD_DIM)
    bm = bm.reshape(Bsz, L, SSM_GROUPS, SSM_STATE)
    cm = cm.reshape(Bsz, L, SSM_GROUPS, SSM_STATE)
    dt = jax.nn.softplus(dt_raw.astype(jnp.float32) + dt_bias.astype(jnp.float32))
    a = -jnp.exp(a_log.astype(jnp.float32))
    y, h_new = ssd_scan(xs, dt, a, bm, cm, h0)
    y = y + d_skip.astype(jnp.float32)[:, None] * xs.astype(jnp.float32)
    y = y.reshape(Bsz, L, SSM_INNER) * jax.nn.silu(z.astype(jnp.float32))
    yg = y.reshape(Bsz, L, SSM_GROUPS, SSM_INNER // SSM_GROUPS)
    yg = yg * lax.rsqrt(jnp.mean(yg * yg, axis=-1, keepdims=True) + EPS)
    y = yg.reshape(Bsz, L, SSM_INNER) * norm_g.astype(jnp.float32)
    return y.astype(z.dtype), h_new.astype(h0.dtype), conv_new.astype(conv_state.dtype)

def chunk_mlp_branch(u, v, ln_g, ln_b, w_sp, b_sp):
    Bsz, L = u.shape[:2]
    v = layernorm(v, ln_g, ln_b)
    Q = CMLP_CHUNK if L % CMLP_CHUNK == 0 else L
    nc = L // Q
    w = jnp.where(jnp.tril(jnp.ones((Q, Q), bool))[None], w_sp[:, :Q, :Q], 0)
    vc = v.reshape(Bsz, nc, Q, CMLP_GROUPS, CMLP_GROUP_DIM)
    s = jnp.einsum('gts,bcsgd->bctgd', w, vc) + b_sp[:, :Q].T[None, None, :, :, None]
    return u * s.reshape(Bsz, L, CMLP_WIDTH), v

def swiglu(h, wg, wu, wd):
    return (jax.nn.silu(h @ wg) * (h @ wu)) @ wd

def moe_swiglu(h, w_router, b_router, wg, wu, wd):
    logits = (h @ w_router + b_router).astype(jnp.float32)
    top_val, top_idx = lax.top_k(logits, TOP_K)
    probs = jax.nn.softmax(top_val, axis=-1)
    combine = jnp.sum(jax.nn.one_hot(top_idx, N_EXPERTS, dtype=jnp.float32) * probs[..., None], axis=-2)
    combine = combine.astype(h.dtype)
    out = jnp.zeros_like(h)
    for e in range(N_EXPERTS):
        out = out + combine[..., e:e + 1] * swiglu(h, wg[e], wu[e], wd[e])
    return out

def run_group(x, c, ssm0, conv0, W):
    ssm_new, conv_new, v_rows = [], [], []
    for l in range(DEPTH):
        mod = jax.nn.silu(c) @ W['w_mod'][l] + W['b_mod'][l]
        sh1, sc1, g1, sh2, sc2, g2 = [t[:, None, :] for t in jnp.split(mod, 6, axis=-1)]
        h = rmsnorm(x, W['mix_pre_g'][l]) * (1 + sc1) + sh1
        z, xbc, dt_raw, u, v, ga, gb = split_cols(h @ W['w_in'][l], IN_SIZES)
        ya, hs, cs = ssd_branch(z, xbc, dt_raw, conv0[l], ssm0[l], W['conv_w'][l], W['conv_b'][l],
                                W['dt_bias'][l], W['a_log'][l], W['d_skip'][l], W['ssm_norm_g'][l])
        yb, vr = chunk_mlp_branch(jax.nn.gelu(u), jax.nn.gelu(v), W['cmlp_ln_g'][l], W['cmlp_ln_b'][l],
                                  W['w_spatial'][l], W['b_spatial'][l])
        merged = jax.nn.sigmoid(ga) * (ya @ W['w_ssd_out'][l]) + jax.nn.sigmoid(gb) * (yb @ W['w_cmlp_out'][l])
        x = x + g1 * rmsnorm(merged @ W['w_o'][l], W['mix_post_g'][l])
        h = rmsnorm(x, W['ffn_pre_g'][l]) * (1 + sc2) + sh2
        j = l // 2
        if l % 2 == 0:
            f = swiglu(h, W['ffn_wg'][j], W['ffn_wu'][j], W['ffn_wd'][j])
        else:
            f = moe_swiglu(h, W['router_w'][j], W['router_b'][j], W['exp_wg'][j], W['exp_wu'][j], W['exp_wd'][j])
        x = x + g2 * rmsnorm(f, W['ffn_post_g'][l])
        ssm_new.append(hs)
        conv_new.append(cs)
        v_rows.append(vr)
    return x, jnp.stack(ssm_new), jnp.stack(conv_new), jnp.stack(v_rows)

def setup_inputs(seed: int = 0) -> dict:
    key = jax.random.key(seed)
    keys = iter(jax.random.split(key, 48))
    f32 = jnp.float32

    def nrm(shape, scale):
        return jax.random.normal(next(keys), shape, f32) * scale

    def gain(shape):
        return 1.0 + nrm(shape, 0.1)

    n_dense = (DEPTH + 1) // 2
    n_moe = DEPTH // 2
    d = D_MODEL
    inp = {}
    inp['x_prompt'] = nrm((BATCH, SEQ, d), 1.0)
    inp['x_sample'] = nrm((DEC_BATCH, DEC_SEQ, d), 1.0)
    inp['state_ssm'] = nrm((DEPTH, DEC_BATCH, SSM_HEADS, SSM_HEAD_DIM, SSM_STATE), 0.1)
    inp['state_conv'] = nrm((DEPTH, DEC_BATCH, CONV_WIDTH - 1, CONV_DIM), 1.0)
    inp['c_prompt'] = nrm((BATCH, d), 1.0)
    inp['c_sample'] = nrm((DEC_BATCH, d), 1.0)
    inp['w_mod'] = nrm((DEPTH, d, 6 * d), 0.5 * d ** -0.5)
    inp['b_mod'] = nrm((DEPTH, 6 * d), 0.02)
    inp['mix_pre_g'] = gain((DEPTH, d))
    inp['mix_post_g'] = gain((DEPTH, d))
    inp['ffn_pre_g'] = gain((DEPTH, d))
    inp['ffn_post_g'] = gain((DEPTH, d))
    inp['w_in'] = nrm((DEPTH, d, IN_DIM), d ** -0.5)
    inp['conv_w'] = nrm((DEPTH, CONV_WIDTH, CONV_DIM), CONV_WIDTH ** -0.5)
    inp['conv_b'] = nrm((DEPTH, CONV_DIM), 0.02)
    dt0 = jnp.exp(jax.random.uniform(next(keys), (DEPTH, SSM_HEADS), f32, np.log(1e-3), np.log(1e-1)))
    inp['dt_bias'] = dt0 + jnp.log(-jnp.expm1(-dt0))
    inp['a_log'] = jnp.log(jax.random.uniform(next(keys), (DEPTH, SSM_HEADS), f32, 1.0, 16.0))
    inp['d_skip'] = gain((DEPTH, SSM_HEADS))
    inp['ssm_norm_g'] = gain((DEPTH, SSM_INNER))
    inp['w_ssd_out'] = nrm((DEPTH, SSM_INNER, d), SSM_INNER ** -0.5)
    inp['cmlp_ln_g'] = gain((DEPTH, CMLP_WIDTH))
    inp['cmlp_ln_b'] = nrm((DEPTH, CMLP_WIDTH), 0.02)
    inp['w_spatial'] = nrm((DEPTH, CMLP_GROUPS, CMLP_CHUNK, CMLP_CHUNK), CMLP_CHUNK ** -0.5)
    inp['b_spatial'] = gain((DEPTH, CMLP_GROUPS, CMLP_CHUNK))
    inp['w_cmlp_out'] = nrm((DEPTH, CMLP_WIDTH, d), CMLP_WIDTH ** -0.5)
    inp['w_o'] = nrm((DEPTH, d, d), d ** -0.5)
    inp['ffn_wg'] = nrm((n_dense, d, FFN_DIM), d ** -0.5)
    inp['ffn_wu'] = nrm((n_dense, d, FFN_DIM), d ** -0.5)
    inp['ffn_wd'] = nrm((n_dense, FFN_DIM, d), FFN_DIM ** -0.5)
    inp['router_w'] = nrm((n_moe, d, N_EXPERTS), d ** -0.5)
    inp['router_b'] = nrm((n_moe, N_EXPERTS), 0.01)
    inp['exp_wg'] = nrm((n_moe, N_EXPERTS, d, FFN_DIM), d ** -0.5)
    inp['exp_wu'] = nrm((n_moe, N_EXPERTS, d, FFN_DIM), d ** -0.5)
    inp['exp_wd'] = nrm((n_moe, N_EXPERTS, FFN_DIM, d), FFN_DIM ** -0.5)
    return inp

def reference(x_prompt, x_sample, state_ssm, state_conv, c_prompt, c_sample, w_mod, b_mod,
              mix_pre_g, mix_post_g, ffn_pre_g, ffn_post_g, w_in, conv_w, conv_b, dt_bias, a_log,
              d_skip, ssm_norm_g, w_ssd_out, cmlp_ln_g, cmlp_ln_b, w_spatial, b_spatial, w_cmlp_out,
              w_o, ffn_wg, ffn_wu, ffn_wd, router_w, router_b, exp_wg, exp_wu, exp_wd):
    W = dict(w_mod=w_mod, b_mod=b_mod, mix_pre_g=mix_pre_g, mix_post_g=mix_post_g,
             ffn_pre_g=ffn_pre_g, ffn_post_g=ffn_post_g, w_in=w_in, conv_w=conv_w, conv_b=conv_b,
             dt_bias=dt_bias, a_log=a_log, d_skip=d_skip, ssm_norm_g=ssm_norm_g, w_ssd_out=w_ssd_out,
             cmlp_ln_g=cmlp_ln_g, cmlp_ln_b=cmlp_ln_b, w_spatial=w_spatial, b_spatial=b_spatial,
             w_cmlp_out=w_cmlp_out, w_o=w_o, ffn_wg=ffn_wg, ffn_wu=ffn_wu, ffn_wd=ffn_wd,
             router_w=router_w, router_b=router_b, exp_wg=exp_wg, exp_wu=exp_wu, exp_wd=exp_wd)
    nb = x_prompt.shape[0]
    ssm0 = jnp.zeros((DEPTH, nb, SSM_HEADS, SSM_HEAD_DIM, SSM_STATE), x_prompt.dtype)
    conv0 = jnp.zeros((DEPTH, nb, CONV_WIDTH - 1, CONV_DIM), x_prompt.dtype)
    y_prompt, ssm_p, conv_p, _ = run_group(x_prompt, c_prompt, ssm0, conv0, W)
    y_sample, ssm_s, conv_s, v_s = run_group(x_sample, c_sample, state_ssm, state_conv, W)
    return (y_prompt, y_sample, ssm_p, conv_p, ssm_s, conv_s, v_s)


_drawn_inputs = setup_inputs


def setup_inputs(seed=0):
    import zlib

    import numpy as np

    out = dict(_drawn_inputs(seed))
    spreads = {}
    factors = {'cmlp_ln_b': 2.789, 'router_b': 5.433}
    for name, (base, spread) in spreads.items():
        noise = np.random.default_rng([zlib.crc32(name.encode()), seed]).standard_normal(out[name].shape)
        drawn = base * np.exp(spread * noise) if base else spread * noise
        out[name] = __import__('jax').numpy.asarray(drawn.astype(out[name].dtype))
    for name, factor in factors.items():
        out[name] = (out[name] * factor).astype(out[name].dtype)
    return out
```

```python
from contextlib import ExitStack

import concourse.bass as bass
from concourse import mybir

F32 = mybir.dt.float32
F32R = mybir.dt.float32r
ALU = mybir.AluOpType
ACT = mybir.ActivationFunctionType
AX = mybir.AxisListType

P = 128
MT = 2
CW = MT * P

SEMAPHORES = """params_in ctok_zero c_in x_in states_in ident_zero consts ones_ready
c_silu c_turned cst_zero c_hi c_lo mt_ready folded mod_added params_turned params_ready state_turned state_ready x_turned x_ready
raw_full0 raw_full1 raw_full2 hi_ready lo_ready w_used acc_free0 acc_free1
sq_ready ssq_ready inv_ready rs_ready h_ready xs_hi xs_lo mod_ready a_exp
conv_done xc_ready tail_turned tail_ready tail_out
dt_biased dt_abs dt_exp dt_ready a_scaled cum_ready samp_decay spread_ready spread_copied
tok_turned tok_ready x_tok b_tok xdt_ready bt_ready cb_ready cbm_ready cumb_ready seg_ready ce_exp
last_ready wend_arg wend_ready mix_exp mix_ready ce_ready xw_ready y_part y_taken st_part st_ready
st_turned st_copied st_out
bc_turned bc_ready bc_spread s_in0 s_in1 s_new s_out0 s_out1 samp_used samp_done
gate_sq gate_ssq gate_inv gate_rs
v_sum v_centered v_sq v_ssq v_inv v_rs v_normed vs_turned vs_copied vs_out v_tok v_tok_ready
w_sp_in w_turned w_ready sp_in diag_ready sp_bcast sp_bcast_ready sp_out sp_taken
sg_ready gu_ready g_hi route_in logits_ready route_exp route_done combine_turned combine_ready
combine_spread combine_spread_ready
route_arg y_normed merged y_turned y_copied y_out conv_keep dve_chain""".split()


def hybrid_ssd_chunkmlp_moe_step(nc, A, O):
    D = A["x_prompt"].shape[2]
    S = A["x_prompt"].shape[1]
    B = A["x_sample"].shape[0]
    L = A["w_in"].shape[0]
    T = S + B
    KT = D // P
    H = A["a_log"].shape[1]
    HD = D // H
    NS = A["state_ssm"].shape[-1]
    CD = A["conv_w"].shape[2]
    CT = CD // P
    CK = A["conv_w"].shape[1]
    G = (CD - D) // (2 * NS)
    R = H // G
    F = A["ffn_wg"].shape[2]
    FT = F // P
    E = A["exp_wg"].shape[1]
    Q = 128
    NQ = S // Q
    EPS = 1e-6
    NC = B + 2
    CL = 32
    R3 = 3
    assert D == 1024 and T % 2 == 0 and NS == P and 2 * HD == P and F % CW == 0 and NQ == 2 and B == E == 8

    IN_COL = {"xbc": D, "z": 0}
    at = D + CD + H
    for name in ("u", "v", "ga", "gb"):
        IN_COL[name] = at
        at += D
    IN_CHUNKS = {"xbc": CD // CW, "z": D // CW, "u": D // CW, "v": D // CW, "ga": D // CW, "gb": D // CW}
    KG = [(k, min(KT, FT - k)) for k in range(0, FT, KT)]

    N0, Q0 = {}, {}
    n = q = 0

    def phase(key, chunks, groups):
        nonlocal n, q
        N0[key], Q0[key] = n, q
        n += chunks
        q += groups

    phase("mod", L * 6 * KT // MT, 0)
    M3 = n // R3
    for l in range(L):
        for name in ("xbc", "dt", "z", "u", "v", "ga", "gb"):
            k = IN_CHUNKS.get(name, 1)
            phase((name, l), k, k)
        for name in ("ssd_out", "cmlp_out", "w_o"):
            phase((name, l), KT // MT, KT // MT)
        for e in range(1 if l % 2 == 0 else E):
            phase(("gu", l, e), 2 * FT // MT, 2 * FT // MT)
            phase(("wd", l, e), len(KG) * KT // MT, KT // MT)
    EN = 2 * FT // MT + len(KG) * KT // MT
    EQ = 2 * FT // MT + KT // MT

    ROWS = {}
    at = 0
    for name, rows in (("b_mod", 6 * KT), ("mix_pre_g", KT), ("mix_post_g", KT), ("ffn_pre_g", KT),
                       ("ffn_post_g", KT), ("conv_w", CK * CT), ("conv_b", CT), ("ssm_norm_g", KT),
                       ("cmlp_ln_g", KT), ("cmlp_ln_b", KT)):
        ROWS[name] = (at, rows)
        at += rows
    NROW = at
    RT = -(-NROW // P)
    assert ROWS["conv_b"][0] == P

    ctx = ExitStack()
    with ctx:
        def sb(name, shape, dt=F32, where=ctx):
            return where.enter_context(nc.sbuf_tensor(name, shape, dt))

        raw01 = sb("raw01", [P, 2, KT, CW])
        whi01 = sb("whi01", [P, 2, KT, CW], F32R)
        wlo01 = sb("wlo01", [P, 2, KT, CW], F32R)
        x = sb("x", [P, KT, T])
        hf = sb("hf", [P, KT, T])
        xhi = sb("xhi", [P, KT, T], F32R)
        xlo = sb("xlo", [P, KT, T], F32R)
        rs = sb("rs", [P, 2, T])
        ident = sb("ident", [P, P])
        ones = sb("ones", [P, P])
        tri = sb("tri", [P, P])
        earlier = sb("earlier", [P, E, E])
        spread = sb("spread", [H, D])
        PT = sb("PT", [P, L, NROW])
        mod = sb("mod", [P, L, 6 * KT, NC])
        fold = sb("fold", [CL + NC, NC])
        stT = sb("stT", [P, L, CT, B * (CK - 1)])
        headp = sb("headp", [H, 3, L])
        expa = sb("expa", [H, L])
        rw = sb("rw", [P, KT, E])
        rb = sb("rb", [1, E])
        spb = sb("spb", [KT, L, Q])
        w00 = sb("w00", [KT, L])

        mixer = ExitStack()
        zs = sb("zs", [P, KT, T], F32, mixer)
        ub = sb("ub", [P, KT, T], F32, mixer)
        vb = sb("vb", [P, KT, T], F32, mixer)
        sga = sb("sga", [P, KT, T], F32, mixer)
        sgb = sb("sgb", [P, KT, T], F32, mixer)
        xraw = sb("xraw", [P, CT * (CK - 1 + T)], F32, mixer)
        xrawv = xraw[:, :].rearrange("p (c t) -> p c t", c=CT)
        xc = sb("xc", [P, CT * T], F32, mixer)
        xcv = xc[:, :].rearrange("p (c t) -> p c t", c=CT)
        xdt = sb("xdt", [P, D], F32, mixer)
        xw = sb("xw", [P, D], F32, mixer)
        mix = sb("mix", [P, H, Q], F32, mixer)
        ce = sb("ce", [P, H, Q], F32, mixer)
        hT = sb("hT", [P, D], F32, mixer)
        bt = sb("bt", [P, G, Q], F32, mixer)
        cbm = sb("cbm", [P, G, Q], F32, mixer)
        dth = sb("dth", [H, 8, T], F32, mixer)
        spin = sb("spin", [H, 2 * B + 1], F32, mixer)
        spx = sb("spx", [P, KT, 2 * B + 1], F32, mixer)
        tokp = sb("tokp", [P, 2, H], F32, mixer)
        lastc = sb("lastc", [P, H], F32, mixer)
        wend = sb("wend", [P, H], F32, mixer)
        elast = sb("elast", [P, H], F32, mixer)
        bct = sb("bct", [B, 4 * P], F32, mixer)
        dtx = sb("dtx", [P, KT, B], F32, mixer)
        ysm = sb("ysm", [P, KT, B], F32, mixer)
        tmp = sb("tmp", [P, CT, B], F32, mixer)
        diag = sb("diag", [KT, 2, KT], F32, mixer)
        spc = sb("spc", [P, 2, KT], F32, mixer)
        mixer.close()
        ffn = ExitStack()
        raw2 = sb("raw2", [P, KT, CW], F32, ffn)
        whi2 = sb("whi2", [P, KT, CW], F32R, ffn)
        wlo2 = sb("wlo2", [P, KT, CW], F32R, ffn)
        cst = sb("cst", [P, KT, P], F32R, ffn)
        ghi = sb("ghi", [P, FT, T], F32R, ffn)
        glo = sb("glo", [P, FT, T], F32R, ffn)
        facc = sb("facc", [P, KT, T], F32, ffn)
        sg = sb("sg", [P, MT, T], F32, ffn)
        gu = sb("gu", [P, MT, T], F32, ffn)
        cbc = sb("cbc", [P, E, T], F32, ffn)
        lg = sb("lg", [P, 3, E], F32, ffn)
        cmp_ = sb("cmp_", [P, E, E], F32, ffn)
        eqm = sb("eqm", [P, E, E], F32, ffn)
        rank = sb("rank", [P, 3, E], F32, ffn)
        top = sb("top", [P, 3, 8], F32, ffn)
        rsum = sb("rsum", [P, 3], F32, ffn)
        comb = sb("comb", [E, T], F32, ffn)
        ffn.close()
        raw = [raw01[:, 0], raw01[:, 1], raw2[:, :, :]]
        whi = [whi01[:, 0], whi01[:, 1], whi2[:, :, :]]
        wlo = [wlo01[:, 0], wlo01[:, 1], wlo2[:, :, :]]
        ctok = xdt
        mtok = sgb[:, :, :].rearrange("p k t -> p (k t)")[:, 0:R3 * CW].rearrange("p (s c) -> p s c", s=R3)
        bmod = sgb[:, :, :].rearrange("p k t -> p (k t)")[:, R3 * CW:R3 * CW + L * 6 * KT]
        modf = mod[:, :, :, :].rearrange("p l r c -> p (l r) c")
        ptok = mix[:, :, :].rearrange("p h q -> p (h q)")
        stok = xc
        xtok = xraw
        tail = ce[:, :, :].rearrange("p h q -> p (h q)")
        sring = ce[:, :, :].rearrange("p (s k) n -> p s k n", s=2)
        sprod = xw[:, :].rearrange("p (k n) -> p k n", k=KT)
        hst = mix[:, 0:KT, :]
        vtok = mix[:, :, :].rearrange("p (c g) q -> p c (g q)", c=NQ)
        wsp = ce[:, 0:KT, :]
        wT = xdt[:, :].rearrange("p (g q) -> p g q", g=KT)

        acc = ctx.enter_context(nc.psum_tensor("acc", [P, 4, 512], F32))
        ms = ctx.enter_context(nc.psum_tensor("ms", [P, 4, 512], F32))
        msf = ms[:, :, :].rearrange("p b n -> p (b n)")

        sem = {s: ctx.enter_context(nc.semaphore(s)) for s in SEMAPHORES}
        raw_full = [sem["raw_full0"], sem["raw_full1"], sem["raw_full2"]]
        acc_free = [sem["acc_free0"], sem["acc_free1"]]
        s_in = [sem["s_in0"], sem["s_in1"]]
        s_out = [sem["s_out0"], sem["s_out1"]]
        block = ctx.enter_context(nc.Block())

        def row(name, l, k=None):
            r0, rows = ROWS[name]
            return PT[:, l, r0:r0 + rows] if k is None else PT[:, l, r0 + k:r0 + k + 1]

        def bc(ap, axis, shape):
            return ap.unsqueeze(axis).to_broadcast(shape)

        def later(i, n):
            return not isinstance(i, int) or i >= n

        def loop(eng, count, body, peel=0):
            for i in range(peel):
                body(i)
            if count > peel:
                with eng.Fori(0, count - peel) as i:
                    body(i + peel)

        def load(sp, n, slot, dst_cols, src, nk=KT):
            sp.wait_ge(sem["lo_ready"], n - 1)
            sp.dma_start(raw[slot][:, 0:nk, 0:dst_cols], src).then_inc(raw_full[slot], 16)

        def landed(base):
            return 16 * (M3 + (base - N0["xbc", 0]) // 2 + 1)

        def load_phase(sp, key, w, col0, count):
            n0 = N0[key]
            wv = w.rearrange("(k p) m -> p k m", p=P)

            def body(i):
                for c in range(2):
                    a = sp.snap(col0 + CW * c + 2 * CW * i)
                    load(sp, n0 + c + 2 * i, (n0 + c) % 2, CW, wv[:, :, bass.ds(a, CW)])
            loop(sp, count // 2, body)

        def split_hi(act, base, i, step=2, e=0):
            slot = base % 2
            act.wait_ge(raw_full[slot], landed(base) + 8 * step * i + 8 * EN * e)
            act.wait_ge(sem["w_used"], base - 1 + step * i + EN * e)
            act.activation(whi[slot], raw[slot], ACT.Copy).then_inc(sem["hi_ready"], 1)

        def split_lo(dve, base, i, step=2, e=0):
            slot = base % 2
            dve.wait_ge(sem["hi_ready"], base + 1 + step * i + EN * e)
            dve.tensor_tensor(wlo[slot], raw[slot], whi[slot].bitcast(F32), ALU.subtract) \
                .then_inc(sem["lo_ready"], 1)

        def products(pe, n, slot, pair, first, last, hi, lo, cols, nk=KT, tiles=MT):
            pe.wait_ge(sem["lo_ready"], n + 1)
            for j in range(tiles):
                out = acc[:, 2 * pair + j, 0:cols]
                for k in range(nk):
                    a = whi[slot][:, k, j * P:(j + 1) * P]
                    b = wlo[slot][:, k, j * P:(j + 1) * P]
                    pe.matmul(out, a, hi(k), start=first and k == 0, stop=False)
                    pe.matmul(out, a, lo(k), start=False, stop=False)
                    ins = pe.matmul(out, b, hi(k), start=False, stop=last and k == nk - 1)
            ins.then_inc(sem["w_used"], 1)

        def pe_phase(pe, key, count, hi, lo, cols, peel=0):
            n0, q0 = N0[key], Q0[key]

            def body(i):
                for c in range(2):
                    if not (isinstance(i, int) and q0 + c + 2 * i < 2):
                        pe.wait_ge(acc_free[(q0 + c) % 2], (q0 + c) // 2 + i)
                    products(pe, n0 + c + 2 * i, (n0 + c) % 2, (q0 + c) % 2, True, True, hi, lo, cols)
            loop(pe, count // 2, body, peel)

        def act_phase(act, key, count, epilogue=None, peel=0):
            n0, q0 = N0[key], Q0[key]

            def body(i):
                for c in range(2):
                    split_hi(act, n0 + c + 1, i)
                    if epilogue:
                        act.wait_ge(sem["w_used"], n0 + c + 1 + 2 * i)
                        pair = (q0 + c) % 2
                        epilogue(i, c, acc[:, 2 * pair:2 * pair + 2, 0:T]).then_inc(acc_free[pair], 1)
            loop(act, count // 2, body, peel)

        def dve_phase(dve, key, count, epilogue=None, peel=0, cols=T):
            n0, q0 = N0[key], Q0[key]

            def body(i):
                for c in range(2):
                    split_lo(dve, n0 + c + 1, i)
                    if epilogue:
                        dve.wait_ge(sem["w_used"], n0 + c + 1 + 2 * i)
                        pair = (q0 + c) % 2
                        epilogue(i, c, acc[:, 2 * pair:2 * pair + 2, 0:cols]).then_inc(acc_free[pair], 1)
            loop(dve, count // 2, body, peel)

        def xs(part):
            return lambda k: part[:, k, :]

        @block.sync
        def _(sp):
            for l in range(L):
                wv = A["w_mod"][l].rearrange("(k p) m -> p k m", p=P)
                per = 6 * KT // MT // R3

                def body(i):
                    for c in range(R3):
                        a = sp.snap(R3 * CW * i + CW * c)
                        if not (isinstance(i, int) and l == 0):
                            sp.wait_ge(sem["lo_ready"], l * per * R3 + c - 2 + R3 * i)
                        sp.dma_start(raw[c], wv[:, :, bass.ds(a, CW)]).then_inc(raw_full[c], 16)
                loop(sp, per, body, 1 if l == 0 else 0)
            sp.wait_ge(sem["lo_ready"], N0["xbc", 0])
            for l in range(L):
                load_phase(sp, ("xbc", l), A["w_in"][l], IN_COL["xbc"], IN_CHUNKS["xbc"])
                n = N0["dt", l]
                load(sp, n, n % 2, H, A["w_in"][l].rearrange("(k p) m -> p k m", p=P)[:, :, D + CD:D + CD + H])
                for name in ("z", "u", "v", "ga", "gb"):
                    load_phase(sp, (name, l), A["w_in"][l], IN_COL[name], IN_CHUNKS[name])
                for name, w in (("ssd_out", A["w_ssd_out"]), ("cmlp_out", A["w_cmlp_out"]), ("w_o", A["w_o"])):
                    load_phase(sp, (name, l), w[l], 0, KT // MT)

                def expert(e, wg, wu, wd):
                    n0 = N0["gu", l, 0]
                    gv, uv = (w.rearrange("(k p) m -> p k m", p=P) for w in (wg, wu))
                    dv = wd.rearrange("(k p) m -> p k m", p=P)

                    def gates(i):
                        a = sp.snap(CW * i)
                        for c, w in enumerate((gv, uv)):
                            load(sp, n0 + c + 2 * i + EN * e, (n0 + c) % 2, CW, w[:, :, bass.ds(a, CW)])
                    with sp.Fori(0, FT // MT) as i:
                        gates(i)
                    n1 = N0["wd", l, 0]

                    def downs(i):
                        for g in range(2):
                            a = sp.snap(2 * CW * i + g * CW)
                            for s, (k0, nk) in enumerate(KG):
                                c = g * len(KG) + s
                                load(sp, n1 + c + 2 * len(KG) * i + EN * e, (n1 + c) % 2, CW,
                                     dv[:, k0:k0 + nk, bass.ds(a, CW)], nk)
                    with sp.Fori(0, KT // MT // 2) as i:
                        downs(i)

                if l % 2 == 0:
                    expert(0, A["ffn_wg"][l // 2], A["ffn_wu"][l // 2], A["ffn_wd"][l // 2])
                else:
                    with sp.Fori(0, E) as e:
                        expert(e, A["exp_wg"][l // 2, e], A["exp_wu"][l // 2, e], A["exp_wd"][l // 2, e])

        @block.gpsimd
        def _(pool):
            pool.wait_ge(sem["ctok_zero"], 1)
            pool.dma_start(ctok[0:1, :], A["c_prompt"]).then_inc(sem["c_in"], 16)
            pool.dma_start(ctok[1:1 + B, :], A["c_sample"]).then_inc(sem["c_in"], 16)
            pool.memset(ident[:, :], 0.0).then_inc(sem["ident_zero"], 1)
            pool.memset(tri[:, :], 1.0).then_inc(sem["ident_zero"], 1)
            pool.memset(spread[:, :], 1.0).then_inc(sem["ident_zero"], 1)
            pool.memset(earlier[:, :, :], 1.0).then_inc(sem["ident_zero"], 1)
            pool.memset(fold[:, :], 0.0).then_inc(sem["ident_zero"], 1)
            pool.wait_ge(sem["ident_zero"], 5)
            pool.affine_select(out=ident[:, :], in_=ident[:, :], compare_op=ALU.not_equal, fill=1.0, base=0,
                               pattern=[[-1, P]], channel_multiplier=1).then_inc(sem["consts"], 1)
            pool.affine_select(out=tri[:, :], in_=tri[:, :], compare_op=ALU.is_ge, fill=0.0, base=0,
                               pattern=[[1, P]], channel_multiplier=-1).then_inc(sem["consts"], 1)
            pool.affine_select(out=spread[:, :], in_=spread[:, :], compare_op=ALU.is_ge, fill=0.0, base=0,
                               pattern=[[1, D]], channel_multiplier=-HD).then_inc(sem["consts"], 1)
            pool.wait_ge(sem["consts"], 3)
            pool.affine_select(out=spread[:, :], in_=spread[:, :], compare_op=ALU.is_ge, fill=0.0, base=HD - 1,
                               pattern=[[-1, D]], channel_multiplier=HD).then_inc(sem["consts"], 1)
            pool.affine_select(out=earlier[:, :, :], in_=earlier[:, :, :], compare_op=ALU.is_gt, fill=0.0, base=0,
                               pattern=[[1, E], [-1, E]], channel_multiplier=0).then_inc(sem["consts"], 1)
            pool.wait_ge(sem["consts"], 5)
            pool.tensor_copy(fold[0:NC, :], ident[0:NC, 0:NC]).then_inc(sem["consts"], 1)
            pool.tensor_copy(fold[CL:CL + NC, :], ident[CL:CL + NC, CL:CL + NC]).then_inc(sem["consts"], 1)
            for l in range(L):
                for name, (r0, rows) in ROWS.items():
                    src = (A["conv_w"][l].rearrange("k (c p) -> (k c) p", p=P) if name == "conv_w"
                           else A["vectors"][name][l].rearrange("(c p) -> c p", p=P))
                    c0 = (l * RT + r0 // P) * P
                    pool.dma_start(ptok[r0 % P:r0 % P + rows, c0:c0 + P], src).then_inc(sem["params_in"], 16)
            for l in range(L):
                pool.dma_start(stok[0:B * (CK - 1), l * CD:(l + 1) * CD],
                               A["state_conv"][l].rearrange("b k c -> (b k) c")).then_inc(sem["states_in"], 16)
            for c in range(NQ):
                pool.dma_start(xtok[:, c * D:(c + 1) * D], A["x_prompt"][0, c * Q:(c + 1) * Q, :]).then_inc(sem["x_in"], 16)
            pool.dma_start(xtok[0:B, NQ * D:(NQ + 1) * D], A["x_sample"][:, 0, :]).then_inc(sem["x_in"], 16)
            for k, v in enumerate((A["dt_bias"], A["a_log"], A["d_skip"])):
                pool.dma_start(headp[:, k, :], v.rearrange("l h -> h l"), allow_slow_non_contiguous=True).then_inc(sem["sp_in"], 16)
            pool.dma_start(spb[:, :, :], A["b_spatial"].rearrange("l g q -> g l q")).then_inc(sem["sp_in"], 16)
            for l in range(L):
                pool.dma_start(w00[:, l:l + 1], A["w_spatial"][l, :, 0, 0:1], allow_slow_non_contiguous=True).then_inc(sem["sp_in"], 16)
            pool.dma_start(rw[:, :, :], A["router_w"][0].rearrange("(k p) e -> p k e", p=P)).then_inc(sem["route_in"], 16)
            pool.dma_start(rb[:, :], A["router_b"]).then_inc(sem["route_in"], 16)
            pool.dma_start(O["conv_s"][:, :, 0:CK - 2, :], A["state_conv"][:, :, 1:CK - 1, :]).then_inc(sem["conv_keep"], 16)

            for l in range(L):
                pool.wait_ge(sem["tail_ready"], l + 1)
                pool.dma_start(O["conv_p"][l, 0], tail[0:CK - 1, 0:CD]).then_inc(sem["tail_out"], 16)
                pool.dma_start(O["conv_s"][l, :, CK - 2, :], tail[CK - 1:CK - 1 + B, 0:CD]).then_inc(sem["tail_out"], 16)
                pool.wait_ge(sem["st_copied"], l + 1)
                pool.dma_start(O["ssm_p"][l, 0].rearrange("(k j) p n -> (j p) k n", j=2), hst).then_inc(sem["st_out"], 16)
                state = A["state_ssm"][l].rearrange("b (k j) p n -> b (j p) k n", j=2)
                new = O["ssm_s"][l].rearrange("b (k j) p n -> b (j p) k n", j=2)
                pool.wait_ge(sem["y_part"], (l + 1) * NQ)
                for b in range(B):
                    s = b % 2
                    if b >= 2:
                        pool.wait_ge(s_out[s], 16 * (l * B // 2 + b // 2))
                        pool.wait_ge(sem["samp_used"], l * B + b - 1)
                    pool.dma_start(sring[:, s], state[b]).then_inc(s_in[s], 16)
                    if b >= 1:
                        pool.wait_ge(sem["s_new"], l * B + b)
                        pool.dma_start(new[b - 1], sring[:, 1 - s]).then_inc(s_out[1 - s], 16)
                pool.wait_ge(sem["s_new"], (l + 1) * B)
                pool.dma_start(new[B - 1], sring[:, (B - 1) % 2]).then_inc(s_out[(B - 1) % 2], 16)
                for s in range(2):
                    pool.wait_ge(s_out[s], 8 * (l + 1) * B)
                pool.wait_ge(sem["samp_used"], (l + 1) * B)
                pool.dma_start(wsp, A["w_spatial"][l].rearrange("g t s -> t g s")).then_inc(sem["w_sp_in"], 16)
                pool.wait_ge(sem["vs_copied"], l + 1)
                pool.dma_start(O["v_s"][l, :, 0, :], xw[0:B, :]).then_inc(sem["vs_out"], 16)
            pool.wait_ge(sem["y_copied"], 3)
            for c in range(NQ):
                pool.dma_start(O["y_p"][0, c * Q:(c + 1) * Q, :], xtok[:, c * D:(c + 1) * D]).then_inc(sem["y_out"], 16)
            pool.dma_start(O["y_s"][:, 0, :], xtok[0:B, NQ * D:(NQ + 1) * D]).then_inc(sem["y_out"], 16)
            pool.wait_ge(sem["y_out"], 16 * (NQ + 1))
            pool.wait_ge(sem["conv_keep"], 16)
            pool.wait_ge(sem["tail_out"], 32 * L)
            pool.wait_ge(sem["st_out"], 16 * L)
            for s in range(2):
                pool.wait_ge(s_out[s], 8 * L * B)
            pool.wait_ge(sem["vs_out"], 16 * L)

        @block.tensor
        def _(pe):
            def sum_tiles(v, src, out, k0=0, k1=KT):
                for k in range(k0, k1):
                    ins = pe.matmul(out, ones[:, :], src[:, k, :], start=k == k0, stop=k == k1 - 1)
                return ins

            def norm(v):
                pe.wait_ge(sem["sq_ready"], v)
                sum_tiles(v, hf, ms[:, 0, 0:T]).then_inc(sem["ssq_ready"], 1)

            pe.wait_ge(sem["consts"], 7)
            pe.wait_ge(sem["c_silu"], 1)
            for k in range(KT):
                ins = pe.transpose(ms[:, 0, NC * k:NC * (k + 1)], ctok[0:NC, k * P:(k + 1) * P], ident[0:NC, 0:NC])
            ins.then_inc(sem["c_turned"], 1)
            pe.wait_ge(sem["params_in"], 16 * L * len(ROWS))
            for l in range(L):
                for r in range(RT):
                    rows = min(P, NROW - r * P)
                    c0 = (l * RT + r) * P
                    ins = pe.transpose(ms[:, 1, l * NROW + r * P:l * NROW + r * P + rows], ptok[0:rows, c0:c0 + P],
                                       ident[0:rows, 0:rows])
            ins.then_inc(sem["params_turned"], 1)
            SR = B * (CK - 1)
            pe.wait_ge(sem["states_in"], 16 * L)
            for l in range(L):
                for k in range(CT):
                    ins = pe.transpose(ms[:, 2 + l, k * SR:(k + 1) * SR], stok[0:SR, l * CD + k * P:l * CD + (k + 1) * P],
                                       ident[0:SR, 0:SR])
            ins.then_inc(sem["state_turned"], 1)
            pe.wait_ge(sem["x_in"], 16 * (NQ + 1))
            pe.wait_ge(sem["state_ready"], 1)
            pe.wait_ge(sem["params_ready"], 1)
            pe.wait_ge(sem["c_lo"], 1)
            for c in range(NQ + 1):
                rows = Q if c < NQ else B
                if c >= 2:
                    pe.wait_ge(sem["x_ready"], c - 1)
                for k in range(KT):
                    bank = 2 * (c % 2) + k // 4
                    ins = pe.transpose(ms[:, bank, (k % 4) * P:(k % 4) * P + rows],
                                       xtok[0:rows, c * D + k * P:c * D + (k + 1) * P], ident[0:rows, 0:rows])
                ins.then_inc(sem["x_turned"], 1)

            def fold_chunk(m, c):
                pe.wait_ge(sem["mt_ready"], m + 1)
                if not isinstance(m, int) or m >= R3:
                    pe.wait_ge(sem["mod_added"], m - 2)
                for j in range(MT):
                    ins = pe.matmul(ms[:, c, j * NC:(j + 1) * NC], mtok[0:CL + NC, c, j * P:(j + 1) * P], fold[:, :],
                                    start=True, stop=True)
                ins.then_inc(sem["folded"], 1)

            def mod_body(i):
                for c in range(R3):
                    pe.wait_ge(sem["lo_ready"], c + 1 + R3 * i)
                    if later(i, 1):
                        pe.wait_ge(sem["mt_ready"], c - 2 + R3 * i)
                    for k in range(KT):
                        pe.matmul(acc[:, c, 0:CW], cst[:, k, :], whi[c][:, k, :], start=k == 0, stop=False)
                        ins = pe.matmul(acc[:, c, 0:CW], cst[:, k, :], wlo[c][:, k, :], start=False, stop=k == KT - 1)
                    ins.then_inc(sem["w_used"], 1)
                    if later(i, 1) or c >= 2:
                        fold_chunk(R3 * i + c - 2, (c - 2) % R3)
            pe.wait_ge(sem["x_ready"], NQ + 1)
            loop(pe, N0["xbc", 0] // R3, mod_body, 2)
            for m in (N0["xbc", 0] - 2, N0["xbc", 0] - 1):
                fold_chunk(m, m % R3)
            pe.wait_ge(sem["mod_added"], N0["xbc", 0])

            for l in range(L):
                norm(4 * l + 1)
                pe.wait_ge(sem["xs_lo"], 5 * l + 1)
                pe_phase(pe, ("xbc", l), IN_CHUNKS["xbc"], xs(xhi), xs(xlo), T, peel=1 if l == 0 else 0)
                n, q = N0["dt", l], Q0["dt", l]
                pe.wait_ge(acc_free[q % 2], q // 2)
                products(pe, n, n % 2, q % 2, True, True, xs(xhi), xs(xlo), T, tiles=1)
                for name in ("z", "u", "v", "ga", "gb"):
                    pe_phase(pe, (name, l), IN_CHUNKS[name], xs(xhi), xs(xlo), T)

                for k in range(CT):
                    ins = pe.transpose(ms[0:CK - 1 + B, k // 4, (k % 4) * P:(k % 4 + 1) * P],
                                       xrawv[:, k, S:S + CK - 1 + B], ident[:, :])
                ins.then_inc(sem["tail_turned"], 1)
                pe.wait_ge(sem["samp_decay"], l + 1)
                for k in range(KT):
                    ins = pe.matmul(ms[:, 3, k * (2 * B + 1):(k + 1) * (2 * B + 1)], spread[:, k * P:(k + 1) * P],
                                    spin[:, :], start=True, stop=True)
                ins.then_inc(sem["spread_ready"], 1)

                pe.wait_ge(sem["xc_ready"], l + 1)
                for c in range(NQ):
                    v = l * NQ + c
                    toks = slice(c * Q, (c + 1) * Q)
                    pe.wait_ge(sem["tail_ready"], l + 1)
                    if c:
                        pe.wait_ge(sem["y_taken"], v)
                        pe.wait_ge(sem["st_ready"], v)
                    for k in range(KT):
                        ins = pe.transpose(ms[:, k // 4, (k % 4) * P:(k % 4 + 1) * P], xcv[:, k, toks], ident[:, :])
                    ins.then_inc(sem["x_tok"], 1)
                    for g in range(G):
                        pe.transpose(ms[:, 2, g * P:(g + 1) * P], xcv[:, KT + g, toks], ident[:, :])
                    pe.transpose(ms[:, 2, 2 * P:2 * P + H], dth[:, 0, toks], ident[0:H, 0:H])
                    pe.transpose(ms[:, 2, 2 * P + H:2 * P + 2 * H], dth[:, 1, toks], ident[0:H, 0:H]) \
                        .then_inc(sem["b_tok"], 1)
                    pe.wait_ge(sem["spread_copied"], l + 1)
                    for g in range(G):
                        ins = pe.matmul(ms[:, 3, g * Q:(g + 1) * Q], xcv[:, KT + g, toks], xcv[:, KT + G + g, toks],
                                        start=True, stop=True)
                    ins.then_inc(sem["cb_ready"], 1)
                    pe.wait_ge(sem["xdt_ready"], v + 1)
                    pe.wait_ge(sem["bt_ready"], v + 1)
                    pe.wait_ge(sem["tok_ready"], v + 1)
                    pe.wait_ge(sem["cbm_ready"], v + 1)
                    for h in range(H):
                        ins = pe.matmul(ms[:, h // 4, (h % 4) * Q:(h % 4 + 1) * Q], ident[0:H, h:h + 1].to_broadcast([H, P]),
                                        dth[:, 0, toks], start=True, stop=True)
                    ins.then_inc(sem["cumb_ready"], 1)
                    pe.wait_ge(sem["mix_ready"], v + 1)
                    pe.wait_ge(sem["wend_ready"], v + 1)
                    if c:
                        pe.wait_ge(sem["ce_ready"], l + 1)
                    for h in range(H):
                        out = ms[(h % 2) * HD:(h % 2 + 1) * HD, h // 8, (h // 2 % 4) * Q:(h // 2 % 4 + 1) * Q]
                        ins = pe.matmul(out, xdt[:, h * HD:(h + 1) * HD], mix[:, h, :], start=True, stop=c == 0)
                        if c:
                            ins = pe.matmul(out, hT[:, h * HD:(h + 1) * HD], ce[:, h, :], start=False, stop=True)
                    ins.then_inc(sem["y_part"], 1)
                    pe.wait_ge(sem["xw_ready"], v + 1)
                    for g in range(G):
                        ins = pe.matmul(ms[:, 2 + g, :], bt[:, g, :], xw[:, g * 512:(g + 1) * 512], start=True, stop=True)
                    ins.then_inc(sem["st_part"], 1)
                pe.wait_ge(sem["st_ready"], (l + 1) * NQ)
                pe.wait_ge(sem["y_taken"], (l + 1) * NQ)
                for k in range(KT):
                    ins = pe.transpose(ms[:, k // 4, (k % 4) * P:(k % 4 + 1) * P], hT[:, k * P:(k + 1) * P], ident[:, :])
                ins.then_inc(sem["st_turned"], 1)
                for k in range(2 * G):
                    ins = pe.transpose(ms[0:B, 2, k * P:(k + 1) * P], xcv[:, KT + k, S:T], ident[:, :])
                ins.then_inc(sem["bc_turned"], 1)
                pe.wait_ge(sem["bc_ready"], l + 1)
                pe.wait_ge(sem["st_copied"], l + 1)
                for b in range(B):
                    if b >= 2:
                        pe.wait_ge(sem["samp_used"], l * B + b - 1)
                    pe.matmul(ms[:, b % 2, :], ident[0:B, b:b + 1].to_broadcast([B, P]), bct[:, :], start=True,
                              stop=True).then_inc(sem["bc_spread"], 1)
                pe.wait_ge(sem["gate_sq"], l + 1)
                for g in range(G):
                    ins = sum_tiles(0, zs, ms[:, 2 + g, 0:T], g * KT // G, (g + 1) * KT // G)
                ins.then_inc(sem["gate_ssq"], 1)
                pe.wait_ge(sem["xs_lo"], 5 * l + 2)
                pe_phase(pe, ("ssd_out", l), KT // MT, xs(xhi), xs(xlo), T)

                pe.wait_ge(sem["gate_rs"], l + 1)
                sum_tiles(0, vb, ms[:, 0, 0:T]).then_inc(sem["v_sum"], 1)
                pe.wait_ge(sem["v_sq"], l + 1)
                sum_tiles(0, xcv, ms[:, 1, 0:T]).then_inc(sem["v_ssq"], 1)
                pe.wait_ge(sem["v_normed"], l + 1)
                for k in range(KT):
                    ins = pe.transpose(ms[0:B, k // 4, (k % 4) * P:(k % 4 + 1) * P], vb[:, k, S:T], ident[:, :])
                ins.then_inc(sem["vs_turned"], 1)
                pe.wait_ge(sem["w_sp_in"], 16 * (l + 1))
                for k in range(KT):
                    ins = pe.transpose(ms[:, 2 + k // 4, (k % 4) * P:(k % 4 + 1) * P], wsp[:, k, :], ident[:, :])
                ins.then_inc(sem["w_turned"], 1)
                pe.wait_ge(sem["vs_copied"], l + 1)
                for c in range(NQ):
                    if c:
                        pe.wait_ge(sem["v_tok_ready"], l * NQ + c)
                    for k in range(KT):
                        ins = pe.transpose(ms[:, k // 4, (k % 4) * P:(k % 4 + 1) * P], vb[:, k, c * Q:(c + 1) * Q],
                                           ident[:, :])
                    ins.then_inc(sem["v_tok"], 1)
                pe.wait_ge(sem["diag_ready"], l + 1)
                pe.wait_ge(sem["v_tok_ready"], (l + 1) * NQ)
                pe.wait_ge(sem["w_ready"], l + 1)
                pe.matmul(ms[:, 0, 0:2 * KT], ones[0:KT, :], diag[:, :, :].rearrange("g a b -> g (a b)"), start=True,
                          stop=True).then_inc(sem["sp_bcast"], 1)
                pe.wait_ge(sem["sp_bcast_ready"], l + 1)
                for c in range(NQ):
                    for k in range(KT):
                        out = ms[:, 2 * c + k // 4, (k % 4) * Q:(k % 4 + 1) * Q]
                        pe.matmul(out, vtok[:, c, k * P:(k + 1) * P], wT[:, k, :], start=True, stop=False)
                        ins = pe.matmul(out, ident[0:KT, k:k + 1].to_broadcast([KT, P]), spb[:, l, :], start=False,
                                        stop=True)
                    ins.then_inc(sem["sp_out"], 1)
                pe.wait_ge(sem["xs_lo"], 5 * l + 3)
                pe_phase(pe, ("cmlp_out", l), KT // MT, xs(xhi), xs(xlo), T)
                pe.wait_ge(sem["xs_lo"], 5 * l + 4)
                pe_phase(pe, ("w_o", l), KT // MT, xs(xhi), xs(xlo), T)
                norm(4 * l + 2)
                norm(4 * l + 3)

                if l % 2:
                    pe.wait_ge(sem["h_ready"], 2 * l + 2)
                    for c in range(3):
                        rows = Q if c < NQ else B
                        for k in range(KT):
                            pe.matmul(ms[0:rows, 1, c * E:(c + 1) * E], hf[:, k, c * Q:c * Q + rows], rw[:, k, :],
                                      start=k == 0, stop=False)
                        ins = pe.matmul(ms[0:rows, 1, c * E:(c + 1) * E], ones[0:1, 0:rows], rb[:, :], start=False,
                                        stop=True)
                    ins.then_inc(sem["logits_ready"], 1)
                    pe.wait_ge(sem["route_done"], 1)
                    for c in range(3):
                        rows = Q if c < NQ else B
                        ins = pe.transpose(ms[0:E, 2, c * Q:c * Q + rows], rank[0:rows, c, :], ident[0:rows, 0:rows])
                    ins.then_inc(sem["combine_turned"], 1)
                    pe.wait_ge(sem["combine_ready"], 1)
                    for e in range(E):
                        if e >= 4:
                            pe.wait_ge(sem["combine_spread_ready"], e - 3)
                        pe.matmul(ms[:, e % 4, 0:T], ident[0:E, e:e + 1].to_broadcast([E, P]), comb[:, :], start=True,
                                  stop=True).then_inc(sem["combine_spread"], 1)
                pe.wait_ge(sem["xs_lo"], 5 * l + 5)

                def expert(e):
                    n0, q0 = N0["gu", l, 0], Q0["gu", l, 0]

                    def gates(i):
                        for c in range(2):
                            pe.wait_ge(acc_free[(q0 + c) % 2], (q0 + c) // 2 + i + EQ // 2 * e)
                            products(pe, n0 + c + 2 * i + EN * e, (n0 + c) % 2, (q0 + c) % 2, True, True, xs(xhi),
                                     xs(xlo), T)
                    with pe.Fori(0, FT // MT) as i:
                        gates(i)
                    n1, q1 = N0["wd", l, 0], Q0["wd", l, 0]

                    def downs(i):
                        for g in range(2):
                            pair = (q1 + g) % 2
                            pe.wait_ge(acc_free[pair], (q1 + g) // 2 + i + EQ // 2 * e)
                            for s, (k0, nk) in enumerate(KG):
                                pe.wait_ge(acc_free[(q0 + 1) % 2], (q0 + 1) // 2 + (k0 + nk) // MT + EQ // 2 * e)
                                c = g * len(KG) + s
                                products(pe, n1 + c + 2 * len(KG) * i + EN * e, (n1 + c) % 2, pair, s == 0,
                                         s == len(KG) - 1, lambda k, k0=k0: ghi[:, k0 + k, :],
                                         lambda k, k0=k0: glo[:, k0 + k, :], T, nk)
                    with pe.Fori(0, KT // MT // 2) as i:
                        downs(i)

                if l % 2 == 0:
                    expert(0)
                else:
                    with pe.Fori(0, E) as e:
                        expert(e)
                norm(4 * l + 4)

            pe.wait_ge(sem["x_ready"], 3 + 2 * L)
            for c in range(NQ + 1):
                rows = Q if c < NQ else B
                if c >= 2:
                    pe.wait_ge(sem["y_copied"], c - 1)
                for k in range(KT):
                    ins = pe.transpose(ms[0:rows, 2 * (c % 2) + k // 4, (k % 4) * P:(k % 4 + 1) * P],
                                       x[:, k, c * Q:c * Q + rows], ident[:, :])
                ins.then_inc(sem["y_turned"], 1)

        @block.scalar
        def _(act):
            def norm_sq(v, src):
                act.activation(hf[:, :, :], src[:, :, :], ACT.Square).then_inc(sem["sq_ready"], 1)

            def norm_rs(v):
                act.wait_ge(sem["inv_ready"], v)
                act.activation(rs[:, 0, :], rs[:, 0, :], ACT.Sqrt).then_inc(sem["rs_ready"], 1)

            def hi_of_x(v, src):
                act.activation(xhi[:, :, :], src[:, :, :], ACT.Copy).then_inc(sem["xs_hi"], 1)

            act.wait_ge(sem["c_in"], 32)
            act.activation(ctok[0:NC, :], ctok[0:NC, :], ACT.Silu).then_inc(sem["c_silu"], 1)
            act.wait_ge(sem["c_turned"], 1)
            act.wait_ge(sem["cst_zero"], 1)
            act.activation(cst[:, :, 0:NC], ms[:, 0, 0:KT * NC].rearrange("p (k c) -> p k c", k=KT), ACT.Copy) \
                .then_inc(sem["c_hi"], 1)

            def mod_rows(m, c):
                act.wait_ge(sem["w_used"], m + 1)
                if not isinstance(m, int) or m >= R3:
                    act.wait_ge(sem["folded"], m - 2)
                act.activation(mtok[0:CL + NC, c, :], acc[0:CL + NC, c, 0:CW], ACT.Copy).then_inc(sem["mt_ready"], 1)

            NM = N0["xbc", 0]

            def mod_body(i, last=False):
                for c in range(R3):
                    if not (last and c == R3 - 1):
                        s = (c + 1) % R3
                        act.wait_ge(raw_full[s], 16 * ((c + 1) // R3 + 1) + 16 * i)
                        if later(i, 1) or c >= 2:
                            act.wait_ge(sem["w_used"], c - 1 + R3 * i)
                        act.activation(whi[s], raw[s], ACT.Copy).then_inc(sem["hi_ready"], 1)
                    if later(i, 1) or c >= 1:
                        mod_rows(R3 * i + c - 1, (c - 1) % R3)
            act.wait_ge(raw_full[0], 16)
            act.activation(whi[0], raw[0], ACT.Copy).then_inc(sem["hi_ready"], 1)
            mod_body(0)
            mod_body(1)
            with act.Fori(0, NM // R3 - 3) as i:
                mod_body(i + 2)
            mod_body(NM // R3 - 1, True)
            mod_rows(NM - 1, (NM - 1) % R3)
            act.wait_ge(sem["sp_in"], 16 * (4 + L))
            act.activation(expa[:, :], headp[:, 1, :], ACT.Exp).then_inc(sem["a_exp"], 1)

            for l in range(L):
                if l == 0:
                    act.wait_ge(sem["x_ready"], 3)
                    split_hi(act, N0["xbc", 0], 0)
                norm_sq(4 * l + 1, x)
                norm_rs(4 * l + 1)
                act.wait_ge(sem["h_ready"], 2 * l + 1)
                hi_of_x(5 * l + 1, hf)
                S3 = CK - 1
                act_phase(act, ("xbc", l), IN_CHUNKS["xbc"], lambda i, c, banks: act.activation(
                    xrawv[:, bass.ds(4 * i + 2 * c, 2), S3:S3 + T], banks, ACT.Copy))
                split_hi(act, N0["dt", l] + 1, 0)
                for name, dst, fn in (("z", zs, ACT.Silu), ("u", ub, ACT.Gelu_apprx_tanh),
                                      ("v", vb, ACT.Gelu_apprx_tanh), ("ga", sga, ACT.Sigmoid),
                                      ("gb", sgb, ACT.Sigmoid)):
                    act.preload_act_table(fn)
                    act_phase(act, (name, l), IN_CHUNKS[name], lambda i, c, banks, dst=dst, fn=fn: act.activation(
                        dst[:, bass.ds(4 * i + 2 * c, 2), :], banks, fn))
                act.wait_ge(sem["tail_turned"], l + 1)
                act.activation(tail[0:CK - 1 + B, 0:CD], msf[0:CK - 1 + B, 0:CD], ACT.Copy).then_inc(sem["tail_ready"], 1)
                act.wait_ge(sem["conv_done"], l + 1)
                act.activation(xc[:, :], xc[:, :], ACT.Silu).then_inc(sem["xc_ready"], 1)
                act.wait_ge(sem["dt_abs"], l + 1)
                act.activation(dth[:, 3, :], dth[:, 3, :], ACT.Exp, scale=-1.0).then_inc(sem["dt_exp"], 1)
                act.wait_ge(sem["cum_ready"], l + 1)
                act.activation(spin[:, 0:B], dth[:, 2, S:T], ACT.Exp).then_inc(sem["samp_decay"], 1)
                act.wait_ge(sem["spread_ready"], l + 1)
                act.activation(spx[:, :, :], ms[:, 3, 0:KT * (2 * B + 1)].rearrange("p (k c) -> p k c", k=KT),
                               ACT.Copy).then_inc(sem["spread_copied"], 1)
                for c in range(NQ):
                    v = l * NQ + c
                    act.wait_ge(sem["tok_ready"], v + 1)
                    if c:
                        act.wait_ge(sem["st_part"], v)
                    act.activation(bt[:, :, :], ms[:, 2, 0:G * P].rearrange("p (g n) -> p g n", g=G), ACT.Copy) \
                        .then_inc(sem["bt_ready"], 1)
                    act.wait_ge(sem["wend_arg"], v + 1)
                    act.activation(wend[:, :], wend[:, :], ACT.Exp).then_inc(sem["wend_ready"], 1)
                    act.activation(elast[:, :], lastc[:, :], ACT.Exp).then_inc(sem["last_ready"], 1)
                    act.wait_ge(sem["seg_ready"], v + 1)
                    if c:
                        act.wait_ge(sem["tail_out"], 32 * (l + 1))
                        act.activation(ce[:, :, :].rearrange("p h q -> p (h q)"), msf, ACT.Exp).then_inc(sem["ce_exp"], 1)
                    act.activation(mix[:, :, :], mix[:, :, :], ACT.Exp).then_inc(sem["mix_exp"], 1)
                    if c == 0:
                        act.wait_ge(sem["st_part"], v + 1)
                        act.activation(hT[:, :], msf[:, 1024:2048], ACT.Copy).then_inc(sem["st_ready"], 1)
                act.wait_ge(sem["st_turned"], l + 1)
                act.activation(hst.rearrange("p k n -> p (k n)"), msf[:, 0:1024], ACT.Copy).then_inc(sem["st_copied"], 1)
                act.wait_ge(sem["bc_turned"], l + 1)
                act.activation(bct[:, :], ms[0:B, 2, :], ACT.Copy).then_inc(sem["bc_ready"], 1)
                act.wait_ge(sem["samp_done"], l + 1)
                act.activation(zs[:, :, :], hf[:, :, :], ACT.Square).then_inc(sem["gate_sq"], 1)
                act.wait_ge(sem["gate_inv"], l + 1)
                act.activation(rs[:, :, :], rs[:, :, :], ACT.Sqrt).then_inc(sem["gate_rs"], 1)
                act.wait_ge(sem["y_normed"], l + 1)
                hi_of_x(5 * l + 2, hf)
                act_phase(act, ("ssd_out", l), KT // MT)
                act.wait_ge(sem["v_centered"], l + 1)
                act.activation(xcv[:, 0:KT, :], vb[:, :, :], ACT.Square).then_inc(sem["v_sq"], 1)
                act.wait_ge(sem["v_inv"], l + 1)
                act.activation(rs[:, 0, :], rs[:, 0, :], ACT.Sqrt).then_inc(sem["v_rs"], 1)
                act.wait_ge(sem["vs_turned"], l + 1)
                act.activation(xw[0:B, :], msf[0:B, 0:D], ACT.Copy).then_inc(sem["vs_copied"], 1)
                act.wait_ge(sem["st_out"], 16 * (l + 1))
                for c in range(NQ):
                    act.wait_ge(sem["v_tok"], l * NQ + c + 1)
                    act.activation(vtok[:, c, :], msf[:, 0:D], ACT.Copy).then_inc(sem["v_tok_ready"], 1)
                act.wait_ge(sem["sp_bcast"], l + 1)
                act.activation(spc[:, :, :].rearrange("p a b -> p (a b)"), ms[:, 0, 0:2 * KT], ACT.Copy) \
                    .then_inc(sem["sp_bcast_ready"], 1)
                act.wait_ge(sem["sp_taken"], l + 1)
                act.wait_ge(sem["w_used"], N0["cmlp_out", l])
                hi_of_x(5 * l + 3, ub)
                act_phase(act, ("cmlp_out", l), KT // MT)
                act.wait_ge(sem["merged"], 1 + l)
                hi_of_x(5 * l + 4, hf)
                act_phase(act, ("w_o", l), KT // MT, lambda i, c, banks: act.activation(
                    zs[:, bass.ds(4 * i + 2 * c, 2), :], banks, ACT.Copy))
                act.wait_ge(acc_free[0], Q0["gu", l, 0] // 2 + Q0["gu", l, 0] % 2)
                act.wait_ge(acc_free[1], Q0["gu", l, 0] // 2)
                norm_sq(4 * l + 2, zs)
                norm_rs(4 * l + 2)
                act.wait_ge(sem["x_ready"], 4 + 2 * l)
                norm_sq(4 * l + 3, x)
                norm_rs(4 * l + 3)
                act.wait_ge(sem["h_ready"], 2 * l + 2)
                hi_of_x(5 * l + 5, hf)
                act.wait_ge(sem["vs_out"], 16 * (l + 1))
                if l % 2:
                    act.wait_ge(sem["logits_ready"], 1)
                    act.wait_ge(sem["route_arg"], 1)
                    act.activation(lg[:, :, :], lg[:, :, :], ACT.Exp).then_inc(sem["route_exp"], 1)
                    act.wait_ge(sem["combine_turned"], 1)
                    act.activation(comb[:, :], ms[0:E, 2, 0:T], ACT.Copy).then_inc(sem["combine_ready"], 1)
                    for e in range(E):
                        act.wait_ge(sem["combine_spread"], e + 1)
                        act.activation(cbc[:, e, :], ms[:, e % 4, 0:T], ACT.Copy).then_inc(sem["combine_spread_ready"], 1)

                def expert(e, pairs_before, last):
                    n0, q0 = N0["gu", l, 0], Q0["gu", l, 0]

                    def gates(i):
                        split_hi(act, n0 + 1, i, 2, e)
                        act.wait_ge(sem["w_used"], n0 + 1 + 2 * i + EN * e)
                        act.wait_ge(sem["gu_ready"], pairs_before + i + FT // MT * e)
                        act.activation(sg[:, :, :], acc[:, 2 * (q0 % 2):2 * (q0 % 2) + 2, 0:T], ACT.Silu) \
                            .then_inc(acc_free[q0 % 2], 1)
                        split_hi(act, n0 + 2, i, 2, e)
                        act.wait_ge(sem["gu_ready"], pairs_before + 1 + i + FT // MT * e)
                        act.activation(ghi[:, bass.ds(2 * i, 2), :], gu[:, :, :], ACT.Copy).then_inc(sem["g_hi"], 1)

                    with act.Fori(0, FT // MT) as i:
                        gates(i)
                    n1 = N0["wd", l, 0]
                    C = 2 * len(KG)

                    def downs(i, last=False):
                        for c in range(C - (1 if last else 0)):
                            split_hi(act, n1 + c + 1, i, C, e)
                    if last:
                        downs(0)
                        downs(1, True)
                    else:
                        with act.Fori(0, KT // MT // 2) as i:
                            downs(i)

                act.preload_act_table(ACT.Silu)
                if l % 2 == 0:
                    expert(0, 1, False)
                else:
                    with act.Fori(0, E - 1) as e:
                        expert(e, 1 + FT // MT, False)
                    expert(E - 1, 1 + FT // MT, True)
                act.wait_ge(acc_free[0], Q0["wd", l, 0] // 2 + (KT // MT // 2) + (EQ // 2 * (E - 1) if l % 2 else 0)
                            + (Q0["wd", l, 0] % 2))
                act.wait_ge(acc_free[1], Q0["wd", l, 0] // 2 + (KT // MT // 2) + (EQ // 2 * (E - 1) if l % 2 else 0))
                norm_sq(4 * l + 4, facc)
                norm_rs(4 * l + 4)
                if l < L - 1:
                    act.wait_ge(sem["x_ready"], 5 + 2 * l)

        @block.vector
        def _(dve):
            steps = 0

            def then(ins):
                nonlocal steps
                steps += 1
                ins.then_inc(sem["dve_chain"], 1)
                dve.wait_ge(sem["dve_chain"], steps)

            def mean_inv(out, sums, count, done):
                then(dve.tensor_scalar(out, sums, 1.0 / count, EPS, ALU.mult, ALU.add))
                dve.reciprocal(out, out).then_inc(done, 1)

            def norm_inv(v):
                dve.wait_ge(sem["ssq_ready"], v)
                mean_inv(rs[:, 0, :], ms[:, 0, 0:T], D, sem["inv_ready"])

            def lo_of_x(v, src):
                dve.wait_ge(sem["xs_hi"], v)
                dve.tensor_tensor(xlo[:, :, :], src[:, :, :], xhi[:, :, :].bitcast(F32), ALU.subtract) \
                    .then_inc(sem["xs_lo"], 1)

            def modulated(l, k, v, hv):
                norm_inv(v)
                dve.wait_ge(sem["rs_ready"], v)
                then(dve.tensor_tensor(hf[:, :, :], x[:, :, :], bc(rs[:, 0, :], 1, [P, KT, T]), ALU.mult))
                sh, sc = mod[:, l, 3 * k * KT:(3 * k + 1) * KT, :], mod[:, l, (3 * k + 1) * KT:(3 * k + 2) * KT, :]
                for t in range(KT):
                    dve.tensor_scalar(hf[:, t, 0:S], hf[:, t, 0:S], sc[:, t, 0:1], sh[:, t, 0:1], ALU.mult, ALU.add)
                then(dve.tensor_tensor(hf[:, :, S:T], hf[:, :, S:T], sc[:, :, 1:1 + B], ALU.mult))
                dve.tensor_tensor(hf[:, :, S:T], hf[:, :, S:T], sh[:, :, 1:1 + B], ALU.add).then_inc(sem["h_ready"], 1)

            def add_normed(l, k, v, src):
                norm_inv(v)
                dve.wait_ge(sem["rs_ready"], v)
                then(dve.tensor_tensor(src[:, :, :], src[:, :, :], bc(rs[:, 0, :], 1, [P, KT, T]), ALU.mult))
                g = mod[:, l, (3 * k + 2) * KT:(3 * k + 3) * KT, :]
                for t in range(KT):
                    dve.scalar_tensor_tensor(out=x[:, t, 0:S], in0=src[:, t, 0:S], scalar=g[:, t, 0:1],
                                             in1=x[:, t, 0:S], op0=ALU.mult, op1=ALU.add)
                then(dve.tensor_tensor(src[:, :, S:T], src[:, :, S:T], g[:, :, 1:1 + B], ALU.mult))
                dve.tensor_tensor(x[:, :, S:T], x[:, :, S:T], src[:, :, S:T], ALU.add).then_inc(sem["x_ready"], 1)

            dve.memset(ctok[0:NC, :], 0.0).then_inc(sem["ctok_zero"], 1)
            dve.memset(cst[:, :, :].bitcast(F32), 0.0).then_inc(sem["cst_zero"], 1)
            then(dve.memset(ones[:, :], 1.0))
            dve.wait_ge(sem["c_hi"], 1)
            dve.tensor_tensor(cst[:, :, CL:CL + NC], ms[:, 0, 0:KT * NC].rearrange("p (k c) -> p k c", k=KT),
                              cst[:, :, 0:NC].bitcast(F32), ALU.subtract).then_inc(sem["c_lo"], 1)
            dve.wait_ge(sem["params_turned"], 1)
            dve.tensor_copy(PT[:, :, :].rearrange("p l r -> p (l r)"), ms[:, 1, 0:L * NROW]) \
                .then_inc(sem["params_ready"], 1)
            dve.wait_ge(sem["params_ready"], 1)
            b0 = ROWS["b_mod"][0]
            dve.tensor_copy(bmod.rearrange("p (l r) -> p l r", l=L), PT[:, :, b0:b0 + 6 * KT])
            dve.wait_ge(sem["state_turned"], 1)
            dve.tensor_copy(stT[:, :, :, :].rearrange("p l c r -> p l (c r)"), ms[:, 2:4, 0:CT * B * (CK - 1)]) \
                .then_inc(sem["state_ready"], 1)
            for c in range(NQ + 1):
                rows = Q if c < NQ else B
                dve.wait_ge(sem["x_turned"], c + 1)
                b0 = 2 * (c % 2)
                dve.tensor_copy(x[:, :, c * Q:c * Q + rows].rearrange("p (b k) t -> p b k t", b=2),
                                ms[:, b0:b0 + 2, :].rearrange("p b (k t) -> p b k t", t=P)[:, :, :, 0:rows]) \
                    .then_inc(sem["x_ready"], 1)
            NM = N0["xbc", 0]

            def mod_lo(m, s):
                dve.wait_ge(sem["hi_ready"], m + 1)
                dve.tensor_tensor(wlo[s], raw[s], whi[s].bitcast(F32), ALU.subtract).then_inc(sem["lo_ready"], 1)

            def mod_add(m, s):
                dve.wait_ge(sem["folded"], m + 1)
                c0 = MT * m if isinstance(m, int) else dve.snap(MT * m)
                dve.tensor_tensor(modf[:, bass.ds(c0, MT), :], ms[:, s, 0:MT * NC].rearrange("p (j c) -> p j c", j=MT),
                                  bc(bmod[:, bass.ds(c0, MT)], 2, [P, MT, NC]), ALU.add).then_inc(sem["mod_added"], 1)

            def mod_body(i, last=False):
                for c in range(R3):
                    if not (last and c == R3 - 1):
                        mod_lo(R3 * i + c + 1, (c + 1) % R3)
                    if later(i, 1):
                        mod_add(R3 * i + c - R3, c)
            mod_lo(0, 0)
            mod_body(0)
            with dve.Fori(0, NM // R3 - 2) as i:
                mod_body(i + 1)
            mod_body(NM // R3 - 1, True)
            for m in range(NM - R3, NM):
                mod_add(m, m % R3)
            dve.wait_ge(sem["mod_added"], NM)
            for l in range(L):
                for k, (pre, post) in enumerate((("mix_pre_g", "mix_post_g"), ("ffn_pre_g", "ffn_post_g"))):
                    sc = mod[:, l, (3 * k + 1) * KT:(3 * k + 2) * KT, :]
                    g = mod[:, l, (3 * k + 2) * KT:(3 * k + 3) * KT, :]
                    dve.scalar_tensor_tensor(out=sc, in0=sc, scalar=1.0, in1=bc(row(pre, l), 2, [P, KT, NC]),
                                             op0=ALU.add, op1=ALU.mult)
                    ins = dve.tensor_tensor(g, g, bc(row(post, l), 2, [P, KT, NC]), ALU.mult)
            ins.then_inc(sem["mod_ready"], 1)
            dve.wait_ge(sem["mod_ready"], 1)

            split_lo(dve, N0["xbc", 0], 0)
            for l in range(L):
                modulated(l, 0, 4 * l + 1, 2 * l + 1)
                lo_of_x(5 * l + 1, hf)
                ins = dve.memset(xrawv[:, :, 0:CK - 1], 0.0)
                then(ins)
                dve_phase(dve, ("xbc", l), IN_CHUNKS["xbc"])
                n, q = N0["dt", l], Q0["dt", l]
                split_lo(dve, n + 1, 0)
                dve.wait_ge(sem["w_used"], n + 1)
                dve.tensor_scalar(dth[:, 1, :], acc[0:H, 2 * (q % 2), 0:T], headp[:, 0, l:l + 1], None, ALU.add) \
                    .then_inc(acc_free[q % 2], 1)
                for name in ("z", "u", "v", "ga", "gb"):
                    dve_phase(dve, (name, l), IN_CHUNKS[name])

                for k in range(CK):
                    for t in range(CT):
                        src = xrawv[:, t, k:k + S]
                        if k == 0:
                            ins = dve.tensor_scalar(xcv[:, t, 0:S], src, row("conv_w", l, t), row("conv_b", l, t),
                                                    ALU.mult, ALU.add)
                        else:
                            ins = dve.scalar_tensor_tensor(out=xcv[:, t, 0:S], in0=src, scalar=row("conv_w", l, k * CT + t),
                                                           in1=xcv[:, t, 0:S], op0=ALU.mult, op1=ALU.add)
                    then(ins)
                st = stT[:, l, :, :].rearrange("p c (b k) -> p c b k", k=CK - 1)
                wk = row("conv_w", l).rearrange("p (k c) -> p k c", k=CK)
                xs_ = xcv[:, :, S:T]
                then(dve.tensor_tensor(xs_, xrawv[:, :, CK - 1 + S:CK - 1 + T],
                                       bc(wk[:, CK - 1, :], 2, [P, CT, B]), ALU.mult))
                for k in range(CK - 1):
                    then(dve.tensor_tensor(tmp[:, :, :], st[:, :, :, k], bc(wk[:, k, :], 2, [P, CT, B]), ALU.mult))
                    then(dve.tensor_tensor(xs_, xs_, tmp[:, :, :], ALU.add))
                dve.tensor_tensor(xs_, xs_, bc(row("conv_b", l), 2, [P, CT, B]), ALU.add).then_inc(sem["conv_done"], 1)

                cum, dt, dta, e_, r_, s2, p_, mx = (dth[:, k, :] for k in range(8))
                dve.scalar_tensor_tensor(out=e_, in0=dt, scalar=-1.0, in1=dt, op0=ALU.mult, op1=ALU.max) \
                    .then_inc(sem["dt_abs"], 1)
                dve.tensor_scalar(mx, dt, 0.0, None, ALU.max)
                dve.wait_ge(sem["dt_exp"], l + 1)
                then(dve.tensor_scalar(r_, e_, 2.0, None, ALU.add))
                then(dve.reciprocal(r_, r_))
                then(dve.tensor_tensor(r_, e_, r_, ALU.mult))
                then(dve.tensor_tensor(s2, r_, r_, ALU.mult))
                then(dve.tensor_scalar(p_, s2, 1.0 / 17, None, ALU.mult))
                for k in range(15, 1, -2):
                    then(dve.scalar_tensor_tensor(out=p_, in0=p_, scalar=1.0 / k, in1=s2, op0=ALU.add, op1=ALU.mult))
                then(dve.scalar_tensor_tensor(out=p_, in0=p_, scalar=1.0, in1=r_, op0=ALU.add, op1=ALU.mult))
                then(dve.scalar_tensor_tensor(out=dt, in0=p_, scalar=2.0, in1=mx, op0=ALU.mult, op1=ALU.add))
                dve.wait_ge(sem["a_exp"], 1)
                then(dve.tensor_scalar(dta, dt, expa[:, l:l + 1], -1.0, ALU.mult, ALU.mult))
                for c in range(NQ):
                    dve.tensor_tensor_scan(cum[:, c * Q:(c + 1) * Q], ones[0:H, 0:Q], dta[:, c * Q:(c + 1) * Q], 0.0,
                                           ALU.mult, ALU.add)
                dve.tensor_copy(spin[:, B:2 * B], dt[:, S:T])
                dve.tensor_copy(spin[:, 2 * B:2 * B + 1], headp[:, 2, l:l + 1]).then_inc(sem["cum_ready"], 1)

                for c in range(NQ):
                    v = l * NQ + c
                    toks = slice(c * Q, (c + 1) * Q)
                    dve.wait_ge(sem["b_tok"], v + 1)
                    dve.tensor_copy(tokp[:, :, :].rearrange("p a h -> p (a h)"), ms[:, 2, 2 * P:2 * P + 2 * H]) \
                        .then_inc(sem["tok_ready"], 1)
                    dve.wait_ge(sem["tok_ready"], v + 1)
                    dve.tensor_tensor(xdt[:, :].rearrange("p (h d) -> p h d", h=H),
                                      msf[:, 0:D].rearrange("p (h d) -> p h d", h=H),
                                      bc(tokp[:, 1, :], 2, [P, H, HD]), ALU.mult).then_inc(sem["xdt_ready"], 1)
                    dve.wait_ge(sem["cb_ready"], v + 1)
                    dve.tensor_tensor(cbm[:, :, :], ms[:, 3, 0:G * Q].rearrange("p (g q) -> p g q", g=G),
                                      bc(tri[:, :], 1, [P, G, Q]), ALU.mult).then_inc(sem["cbm_ready"], 1)
                    dve.wait_ge(sem["cumb_ready"], v + 1)
                    last = ms[:, :, :].rearrange("p b (h q) -> p (b h) q", q=Q)[:, :, Q - 1]
                    then(dve.tensor_copy(lastc[:, :], last))
                    dve.tensor_tensor(wend[:, :], lastc[:, :], tokp[:, 0, :], ALU.subtract).then_inc(sem["wend_arg"], 1)
                    for h in range(H):
                        cs = tokp[:, 0, h:h + 1]
                        ins = dve.tensor_scalar(mix[:, h, :], ms[:, h // 4, (h % 4) * Q:(h % 4 + 1) * Q], cs, cs,
                                                ALU.min, ALU.subtract)
                    ins.then_inc(sem["seg_ready"], 1)
                    dve.wait_ge(sem["wend_ready"], v + 1)
                    dve.tensor_tensor(xw[:, :].rearrange("p (h d) -> p h d", h=H),
                                      xdt[:, :].rearrange("p (h d) -> p h d", h=H),
                                      bc(wend[:, :], 2, [P, H, HD]), ALU.mult).then_inc(sem["xw_ready"], 1)
                    if c:
                        dve.wait_ge(sem["ce_exp"], l + 1)
                        for g in range(G):
                            ins = dve.tensor_tensor(ce[:, g * R:(g + 1) * R, :], ce[:, g * R:(g + 1) * R, :],
                                                    bc(xcv[:, KT + G + g, toks], 1, [P, R, Q]), ALU.mult)
                        ins.then_inc(sem["ce_ready"], 1)
                    dve.wait_ge(sem["mix_exp"], v + 1)
                    for g in range(G):
                        ins = dve.tensor_tensor(mix[:, g * R:(g + 1) * R, :], mix[:, g * R:(g + 1) * R, :],
                                                bc(cbm[:, g, :], 1, [P, R, Q]), ALU.mult)
                    ins.then_inc(sem["mix_ready"], 1)
                    dve.wait_ge(sem["spread_copied"], l + 1)
                    dve.wait_ge(sem["y_part"], v + 1)
                    for t in range(KT):
                        ins = dve.scalar_tensor_tensor(out=hf[:, t, toks], in0=xcv[:, t, toks],
                                                       scalar=spx[:, t, 2 * B:2 * B + 1],
                                                       in1=ms[:, t // 4, (t % 4) * Q:(t % 4 + 1) * Q],
                                                       op0=ALU.mult, op1=ALU.add)
                    ins.then_inc(sem["y_taken"], 1)
                    if c:
                        dve.wait_ge(sem["last_ready"], v + 1)
                        hv = hT[:, :].rearrange("p (h d) -> p h d", h=H)
                        then(dve.tensor_tensor(hv, hv, bc(elast[:, :], 2, [P, H, HD]), ALU.mult))
                        dve.wait_ge(sem["st_part"], v + 1)
                        dve.tensor_tensor(hT[:, :], hT[:, :], msf[:, 1024:2048], ALU.add).then_inc(sem["st_ready"], 1)

                then(dve.tensor_tensor(dtx[:, :, :], xcv[:, 0:KT, S:T], spx[:, :, B:2 * B], ALU.mult))
                for b in range(B):
                    s = b % 2
                    dve.wait_ge(sem["bc_spread"], l * B + b + 1)
                    if b:
                        dve.wait_ge(sem["samp_used"], l * B + b)
                    Sb = sring[:, s]
                    def bcast(g0):
                        return (ms[:, b % 2, g0 * P:(g0 + G) * P].rearrange("p (g n) -> p g n", g=G)
                                .unsqueeze(2).to_broadcast([P, G, KT // G, P]))
                    Pv = sprod.rearrange("p (g k) n -> p g k n", g=G)
                    Sv = Sb.rearrange("p (g k) n -> p g k n", g=G)
                    dve.tensor_tensor(Pv, bcast(0), bc(dtx[:, :, b], 2, [P, KT, P]).rearrange(
                        "p (g k) n -> p g k n", g=G), ALU.mult)
                    dve.wait_ge(s_in[s], 16 * (l * B // 2 + b // 2 + 1))
                    then(dve.tensor_tensor(Sb, Sb, bc(spx[:, :, b], 2, [P, KT, P]), ALU.mult))
                    dve.tensor_tensor(Sb, Sb, sprod, ALU.add).then_inc(sem["s_new"], 1)
                    dve.wait_ge(sem["s_new"], l * B + b + 1)
                    then(dve.tensor_tensor(Pv, Sv, bcast(G), ALU.mult))
                    dve.tensor_reduce(ysm[:, :, b], sprod, AX.X, ALU.add).then_inc(sem["samp_used"], 1)
                dve.wait_ge(sem["samp_used"], (l + 1) * B)
                then(dve.tensor_tensor(hf[:, :, S:T], xcv[:, 0:KT, S:T],
                                       spx[:, :, 2 * B:2 * B + 1].to_broadcast([P, KT, B]), ALU.mult))
                then(dve.tensor_tensor(hf[:, :, S:T], hf[:, :, S:T], ysm[:, :, :], ALU.add))
                dve.tensor_tensor(hf[:, :, :], hf[:, :, :], zs[:, :, :], ALU.mult).then_inc(sem["samp_done"], 1)
                dve.wait_ge(sem["gate_ssq"], l + 1)
                mean_inv(rs[:, :, :], ms[:, 2:4, 0:T], D // G, sem["gate_inv"])
                dve.wait_ge(sem["gate_rs"], l + 1)
                for g in range(G):
                    k0, k1 = g * KT // G, (g + 1) * KT // G
                    ins = dve.tensor_tensor(hf[:, k0:k1, :], hf[:, k0:k1, :], bc(rs[:, g, :], 1, [P, KT // G, T]),
                                            ALU.mult)
                then(ins)
                dve.tensor_tensor(hf[:, :, :], hf[:, :, :], bc(row("ssm_norm_g", l), 2, [P, KT, T]), ALU.mult) \
                    .then_inc(sem["y_normed"], 1)
                lo_of_x(5 * l + 2, hf)
                dve_phase(dve, ("ssd_out", l), KT // MT, lambda i, c, banks: dve.tensor_tensor(
                    sga[:, bass.ds(4 * i + 2 * c, 2), :], sga[:, bass.ds(4 * i + 2 * c, 2), :], banks, ALU.mult))

                dve.wait_ge(sem["v_sum"], l + 1)
                then(dve.tensor_scalar(rs[:, 1, :], ms[:, 0, 0:T], 1.0 / D, None, ALU.mult))
                dve.tensor_tensor(vb[:, :, :], vb[:, :, :], bc(rs[:, 1, :], 1, [P, KT, T]), ALU.subtract) \
                    .then_inc(sem["v_centered"], 1)
                dve.wait_ge(sem["v_ssq"], l + 1)
                mean_inv(rs[:, 0, :], ms[:, 1, 0:T], D, sem["v_inv"])
                dve.wait_ge(sem["v_rs"], l + 1)
                then(dve.tensor_tensor(vb[:, :, :], vb[:, :, :], bc(rs[:, 0, :], 1, [P, KT, T]), ALU.mult))
                for t in range(KT):
                    ins = dve.tensor_scalar(vb[:, t, :], vb[:, t, :], row("cmlp_ln_g", l, t), row("cmlp_ln_b", l, t),
                                            ALU.mult, ALU.add)
                ins.then_inc(sem["v_normed"], 1)
                dve.wait_ge(sem["sp_in"], 16 * (4 + L))
                dve.tensor_scalar(diag[:, 0, :], ident[0:KT, 0:KT], w00[:, l:l + 1], None, ALU.mult)
                dve.tensor_scalar(diag[:, 1, :], ident[0:KT, 0:KT], spb[:, l, 0:1], None, ALU.mult) \
                    .then_inc(sem["diag_ready"], 1)
                dve.wait_ge(sem["w_turned"], l + 1)
                dve.tensor_tensor(wT, msf[:, 1024:2048].rearrange("p (g q) -> p g q", g=KT),
                                  bc(tri[:, :], 1, [P, KT, Q]), ALU.mult).then_inc(sem["w_ready"], 1)
                dve.wait_ge(sem["v_normed"], l + 1)
                dve.wait_ge(sem["sp_bcast_ready"], l + 1)
                g0 = ysm[:, :, :]
                then(dve.tensor_tensor(g0, vb[:, :, S:T], bc(spc[:, 0, :], 2, [P, KT, B]), ALU.mult))
                then(dve.tensor_tensor(g0, g0, bc(spc[:, 1, :], 2, [P, KT, B]), ALU.add))
                dve.tensor_tensor(ub[:, :, S:T], ub[:, :, S:T], g0, ALU.mult)
                for c in range(NQ):
                    dve.wait_ge(sem["sp_out"], l * NQ + c + 1)
                    ins = dve.tensor_tensor(ub[:, :, c * Q:(c + 1) * Q], ub[:, :, c * Q:(c + 1) * Q],
                                            msf[:, c * 1024:(c + 1) * 1024].rearrange("p (k q) -> p k q", k=KT), ALU.mult)
                ins.then_inc(sem["sp_taken"], 1)
                lo_of_x(5 * l + 3, ub)
                dve_phase(dve, ("cmlp_out", l), KT // MT, lambda i, c, banks: dve.tensor_tensor(
                    sgb[:, bass.ds(4 * i + 2 * c, 2), :], sgb[:, bass.ds(4 * i + 2 * c, 2), :], banks, ALU.mult))
                for p in range(2):
                    dve.wait_ge(acc_free[p], (Q0["w_o", l] + 1 - p) // 2)
                dve.tensor_tensor(hf[:, :, :], sga[:, :, :], sgb[:, :, :], ALU.add).then_inc(sem["merged"], 1)
                lo_of_x(5 * l + 4, hf)
                dve_phase(dve, ("w_o", l), KT // MT)
                add_normed(l, 0, 4 * l + 2, zs)
                dve.wait_ge(sem["x_ready"], 4 + 2 * l)
                modulated(l, 1, 4 * l + 3, 2 * l + 2)
                lo_of_x(5 * l + 5, hf)
                dve.wait_ge(sem["vs_out"], 16 * (l + 1))

                if l % 2:
                    dve.wait_ge(sem["logits_ready"], 1)
                    then(dve.memset(lg[:, :, :], 0.0))
                    then(dve.tensor_copy(lg[:, 0:NQ, :], ms[:, 1, 0:NQ * E].rearrange("p (c e) -> p c e", e=E)))
                    then(dve.tensor_copy(lg[0:B, NQ, :], ms[0:B, 1, NQ * E:(NQ + 1) * E]))
                    for c in range(3):
                        mine, other = bc(lg[:, c, :], 2, [P, E, E]), bc(lg[:, c, :], 1, [P, E, E])
                        dve.tensor_reduce(top[:, c, 0:1], lg[:, c, :], AX.X, ALU.max)
                        then(dve.tensor_tensor(eqm[:, :, :], other, mine, ALU.is_equal))
                        then(dve.tensor_tensor(eqm[:, :, :], eqm[:, :, :], earlier[:, :, :], ALU.mult))
                        then(dve.tensor_tensor(cmp_[:, :, :], other, mine, ALU.is_gt))
                        then(dve.tensor_tensor(cmp_[:, :, :], cmp_[:, :, :], eqm[:, :, :], ALU.add))
                        then(dve.tensor_reduce(rank[:, c, :], cmp_[:, :, :], AX.X, ALU.add))
                    then(dve.tensor_scalar(rank[:, :, :], rank[:, :, :], 1.5, None, ALU.is_lt))
                    dve.tensor_tensor(lg[:, :, :], lg[:, :, :], top[:, :, 0:1].to_broadcast([P, 3, E]), ALU.subtract) \
                        .then_inc(sem["route_arg"], 1)
                    dve.wait_ge(sem["route_exp"], 1)
                    then(dve.tensor_tensor(rank[:, :, :], rank[:, :, :], lg[:, :, :], ALU.mult))
                    then(dve.tensor_reduce(rsum[:, :], rank[:, :, :], AX.X, ALU.add))
                    then(dve.reciprocal(rsum[:, :], rsum[:, :]))
                    dve.tensor_tensor(rank[:, :, :], rank[:, :, :], bc(rsum[:, :], 2, [P, 3, E]), ALU.mult) \
                        .then_inc(sem["route_done"], 1)
                    dve.wait_ge(sem["combine_spread_ready"], E)
                if l == 0:
                    dve.memset(facc[:, :, :], 0.0).then_inc(sem["gu_ready"], 1)
                    dve.wait_ge(sem["gu_ready"], 1)
                else:
                    then(dve.memset(facc[:, :, :], 0.0))

                def expert(e, gated, last):
                    n0, q0 = N0["gu", l, 0], Q0["gu", l, 0]
                    gb = 0 if l % 2 == 0 else FT // MT

                    def gates(i):
                        split_lo(dve, n0 + 1, i, 2, e)
                        pair = (q0 + 1) % 2
                        split_lo(dve, n0 + 2, i, 2, e)
                        dve.wait_ge(sem["w_used"], n0 + 2 + 2 * i + EN * e)
                        dve.wait_ge(acc_free[q0 % 2], q0 // 2 + 1 + i + EQ // 2 * e)
                        up = acc[:, 2 * pair:2 * pair + 2, 0:T]
                        if gated:
                            dve.tensor_tensor(sg[:, :, :], sg[:, :, :], cbc[:, bass.ds(e, 1), :].to_broadcast([P, MT, T]),
                                              ALU.mult).then_inc(sem["sg_ready"], 1)
                            dve.wait_ge(sem["sg_ready"], 1 + i + FT // MT * e)
                        dve.tensor_tensor(gu[:, :, :], sg[:, :, :], up, ALU.mult).then_inc(sem["gu_ready"], 1)
                        dve.wait_ge(sem["g_hi"], gb + 1 + i + FT // MT * e)
                        dve.tensor_tensor(glo[:, bass.ds(2 * i, 2), :], gu[:, :, :],
                                          ghi[:, bass.ds(2 * i, 2), :].bitcast(F32), ALU.subtract) \
                            .then_inc(acc_free[pair], 1)
                    with dve.Fori(0, FT // MT) as i:
                        gates(i)
                    n1, q1 = N0["wd", l, 0], Q0["wd", l, 0]
                    C = 2 * len(KG)

                    def downs(i, last=False):
                        for g in range(2):
                            for s in range(len(KG)):
                                c = g * len(KG) + s
                                if not (last and c == C - 1):
                                    split_lo(dve, n1 + c + 1, i, C, e)
                            dve.wait_ge(sem["w_used"], n1 + g * len(KG) + len(KG) + C * i + EN * e)
                            pair = (q1 + g) % 2
                            f = facc[:, bass.ds(4 * i + 2 * g, 2), :]
                            dve.tensor_tensor(f, f, acc[:, 2 * pair:2 * pair + 2, 0:T], ALU.add) \
                                .then_inc(acc_free[pair], 1)
                    if last:
                        downs(0)
                        downs(1, True)
                    else:
                        with dve.Fori(0, KT // MT // 2) as i:
                            downs(i)

                if l % 2 == 0:
                    expert(0, False, False)
                else:
                    with dve.Fori(0, E - 1) as e:
                        expert(e, True, False)
                    expert(E - 1, True, True)
                add_normed(l, 1, 4 * l + 4, facc)
                dve.wait_ge(sem["x_ready"], 5 + 2 * l)

            for c in range(NQ + 1):
                rows = Q if c < NQ else B
                dve.wait_ge(sem["y_turned"], c + 1)
                dve.tensor_copy(xtok[0:rows, c * D:(c + 1) * D], msf[0:rows, (c % 2) * D:(c % 2 + 1) * D]) \
                    .then_inc(sem["y_copied"], 1)


_VECTORS = ["b_mod", "mix_pre_g", "mix_post_g", "ffn_pre_g", "ffn_post_g", "conv_b", "ssm_norm_g", "cmlp_ln_g",
            "cmlp_ln_b"]


def kernel(**inputs):
    import numpy as _np
    import concourse.bacc as _bacc
    from concourse import mybir as _mybir
    from concourse.bass_utils import run_bass_kernel_spmd as _run

    nc = _bacc.Bacc("TRN2", target_bir_lowering=False, num_devices=1)
    arrays, args = {}, {}
    for name, a in inputs.items():
        a = _np.ascontiguousarray(a)
        arrays[f"in_{name}_dram"] = a
        args[name] = nc.dram_tensor(f"in_{name}_dram", a.shape, _mybir.dt.from_np(a.dtype), kind="ExternalInput").ap()
    depth, samples, heads, head_dim, states = inputs["state_ssm"].shape
    _, _, rows, conv_dim = inputs["state_conv"].shape
    batch, seq, width = inputs["x_prompt"].shape
    outs = {
        "y_p": (batch, seq, width), "y_s": tuple(inputs["x_sample"].shape),
        "ssm_p": (depth, batch, heads, head_dim, states), "conv_p": (depth, batch, rows, conv_dim),
        "ssm_s": (depth, samples, heads, head_dim, states), "conv_s": (depth, samples, rows, conv_dim),
        "v_s": (depth, samples, 1, width),
    }
    handles = {name: nc.dram_tensor(f"out_{name}_dram", shape, _mybir.dt.float32, kind="ExternalOutput").ap()
               for name, shape in outs.items()}
    args["vectors"] = {name: args[name] for name in _VECTORS}
    hybrid_ssd_chunkmlp_moe_step(nc, args, handles)
    r = _run(nc, [arrays], core_ids=[0])
    return tuple(r.results[0][f"out_{name}_dram"] for name in outs)
```

```python
from contextlib import ExitStack

import concourse.bass as bass
from concourse import mybir

F32 = mybir.dt.float32
F32R = mybir.dt.float32r
ALU = mybir.AluOpType
ACT = mybir.ActivationFunctionType
AX = mybir.AxisListType

P = 128
MT = 2
CW = MT * P

SEMAPHORES = """params_in ctok_zero c_in x_in states_in ident_zero consts
c_silu c_turned cst_zero c_hi c_lo mt_ready folded mod_added params_turned params_ready state_turned state_ready x_turned x_ready
raw_full0 raw_full1 raw_full2 hi_ready lo_ready w_used acc_free0 acc_free1
sq_ready ssq_ready inv_ready rs_ready h_ready xs_hi xs_lo mod_ready a_exp
conv_done xc_ready tail_turned tail_ready tail_out
dt_abs dt_exp cum_ready samp_decay spread_ready spread_copied
tok_ready x_tok b_tok xdt_ready bt_ready cb_ready cbm_ready cumb_ready seg_ready ce_exp
last_ready wend_arg wend_ready mix_exp mix_ready ce_ready xw_ready y_part y_taken st_part st_ready
st_turned st_copied st_out
bc_turned bc_ready bc_spread s_in0 s_in1 s_new s_out0 s_out1 samp_used samp_done
gate_sq gate_ssq gate_inv gate_rs
v_sum v_centered v_sq v_ssq v_inv v_rs v_normed vs_turned vs_copied vs_out v_tok v_tok_ready
w_sp_in w_turned w_ready sp_in diag_ready sp_bcast sp_bcast_ready sp_out sp_taken
sg_ready gu_ready g_hi route_in logits_ready route_exp route_done combine_turned combine_ready
combine_spread combine_spread_ready sel_ready counted flag_ready
h_turned htok_hi htok_lo g_built gathered hg_hi hg_lo gw_turned gw_ready gate_ready gu_done gu_turned gt_hi gt_lo
ys_ready scattered scat_added moe_done
route_arg y_normed merged y_turned y_copied y_out conv_keep dve_chain""".split()


def hybrid_ssd_chunkmlp_moe_step(nc, A, O):
    D = A["x_prompt"].shape[2]
    S = A["x_prompt"].shape[1]
    B = A["x_sample"].shape[0]
    L = A["w_in"].shape[0]
    T = S + B
    KT = D // P
    H = A["a_log"].shape[1]
    HD = D // H
    NS = A["state_ssm"].shape[-1]
    CD = A["conv_w"].shape[2]
    CT = CD // P
    CK = A["conv_w"].shape[1]
    G = (CD - D) // (2 * NS)
    R = H // G
    F = A["ffn_wg"].shape[2]
    FT = F // P
    E = A["exp_wg"].shape[1]
    Q = 128
    NQ = S // Q
    EPS = 1e-6
    NC = B + 2
    CL = 32
    R3 = 3
    assert D == 1024 and T % 2 == 0 and NS == P and 2 * HD == P and F % CW == 0 and NQ == 2 and B == E == 8

    IN_COL = {"xbc": D, "z": 0}
    at = D + CD + H
    for name in ("u", "v", "ga", "gb"):
        IN_COL[name] = at
        at += D
    IN_CHUNKS = {"xbc": CD // CW, "z": D // CW, "u": D // CW, "v": D // CW, "ga": D // CW, "gb": D // CW}
    KG = [(k, min(KT, FT - k)) for k in range(0, FT, KT)]

    N0, Q0 = {}, {}
    n = q = 0

    def phase(key, chunks, groups):
        nonlocal n, q
        N0[key], Q0[key] = n, q
        n += chunks
        q += groups

    phase("mod", L * 6 * KT // MT, 0)
    M3 = n // R3
    for l in range(L):
        for name in ("xbc", "dt", "v", "u", "z", "ga", "gb"):
            k = IN_CHUNKS.get(name, 1)
            phase((name, l), k, k)
        for name in ("cmlp_out", "ssd_out", "w_o"):
            phase((name, l), KT // MT, KT // MT)
        phase(("gu", l), 2 * FT // MT, 2 * FT // MT)
        phase(("wd", l), len(KG) * KT // MT, KT // MT)
    EN = 2 * FT // MT + len(KG) * KT // MT
    EQ = 2 * FT // MT + KT // MT

    FP = FT // MT
    DK = KT * CW // D
    FD = FT // DK
    SN = 2 * FP + FD
    assert L == 2 and SN % R3 == 0 and FP == FD and FP % R3 == 2

    ROWS = {}
    at = 0
    for name, rows in (("b_mod", 6 * KT), ("mix_pre_g", KT), ("mix_post_g", KT), ("ffn_pre_g", KT),
                       ("ffn_post_g", KT), ("conv_w", CK * CT), ("conv_b", CT), ("ssm_norm_g", KT),
                       ("cmlp_ln_g", KT), ("cmlp_ln_b", KT)):
        ROWS[name] = (at, rows)
        at += rows
    NROW = at
    RT = -(-NROW // P)
    assert ROWS["conv_b"][0] == P

    ctx = ExitStack()
    with ctx:
        def sb(name, shape, dt=F32, where=ctx):
            return where.enter_context(nc.sbuf_tensor(name, shape, dt))

        raw01 = sb("raw01", [P, 2, KT, CW])
        whi01 = sb("whi01", [P, 2, KT, CW], F32R)
        wlo01 = sb("wlo01", [P, 2, KT, CW], F32R)
        x = sb("x", [P, KT, T])
        hf = sb("hf", [P, KT, T])
        xhi = sb("xhi", [P, KT, T], F32R)
        xlo = sb("xlo", [P, KT, T], F32R)
        rs = sb("rs", [P, 2, T])
        ident = sb("ident", [P, P])
        ones = sb("ones", [P, P])
        tri = sb("tri", [P, P])
        earlier = sb("earlier", [P, E, E])
        spread = sb("spread", [H, D])
        PT = sb("PT", [P, L, NROW])
        mod = sb("mod", [P, L, 6 * KT, NC])
        fold = sb("fold", [CL + NC, NC])
        stT = sb("stT", [P, L, CT, B * (CK - 1)])
        headp = sb("headp", [H, 3, L])
        expa = sb("expa", [H, L])
        rw = sb("rw", [P, KT, E])
        rb = sb("rb", [1, E])
        spb = sb("spb", [KT, L, Q])
        w00 = sb("w00", [KT, L])

        mixer = ExitStack()
        zs = sb("zs", [P, KT, T], F32, mixer)
        ub = sb("ub", [P, KT, T], F32, mixer)
        vb = sb("vb", [P, KT, T], F32, mixer)
        sga = sb("sga", [P, KT, T], F32, mixer)
        sgb = sb("sgb", [P, KT, T], F32, mixer)
        xraw = sb("xraw", [P, CT * (CK - 1 + T)], F32, mixer)
        xrawv = xraw[:, :].rearrange("p (c t) -> p c t", c=CT)
        xc = sb("xc", [P, CT * T], F32, mixer)
        xcv = xc[:, :].rearrange("p (c t) -> p c t", c=CT)
        xdt = sb("xdt", [P, D], F32, mixer)
        xw = sb("xw", [P, D], F32, mixer)
        mix = sb("mix", [P, H, Q], F32, mixer)
        ce = sb("ce", [P, H, Q], F32, mixer)
        hT = sb("hT", [P, D], F32, mixer)
        bt = sb("bt", [P, G, Q], F32, mixer)
        cbm = sb("cbm", [P, G, Q], F32, mixer)
        dth = sb("dth", [H, 8, T], F32, mixer)
        spin = sb("spin", [H, 2 * B + 1], F32, mixer)
        spx = sb("spx", [P, KT, 2 * B + 1], F32, mixer)
        tokp = sb("tokp", [P, 2, H], F32, mixer)
        lastc = sb("lastc", [P, H], F32, mixer)
        wend = sb("wend", [P, H], F32, mixer)
        elast = sb("elast", [P, H], F32, mixer)
        bct = sb("bct", [B, 4 * P], F32, mixer)
        dtx = sb("dtx", [P, KT, B], F32, mixer)
        ysm = sb("ysm", [P, KT, B], F32, mixer)
        tmp = sb("tmp", [P, CT, B], F32, mixer)
        diag = sb("diag", [KT, 2, KT], F32, mixer)
        spc = sb("spc", [P, 2, KT], F32, mixer)
        mixer.close()
        ffn = ExitStack()
        raw2 = sb("raw2", [P, KT, CW], F32, ffn)
        whi2 = sb("whi2", [P, KT, CW], F32R, ffn)
        wlo2 = sb("wlo2", [P, KT, CW], F32R, ffn)
        cst = sb("cst", [P, KT, P], F32R, ffn)
        facc = sb("facc", [P, KT, T], F32, ffn)
        lg = sb("lg", [P, 3, E], F32, ffn)
        cmp_ = sb("cmp_", [P, E, E], F32, ffn)
        eqm = sb("eqm", [P, E, E], F32, ffn)
        rank = sb("rank", [P, 3, E], F32, ffn)
        top = sb("top", [P, 3, 8], F32, ffn)
        rsum = sb("rsum", [P, 3], F32, ffn)
        sel = sb("sel", [P, 3, E], F32, ffn)
        place = sb("place", [P, 4, E], F32, ffn)
        most = sb("most", [P, 1], F32, ffn)
        flag = sb("flag", [P, 1], mybir.dt.int32, ffn)
        dense = ExitStack()
        ghi = sb("ghi", [P, FT, T], F32R, dense)
        glo = sb("glo", [P, FT, T], F32R, dense)
        sg = sb("sg", [P, MT, T], F32, dense)
        gu = sb("gu", [P, MT, T], F32, dense)
        cbc = sb("cbc", [P, E, T], F32, dense)
        comb = sb("comb", [E, T], F32, dense)
        dense.close()
        sparse = ExitStack()
        htokhi = sb("htokhi", [P, 3, D], F32R, sparse)
        htoklo = sb("htoklo", [P, 3, D], F32R, sparse)
        hghi = sb("hghi", [P, KT, P], F32R, sparse)
        hglo = sb("hglo", [P, KT, P], F32R, sparse)
        gthi = sb("gthi", [P, FT, P], F32R, sparse)
        gtlo = sb("gtlo", [P, FT, P], F32R, sparse)
        pick = sb("pick", [P, 3, P], F32R, sparse)
        give = sb("give", [P, 3, P], F32, sparse)
        giveT = sb("giveT", [P, T], F32, sparse)
        ys = sb("ys", [P, D], F32, sparse)
        sgs = sb("sgs", [P, CW], F32, sparse)
        gus = sb("gus", [P, CW], F32, sparse)
        count = sb("count", [P, P], F32, sparse)
        sparse.close()
        ffn.close()
        raw = [raw01[:, 0], raw01[:, 1], raw2[:, :, :]]
        whi = [whi01[:, 0], whi01[:, 1], whi2[:, :, :]]
        wlo = [wlo01[:, 0], wlo01[:, 1], wlo2[:, :, :]]
        ctok = xdt
        mtok = sgb[:, :, :].rearrange("p k t -> p (k t)")[:, 0:R3 * CW].rearrange("p (s c) -> p s c", s=R3)
        bmod = sgb[:, :, :].rearrange("p k t -> p (k t)")[:, R3 * CW:R3 * CW + L * 6 * KT]
        modf = mod[:, :, :, :].rearrange("p l r c -> p (l r) c")
        ptok = mix[:, :, :].rearrange("p h q -> p (h q)")
        stok = xc
        xtok = xraw
        tail = ce[:, :, :].rearrange("p h q -> p (h q)")
        sring = ce[:, :, :].rearrange("p (s k) n -> p s k n", s=2)
        sprod = xw[:, :].rearrange("p (k n) -> p k n", k=KT)
        hst = mix[:, 0:KT, :]
        vtok = mix[:, :, :].rearrange("p (c g) q -> p c (g q)", c=NQ)
        wsp = hT[:, :].rearrange("p (g q) -> p g q", g=KT)
        vrow = hf[0:B, :, :].rearrange("b k t -> b (k t)")[:, 0:D]
        wT = xdt[:, :].rearrange("p (g q) -> p g q", g=KT)

        acc = ctx.enter_context(nc.psum_tensor("acc", [P, 4, 512], F32))
        ms = ctx.enter_context(nc.psum_tensor("ms", [P, 4, 512], F32))
        msf = ms[:, :, :].rearrange("p b n -> p (b n)")

        sem = {s: ctx.enter_context(nc.semaphore(s)) for s in SEMAPHORES}
        raw_full = [sem["raw_full0"], sem["raw_full1"], sem["raw_full2"]]
        acc_free = [sem["acc_free0"], sem["acc_free1"]]
        s_in = [sem["s_in0"], sem["s_in1"]]
        s_out = [sem["s_out0"], sem["s_out1"]]
        block = ctx.enter_context(nc.Block())

        def row(name, l, k=None):
            r0, rows = ROWS[name]
            return PT[:, l, r0:r0 + rows] if k is None else PT[:, l, r0 + k:r0 + k + 1]

        def bc(ap, axis, shape):
            return ap.unsqueeze(axis).to_broadcast(shape)

        def later(i, n):
            return not isinstance(i, int) or i >= n

        def loop(eng, count, body, peel=0):
            for i in range(peel):
                body(i)
            if count > peel:
                with eng.Fori(0, count - peel) as i:
                    body(i + peel)

        def load(sp, n, slot, dst_cols, src, nk=KT):
            sp.wait_ge(sem["lo_ready"], n - 1)
            sp.dma_start(raw[slot][:, 0:nk, 0:dst_cols], src).then_inc(raw_full[slot], 16)

        def landed(base):
            return 16 * (M3 + (base - N0["xbc", 0]) // 2 + 1)

        def load_phase(sp, key, w, col0, count):
            n0 = N0[key]
            wv = w.rearrange("(k p) m -> p k m", p=P)

            def body(i):
                for c in range(2):
                    a = sp.snap(col0 + CW * c + 2 * CW * i)
                    load(sp, n0 + c + 2 * i, (n0 + c) % 2, CW, wv[:, :, bass.ds(a, CW)])
            loop(sp, count // 2, body)

        def split_hi(act, base, i, step=2, e=0):
            slot = base % 2
            act.wait_ge(raw_full[slot], landed(base) + 8 * step * i + 8 * EN * e)
            act.wait_ge(sem["w_used"], base - 1 + step * i + EN * e)
            act.activation(whi[slot], raw[slot], ACT.Copy).then_inc(sem["hi_ready"], 1)

        def split_lo(dve, base, i, step=2, e=0):
            slot = base % 2
            dve.wait_ge(sem["hi_ready"], base + 1 + step * i + EN * e)
            dve.tensor_tensor(wlo[slot], raw[slot], whi[slot].bitcast(F32), ALU.subtract) \
                .then_inc(sem["lo_ready"], 1)

        NX = N0["gu", L - 1]
        FILLS = [M3 + sum(m % 2 == s for m in range(N0["xbc", 0], NX)) for s in range(2)] + [M3]

        def split_hi3(act, j, e):
            act.wait_ge(raw_full[j % R3], 16 * (FILLS[j % R3] + j // R3 + 1) + 16 * (SN // R3) * e)
            act.wait_ge(sem["w_used"], NX + j - R3 + 1 + SN * e)
            act.activation(whi[j % R3], raw[j % R3], ACT.Copy).then_inc(sem["hi_ready"], 1)

        def split_lo3(dve, j, e):
            dve.wait_ge(sem["hi_ready"], NX + j + 1 + SN * e)
            dve.tensor_tensor(wlo[j % R3], raw[j % R3], whi[j % R3].bitcast(F32), ALU.subtract) \
                .then_inc(sem["lo_ready"], 1)

        def crowded(eng):
            eng.wait_ge(sem["flag_ready"], 1)
            return eng.value_load(flag[0:1, 0:1]) > 0

        def pairs(eng, pair):
            for q in range(2):
                pair(0, q)
            with eng.Fori(0, FP // R3) as b:
                for q in range(2, 2 + R3):
                    pair(b, q)

        def products(pe, n, slot, pair, first, last, hi, lo, cols, nk=KT, tiles=MT):
            pe.wait_ge(sem["lo_ready"], n + 1)
            for j in range(tiles):
                out = acc[:, 2 * pair + j, 0:cols]
                for k in range(nk):
                    a = whi[slot][:, k, j * P:(j + 1) * P]
                    b = wlo[slot][:, k, j * P:(j + 1) * P]
                    pe.matmul(out, a, hi(k), start=first and k == 0, stop=False)
                    pe.matmul(out, a, lo(k), start=False, stop=False)
                    ins = pe.matmul(out, b, hi(k), start=False, stop=last and k == nk - 1)
            ins.then_inc(sem["w_used"], 1)

        def pe_phase(pe, key, count, hi, lo, cols, peel=0, after=None):
            n0, q0 = N0[key], Q0[key]

            def body(i):
                for c in range(2):
                    if not (isinstance(i, int) and q0 + c + 2 * i < 2):
                        pe.wait_ge(acc_free[(q0 + c) % 2], (q0 + c) // 2 + i)
                    products(pe, n0 + c + 2 * i, (n0 + c) % 2, (q0 + c) % 2, True, True, hi, lo, cols)
                    if after:
                        after(c + 2 * i)
            loop(pe, count // 2, body, count // 2 if after else peel)

        def act_phase(act, key, count, epilogue=None, peel=0, end=False, after=None):
            n0, q0 = N0[key], Q0[key]

            def body(i):
                for c in range(2):
                    if not (end and c + 1 + 2 * i == count):
                        split_hi(act, n0 + c + 1, i)
                    if epilogue:
                        act.wait_ge(sem["w_used"], n0 + c + 1 + 2 * i)
                        pair = (q0 + c) % 2
                        epilogue(i, c, acc[:, 2 * pair:2 * pair + 2, 0:T]).then_inc(acc_free[pair], 1)
                    if after:
                        after(c + 2 * i)
            loop(act, count // 2, body, count // 2 if end or after else peel)

        def dve_phase(dve, key, count, epilogue=None, peel=0, cols=T, end=False, after=None):
            n0, q0 = N0[key], Q0[key]

            def body(i):
                for c in range(2):
                    if not (end and c + 1 + 2 * i == count):
                        split_lo(dve, n0 + c + 1, i)
                    if epilogue:
                        dve.wait_ge(sem["w_used"], n0 + c + 1 + 2 * i)
                        pair = (q0 + c) % 2
                        epilogue(i, c, acc[:, 2 * pair:2 * pair + 2, 0:cols]).then_inc(acc_free[pair], 1)
                    if after:
                        after(c + 2 * i)
            loop(dve, count // 2, body, count // 2 if end or after else peel)

        def xs(part):
            return lambda k: part[:, k, :]

        @block.sync
        def _(sp):
            for l in range(L):
                wv = A["w_mod"][l].rearrange("(k p) m -> p k m", p=P)
                per = 6 * KT // MT // R3

                def body(i):
                    for c in range(R3):
                        a = sp.snap(R3 * CW * i + CW * c)
                        if not (isinstance(i, int) and l == 0):
                            sp.wait_ge(sem["lo_ready"], l * per * R3 + c - 2 + R3 * i)
                        sp.dma_start(raw[c], wv[:, :, bass.ds(a, CW)]).then_inc(raw_full[c], 16)
                loop(sp, per, body, 1 if l == 0 else 0)
            sp.wait_ge(sem["lo_ready"], N0["xbc", 0])
            for l in range(L):
                load_phase(sp, ("xbc", l), A["w_in"][l], IN_COL["xbc"], IN_CHUNKS["xbc"])
                n = N0["dt", l]
                load(sp, n, n % 2, H, A["w_in"][l].rearrange("(k p) m -> p k m", p=P)[:, :, D + CD:D + CD + H])
                for name in ("v", "u", "z", "ga", "gb"):
                    load_phase(sp, (name, l), A["w_in"][l], IN_COL[name], IN_CHUNKS[name])
                for name, w in (("cmlp_out", A["w_cmlp_out"]), ("ssd_out", A["w_ssd_out"]), ("w_o", A["w_o"])):
                    load_phase(sp, (name, l), w[l], 0, KT // MT)

                def expert(e, wg, wu, wd):
                    n0 = N0["gu", l]
                    gv, uv = (w.rearrange("(k p) m -> p k m", p=P) for w in (wg, wu))
                    dv = wd.rearrange("(k p) m -> p k m", p=P)

                    def gates(i):
                        a = sp.snap(CW * i)
                        for c, w in enumerate((gv, uv)):
                            load(sp, n0 + c + 2 * i + EN * e, (n0 + c) % 2, CW, w[:, :, bass.ds(a, CW)])
                    with sp.Fori(0, FT // MT) as i:
                        gates(i)
                    n1 = N0["wd", l]

                    def downs(i):
                        for g in range(2):
                            a = sp.snap(2 * CW * i + g * CW)
                            for s, (k0, nk) in enumerate(KG):
                                c = g * len(KG) + s
                                load(sp, n1 + c + 2 * len(KG) * i + EN * e, (n1 + c) % 2, CW,
                                     dv[:, k0:k0 + nk, bass.ds(a, CW)], nk)
                    with sp.Fori(0, KT // MT // 2) as i:
                        downs(i)

                if l % 2 == 0:
                    expert(0, A["ffn_wg"][l // 2], A["ffn_wu"][l // 2], A["ffn_wd"][l // 2])
                    continue
                with sp.If(crowded(sp)):
                    with sp.Fori(0, E) as e:
                        expert(e, A["exp_wg"][l // 2, e], A["exp_wu"][l // 2, e], A["exp_wd"][l // 2, e])
                with sp.Else():
                    with sp.Fori(0, E) as e:
                        gv, uv = (w[l // 2, e].rearrange("(k p) m -> p k m", p=P) for w in (A["exp_wg"], A["exp_wu"]))
                        dv = A["exp_wd"][l // 2, e].rearrange("(d k p) m -> d p k m", k=DK, p=P)

                        def fetch(j, b, dst, src):
                            sp.wait_ge(sem["lo_ready"], NX + j - R3 + 1 + SN * e + 2 * R3 * b)
                            sp.dma_start(dst, src).then_inc(raw_full[j % R3], 16)

                        def pair(b, q):
                            a = sp.snap(CW * R3 * b + CW * q)
                            for c, w in enumerate((gv, uv)):
                                fetch(2 * q + c, b, raw[(2 * q + c) % R3], w[:, :, bass.ds(a, CW)])
                        pairs(sp, pair)
                        for d in range(FD):
                            j = 2 * FP + d
                            fetch(j, 0, raw[j % R3].rearrange("p k c -> p (k c)").rearrange("p (k m) -> p k m", k=DK),
                                  dv[d])

        @block.gpsimd
        def _(pool):
            pool.wait_ge(sem["ctok_zero"], 1)
            pool.dma_start(ctok[0:1, :], A["c_prompt"]).then_inc(sem["c_in"], 16)
            pool.dma_start(ctok[1:1 + B, :], A["c_sample"]).then_inc(sem["c_in"], 16)
            pool.memset(ident[:, :], 0.0).then_inc(sem["ident_zero"], 1)
            pool.memset(tri[:, :], 1.0).then_inc(sem["ident_zero"], 1)
            pool.memset(spread[:, :], 1.0).then_inc(sem["ident_zero"], 1)
            pool.memset(earlier[:, :, :], 1.0).then_inc(sem["ident_zero"], 1)
            pool.memset(fold[:, :], 0.0).then_inc(sem["ident_zero"], 1)
            pool.wait_ge(sem["ident_zero"], 5)
            pool.affine_select(out=ident[:, :], in_=ident[:, :], compare_op=ALU.not_equal, fill=1.0, base=0,
                               pattern=[[-1, P]], channel_multiplier=1).then_inc(sem["consts"], 1)
            pool.affine_select(out=tri[:, :], in_=tri[:, :], compare_op=ALU.is_ge, fill=0.0, base=0,
                               pattern=[[1, P]], channel_multiplier=-1).then_inc(sem["consts"], 1)
            pool.affine_select(out=spread[:, :], in_=spread[:, :], compare_op=ALU.is_ge, fill=0.0, base=0,
                               pattern=[[1, D]], channel_multiplier=-HD).then_inc(sem["consts"], 1)
            pool.wait_ge(sem["consts"], 3)
            pool.affine_select(out=spread[:, :], in_=spread[:, :], compare_op=ALU.is_ge, fill=0.0, base=HD - 1,
                               pattern=[[-1, D]], channel_multiplier=HD).then_inc(sem["consts"], 1)
            pool.affine_select(out=earlier[:, :, :], in_=earlier[:, :, :], compare_op=ALU.is_gt, fill=0.0, base=0,
                               pattern=[[1, E], [-1, E]], channel_multiplier=0).then_inc(sem["consts"], 1)
            pool.wait_ge(sem["consts"], 5)
            pool.tensor_copy(fold[0:NC, :], ident[0:NC, 0:NC]).then_inc(sem["consts"], 1)
            pool.tensor_copy(fold[CL:CL + NC, :], ident[CL:CL + NC, CL:CL + NC]).then_inc(sem["consts"], 1)
            for l in range(L):
                for name, (r0, rows) in ROWS.items():
                    src = (A["conv_w"][l].rearrange("k (c p) -> (k c) p", p=P) if name == "conv_w"
                           else A["vectors"][name][l].rearrange("(c p) -> c p", p=P))
                    c0 = (l * RT + r0 // P) * P
                    pool.dma_start(ptok[r0 % P:r0 % P + rows, c0:c0 + P], src).then_inc(sem["params_in"], 16)
            for l in range(L):
                pool.dma_start(stok[0:B * (CK - 1), l * CD:(l + 1) * CD],
                               A["state_conv"][l].rearrange("b k c -> (b k) c")).then_inc(sem["states_in"], 16)
            for c in range(NQ):
                pool.dma_start(xtok[:, c * D:(c + 1) * D], A["x_prompt"][0, c * Q:(c + 1) * Q, :]).then_inc(sem["x_in"], 16)
            pool.dma_start(xtok[0:B, NQ * D:(NQ + 1) * D], A["x_sample"][:, 0, :]).then_inc(sem["x_in"], 16)
            for k, v in enumerate((A["dt_bias"], A["a_log"], A["d_skip"])):
                pool.dma_start(headp[:, k, :], v.rearrange("l h -> h l"), allow_slow_non_contiguous=True).then_inc(sem["sp_in"], 16)
            pool.dma_start(spb[:, :, :], A["b_spatial"].rearrange("l g q -> g l q")).then_inc(sem["sp_in"], 16)
            for l in range(L):
                pool.dma_start(w00[:, l:l + 1], A["w_spatial"][l, :, 0, 0:1], allow_slow_non_contiguous=True).then_inc(sem["sp_in"], 16)
            pool.dma_start(rw[:, :, :], A["router_w"][0].rearrange("(k p) e -> p k e", p=P)).then_inc(sem["route_in"], 16)
            pool.dma_start(rb[:, :], A["router_b"]).then_inc(sem["route_in"], 16)
            pool.dma_start(O["conv_s"][:, :, 0:CK - 2, :], A["state_conv"][:, :, 1:CK - 1, :]).then_inc(sem["conv_keep"], 16)

            for l in range(L):
                pool.wait_ge(sem["tail_ready"], l + 1)
                pool.dma_start(O["conv_p"][l, 0], tail[0:CK - 1, 0:CD]).then_inc(sem["tail_out"], 16)
                pool.dma_start(O["conv_s"][l, :, CK - 2, :], tail[CK - 1:CK - 1 + B, 0:CD]).then_inc(sem["tail_out"], 16)
                pool.dma_start(wsp, A["w_spatial"][l].rearrange("g t s -> t g s")).then_inc(sem["w_sp_in"], 16)
                state = A["state_ssm"][l].rearrange("b (k j) p n -> b (j p) k n", j=2)
                new = O["ssm_s"][l].rearrange("b (k j) p n -> b (j p) k n", j=2)
                pool.wait_ge(sem["tail_out"], 32 * (l + 1))
                for b in range(B):
                    s = b % 2
                    if b >= 2:
                        pool.wait_ge(s_out[s], 16 * (l * B // 2 + b // 2))
                        pool.wait_ge(sem["samp_used"], l * B + b - 1)
                    pool.dma_start(sring[:, s], state[b]).then_inc(s_in[s], 16)
                    if b >= 1:
                        pool.wait_ge(sem["s_new"], l * B + b)
                        pool.dma_start(new[b - 1], sring[:, 1 - s]).then_inc(s_out[1 - s], 16)
                pool.wait_ge(sem["s_new"], (l + 1) * B)
                pool.dma_start(new[B - 1], sring[:, (B - 1) % 2]).then_inc(s_out[(B - 1) % 2], 16)
                pool.wait_ge(sem["vs_copied"], l + 1)
                pool.dma_start(O["v_s"][l, :, 0, :], vrow).then_inc(sem["vs_out"], 16)
                pool.wait_ge(sem["st_copied"], l + 1)
                pool.dma_start(O["ssm_p"][l, 0].rearrange("(k j) p n -> (j p) k n", j=2), hst).then_inc(sem["st_out"], 16)
            pool.wait_ge(sem["y_copied"], 3)
            for c in range(NQ):
                pool.dma_start(O["y_p"][0, c * Q:(c + 1) * Q, :], xtok[:, c * D:(c + 1) * D]).then_inc(sem["y_out"], 16)
            pool.dma_start(O["y_s"][:, 0, :], xtok[0:B, NQ * D:(NQ + 1) * D]).then_inc(sem["y_out"], 16)
            pool.wait_ge(sem["y_out"], 16 * (NQ + 1))
            pool.wait_ge(sem["conv_keep"], 16)
            pool.wait_ge(sem["tail_out"], 32 * L)
            pool.wait_ge(sem["st_out"], 16 * L)
            for s in range(2):
                pool.wait_ge(s_out[s], 8 * L * B)
            pool.wait_ge(sem["vs_out"], 16 * L)

        @block.tensor
        def _(pe):
            def sum_tiles(v, src, out, k0=0, k1=KT):
                for k in range(k0, k1):
                    ins = pe.matmul(out, ones[:, :], src[:, k, :], start=k == k0, stop=k == k1 - 1)
                return ins

            def norm(v):
                pe.wait_ge(sem["sq_ready"], v)
                sum_tiles(v, hf, ms[:, 0, 0:T]).then_inc(sem["ssq_ready"], 1)

            pe.wait_ge(sem["consts"], 7)
            pe.wait_ge(sem["c_silu"], 1)
            for k in range(KT):
                ins = pe.transpose(ms[:, 0, NC * k:NC * (k + 1)], ctok[0:NC, k * P:(k + 1) * P], ident[0:NC, 0:NC])
            ins.then_inc(sem["c_turned"], 1)
            pe.wait_ge(sem["params_in"], 16 * L * len(ROWS))
            for l in range(L):
                for r in range(RT):
                    rows = min(P, NROW - r * P)
                    c0 = (l * RT + r) * P
                    ins = pe.transpose(ms[:, 1, l * NROW + r * P:l * NROW + r * P + rows], ptok[0:rows, c0:c0 + P],
                                       ident[0:rows, 0:rows])
            ins.then_inc(sem["params_turned"], 1)
            SR = B * (CK - 1)
            pe.wait_ge(sem["states_in"], 16 * L)
            for l in range(L):
                for k in range(CT):
                    ins = pe.transpose(ms[:, 2 + l, k * SR:(k + 1) * SR], stok[0:SR, l * CD + k * P:l * CD + (k + 1) * P],
                                       ident[0:SR, 0:SR])
            ins.then_inc(sem["state_turned"], 1)
            pe.wait_ge(sem["x_in"], 16 * (NQ + 1))
            pe.wait_ge(sem["state_ready"], 1)
            pe.wait_ge(sem["params_ready"], 1)
            pe.wait_ge(sem["c_lo"], 1)
            for c in range(NQ + 1):
                rows = Q if c < NQ else B
                if c >= 2:
                    pe.wait_ge(sem["x_ready"], c - 1)
                for k in range(KT):
                    bank = 2 * (c % 2) + k // 4
                    ins = pe.transpose(ms[:, bank, (k % 4) * P:(k % 4) * P + rows],
                                       xtok[0:rows, c * D + k * P:c * D + (k + 1) * P], ident[0:rows, 0:rows])
                ins.then_inc(sem["x_turned"], 1)

            def fold_chunk(m, c):
                pe.wait_ge(sem["mt_ready"], m + 1)
                if not isinstance(m, int) or m >= R3:
                    pe.wait_ge(sem["mod_added"], m - 2)
                for j in range(MT):
                    ins = pe.matmul(ms[:, c, j * NC:(j + 1) * NC], mtok[0:CL + NC, c, j * P:(j + 1) * P], fold[:, :],
                                    start=True, stop=True)
                ins.then_inc(sem["folded"], 1)

            def mod_body(i):
                for c in range(R3):
                    pe.wait_ge(sem["lo_ready"], c + 1 + R3 * i)
                    if later(i, 1):
                        pe.wait_ge(sem["mt_ready"], c - 2 + R3 * i)
                    for k in range(KT):
                        pe.matmul(acc[:, c, 0:CW], cst[:, k, :], whi[c][:, k, :], start=k == 0, stop=False)
                        ins = pe.matmul(acc[:, c, 0:CW], cst[:, k, :], wlo[c][:, k, :], start=False, stop=k == KT - 1)
                    ins.then_inc(sem["w_used"], 1)
                    if later(i, 1) or c >= 2:
                        fold_chunk(R3 * i + c - 2, (c - 2) % R3)
            pe.wait_ge(sem["x_ready"], NQ + 1)
            loop(pe, N0["xbc", 0] // R3, mod_body, 2)
            for m in (N0["xbc", 0] - 2, N0["xbc", 0] - 1):
                fold_chunk(m, m % R3)
            pe.wait_ge(sem["mod_added"], N0["xbc", 0])

            for l in range(L):
                norm(4 * l + 1)
                pe.wait_ge(sem["xs_lo"], 5 * l + 1)
                pe_phase(pe, ("xbc", l), IN_CHUNKS["xbc"], xs(xhi), xs(xlo), T, peel=1 if l == 0 else 0)
                n, q = N0["dt", l], Q0["dt", l]
                pe.wait_ge(acc_free[q % 2], q // 2)
                products(pe, n, n % 2, q % 2, True, True, xs(xhi), xs(xlo), T, tiles=1)
                pe_phase(pe, ("v", l), IN_CHUNKS["v"], xs(xhi), xs(xlo), T)
                for k in range(CT):
                    ins = pe.transpose(ms[0:CK - 1 + B, k // 4, (k % 4) * P:(k % 4 + 1) * P],
                                       xrawv[:, k, S:S + CK - 1 + B], ident[:, :])
                ins.then_inc(sem["tail_turned"], 1)
                pe_phase(pe, ("u", l), IN_CHUNKS["u"], xs(xhi), xs(xlo), T)
                pe.wait_ge(sem["tail_ready"], l + 1)
                sum_tiles(0, vb, ms[:, 0, 0:T]).then_inc(sem["v_sum"], 1)
                pe.wait_ge(sem["samp_decay"], l + 1)
                for k in range(KT):
                    ins = pe.matmul(ms[:, 3, k * (2 * B + 1):(k + 1) * (2 * B + 1)], spread[:, k * P:(k + 1) * P],
                                    spin[:, :], start=True, stop=True)
                ins.then_inc(sem["spread_ready"], 1)
                pe_phase(pe, ("z", l), IN_CHUNKS["z"], xs(xhi), xs(xlo), T)

                def sample_rows(b):
                    if b >= 2:
                        pe.wait_ge(sem["samp_used"], l * B + b - 1)
                    pe.matmul(ms[:, 2 + b % 2, :], ident[0:B, b:b + 1].to_broadcast([B, P]), bct[:, :], start=True,
                              stop=True).then_inc(sem["bc_spread"], 1)

                def after_ga(c):
                    if c == 0:
                        pe.wait_ge(sem["xc_ready"], l + 1)
                        for k in range(2 * G):
                            ins = pe.transpose(ms[0:B, 2, k * P:(k + 1) * P], xcv[:, KT + k, S:T], ident[:, :])
                        ins.then_inc(sem["bc_turned"], 1)
                        pe.wait_ge(sem["v_sq"], l + 1)
                        sum_tiles(0, hf, ms[:, 1, 0:T]).then_inc(sem["v_ssq"], 1)
                        pe.wait_ge(sem["bc_ready"], l + 1)
                        pe.wait_ge(sem["spread_copied"], l + 1)
                    sample_rows(c)
                pe_phase(pe, ("ga", l), IN_CHUNKS["ga"], xs(xhi), xs(xlo), T, after=after_ga)
                pe_phase(pe, ("gb", l), IN_CHUNKS["gb"], xs(xhi), xs(xlo), T, after=lambda c: sample_rows(B // 2 + c))

                pe.wait_ge(sem["v_normed"], l + 1)
                for k in range(KT):
                    ins = pe.transpose(ms[0:B, k // 4, (k % 4) * P:(k % 4 + 1) * P], vb[:, k, S:T], ident[:, :])
                ins.then_inc(sem["vs_turned"], 1)
                pe.wait_ge(sem["vs_copied"], l + 1)
                for c in range(NQ):
                    if c:
                        pe.wait_ge(sem["w_sp_in"], 16 * (l + 1))
                        pe.wait_ge(sem["samp_used"], (l + 1) * B)
                        for k in range(KT):
                            ins = pe.transpose(ms[:, 2 + k // 4, (k % 4) * P:(k % 4 + 1) * P], wsp[:, k, :], ident[:, :])
                        ins.then_inc(sem["w_turned"], 1)
                        pe.wait_ge(sem["v_tok_ready"], l * NQ + c)
                    for k in range(KT):
                        ins = pe.transpose(ms[:, k // 4, (k % 4) * P:(k % 4 + 1) * P], vb[:, k, c * Q:(c + 1) * Q],
                                           ident[:, :])
                    ins.then_inc(sem["v_tok"], 1)
                pe.wait_ge(sem["diag_ready"], l + 1)
                pe.wait_ge(sem["v_tok_ready"], (l + 1) * NQ)
                pe.wait_ge(sem["w_ready"], l + 1)
                pe.matmul(ms[:, 0, 0:2 * KT], ones[0:KT, :], diag[:, :, :].rearrange("g a b -> g (a b)"), start=True,
                          stop=True).then_inc(sem["sp_bcast"], 1)
                pe.wait_ge(sem["sp_bcast_ready"], l + 1)
                for c in range(NQ):
                    for k in range(KT):
                        out = ms[:, 2 * c + k // 4, (k % 4) * Q:(k % 4 + 1) * Q]
                        pe.matmul(out, vtok[:, c, k * P:(k + 1) * P], wT[:, k, :], start=True, stop=False)
                        ins = pe.matmul(out, ident[0:KT, k:k + 1].to_broadcast([KT, P]), spb[:, l, :], start=False,
                                        stop=True)
                    ins.then_inc(sem["sp_out"], 1)
                pe.wait_ge(sem["xs_lo"], 5 * l + 2)
                pe_phase(pe, ("cmlp_out", l), KT // MT, xs(xhi), xs(xlo), T)

                pe.wait_ge(sem["sp_taken"], l + 1)
                for c in range(NQ):
                    v = l * NQ + c
                    toks = slice(c * Q, (c + 1) * Q)
                    if c:
                        pe.wait_ge(sem["y_taken"], v)
                        pe.wait_ge(sem["st_ready"], v)
                    for k in range(KT):
                        ins = pe.transpose(ms[:, k // 4, (k % 4) * P:(k % 4 + 1) * P], xcv[:, k, toks], ident[:, :])
                    ins.then_inc(sem["x_tok"], 1)
                    for g in range(G):
                        pe.transpose(ms[:, 2, g * P:(g + 1) * P], xcv[:, KT + g, toks], ident[:, :])
                    pe.transpose(ms[:, 2, 2 * P:2 * P + H], dth[:, 0, toks], ident[0:H, 0:H])
                    pe.transpose(ms[:, 2, 2 * P + H:2 * P + 2 * H], dth[:, 1, toks], ident[0:H, 0:H]) \
                        .then_inc(sem["b_tok"], 1)
                    pe.wait_ge(sem["spread_copied"], l + 1)
                    for g in range(G):
                        ins = pe.matmul(ms[:, 3, g * Q:(g + 1) * Q], xcv[:, KT + g, toks], xcv[:, KT + G + g, toks],
                                        start=True, stop=True)
                    ins.then_inc(sem["cb_ready"], 1)
                    pe.wait_ge(sem["xdt_ready"], v + 1)
                    pe.wait_ge(sem["bt_ready"], v + 1)
                    pe.wait_ge(sem["tok_ready"], v + 1)
                    pe.wait_ge(sem["cbm_ready"], v + 1)
                    for h in range(H):
                        ins = pe.matmul(ms[:, h // 4, (h % 4) * Q:(h % 4 + 1) * Q], ident[0:H, h:h + 1].to_broadcast([H, P]),
                                        dth[:, 0, toks], start=True, stop=True)
                    ins.then_inc(sem["cumb_ready"], 1)
                    pe.wait_ge(sem["mix_ready"], v + 1)
                    pe.wait_ge(sem["wend_ready"], v + 1)
                    if c:
                        pe.wait_ge(sem["ce_ready"], l + 1)
                    for h in range(H):
                        out = ms[(h % 2) * HD:(h % 2 + 1) * HD, h // 8, (h // 2 % 4) * Q:(h // 2 % 4 + 1) * Q]
                        ins = pe.matmul(out, xdt[:, h * HD:(h + 1) * HD], mix[:, h, :], start=True, stop=c == 0)
                        if c:
                            ins = pe.matmul(out, hT[:, h * HD:(h + 1) * HD], ce[:, h, :], start=False, stop=True)
                    ins.then_inc(sem["y_part"], 1)
                    pe.wait_ge(sem["xw_ready"], v + 1)
                    for g in range(G):
                        ins = pe.matmul(ms[:, 2 + g, :], bt[:, g, :], xw[:, g * 512:(g + 1) * 512], start=True, stop=True)
                    ins.then_inc(sem["st_part"], 1)
                pe.wait_ge(sem["st_ready"], (l + 1) * NQ)
                pe.wait_ge(sem["y_taken"], (l + 1) * NQ)
                for k in range(KT):
                    ins = pe.transpose(ms[:, k // 4, (k % 4) * P:(k % 4 + 1) * P], hT[:, k * P:(k + 1) * P], ident[:, :])
                ins.then_inc(sem["st_turned"], 1)
                pe.wait_ge(sem["gate_sq"], l + 1)
                for g in range(G):
                    ins = sum_tiles(0, zs, ms[:, 2 + g, 0:T], g * KT // G, (g + 1) * KT // G)
                ins.then_inc(sem["gate_ssq"], 1)
                pe.wait_ge(sem["xs_lo"], 5 * l + 3)
                pe_phase(pe, ("ssd_out", l), KT // MT, xs(xhi), xs(xlo), T)

                pe.wait_ge(sem["xs_lo"], 5 * l + 4)
                pe_phase(pe, ("w_o", l), KT // MT, xs(xhi), xs(xlo), T)
                norm(4 * l + 2)
                norm(4 * l + 3)

                if l % 2:
                    pe.wait_ge(sem["h_ready"], 2 * l + 2)
                    for c in range(3):
                        rows = Q if c < NQ else B
                        for k in range(KT):
                            pe.matmul(ms[0:rows, 1, c * E:(c + 1) * E], hf[:, k, c * Q:c * Q + rows], rw[:, k, :],
                                      start=k == 0, stop=False)
                        ins = pe.matmul(ms[0:rows, 1, c * E:(c + 1) * E], ones[0:1, 0:rows], rb[:, :], start=False,
                                        stop=True)
                    ins.then_inc(sem["logits_ready"], 1)
                    pe.wait_ge(sem["sel_ready"], 1)
                    for c in range(4):
                        for d in range(min(c, 2) + 1):
                            ins = pe.matmul(ms[:, 3, c * E:(c + 1) * E], tri[:, :] if d == c else ones[:, :],
                                            sel[:, d, :], start=d == 0, stop=d == min(c, 2))
                    ins.then_inc(sem["counted"], 1)
                pe.wait_ge(sem["xs_lo"], 5 * l + 5)

                def all_tokens(pe, expert):
                    pe.wait_ge(sem["route_done"], 1)
                    for c in range(3):
                        rows = Q if c < NQ else B
                        ins = pe.transpose(ms[0:E, 2, c * Q:c * Q + rows], rank[0:rows, c, :], ident[0:rows, 0:rows])
                    ins.then_inc(sem["combine_turned"], 1)
                    pe.wait_ge(sem["combine_ready"], 1)
                    for e in range(E):
                        if e >= 4:
                            pe.wait_ge(sem["combine_spread_ready"], e - 3)
                        pe.matmul(ms[:, e % 4, 0:T], ident[0:E, e:e + 1].to_broadcast([E, P]), comb[:, :], start=True,
                                  stop=True).then_inc(sem["combine_spread"], 1)
                    with pe.Fori(0, E) as e:
                        expert(e)

                def expert(e):
                    n0, q0 = N0["gu", l], Q0["gu", l]

                    def gates(i):
                        for c in range(2):
                            pe.wait_ge(acc_free[(q0 + c) % 2], (q0 + c) // 2 + i + EQ // 2 * e)
                            products(pe, n0 + c + 2 * i + EN * e, (n0 + c) % 2, (q0 + c) % 2, True, True, xs(xhi),
                                     xs(xlo), T)
                    with pe.Fori(0, FT // MT) as i:
                        gates(i)
                    n1, q1 = N0["wd", l], Q0["wd", l]

                    def downs(i):
                        for g in range(2):
                            pair = (q1 + g) % 2
                            pe.wait_ge(acc_free[pair], (q1 + g) // 2 + i + EQ // 2 * e)
                            for s, (k0, nk) in enumerate(KG):
                                pe.wait_ge(acc_free[(q0 + 1) % 2], (q0 + 1) // 2 + (k0 + nk) // MT + EQ // 2 * e)
                                c = g * len(KG) + s
                                products(pe, n1 + c + 2 * len(KG) * i + EN * e, (n1 + c) % 2, pair, s == 0,
                                         s == len(KG) - 1, lambda k, k0=k0: ghi[:, k0 + k, :],
                                         lambda k, k0=k0: glo[:, k0 + k, :], T, nk)
                    with pe.Fori(0, KT // MT // 2) as i:
                        downs(i)

                if l % 2 == 0:
                    expert(0)
                    norm(4 * l + 4)
                    continue
                with pe.If(crowded(pe)):
                    all_tokens(pe, expert)
                with pe.Else():
                    for c in range(3):
                        rows = Q if c < NQ else B
                        if c == 2:
                            pe.wait_ge(sem["htok_lo"], 1)
                        for k in range(KT):
                            ins = pe.transpose(ms[0:rows, 2 * (c % 2) + k // 4, (k % 4) * P:(k % 4 + 1) * P],
                                               hf[:, k, c * Q:c * Q + rows], ident[:, :])
                        ins.then_inc(sem["h_turned"], 1)

                    def gather(e):
                        pe.wait_ge(sem["g_built"], 1 + e)
                        pe.wait_ge(sem["gt_lo"], R3 + FP * e)
                        for part, src in enumerate((htokhi, htoklo)):
                            for k in range(KT):
                                for c in range(3):
                                    rows = Q if c < NQ else B
                                    ins = pe.matmul(ms[:, 2 * part + k // 4, (k % 4) * P:(k % 4 + 1) * P],
                                                    src[0:rows, c, k * P:(k + 1) * P], pick[0:rows, c, :],
                                                    start=c == 0, stop=c == 2)
                        ins.then_inc(sem["gathered"], 1)

                    pe.wait_ge(sem["htok_lo"], 3)
                    gather(0)

                    def turn(b, q, e):
                        pe.wait_ge(sem["gu_done"], R3 + 1 + q + R3 * b + FP * e)
                        pe.wait_ge(sem["gt_lo"], 1 + q + R3 * b + FP * e)
                        for k in range(MT):
                            ins = pe.transpose(ms[:, q % R3, k * P:(k + 1) * P], gus[:, k * P:(k + 1) * P], ident[:, :])
                        ins.then_inc(sem["gu_turned"], 1)

                    def picked(e, last):
                        def pair(b, q):
                            peeled = isinstance(b, int)
                            for c in range(2):
                                if c == 0:
                                    pe.wait_ge(sem["gu_done"], 1 + q + R3 * b + FP * e)
                                    if peeled:
                                        pe.wait_ge(sem["scat_added"], 1 + 4 * e)
                                    elif q == 2:
                                        pe.wait_ge(sem["scat_added"], 2 + 4 * e)
                                s = (2 * q + c) % R3
                                pe.wait_ge(sem["lo_ready"], NX + 2 * q + c + 1 + 2 * R3 * b + SN * e)
                                out = acc[:, q % R3, c * CW:(c + 1) * CW]
                                for k in range(KT):
                                    pe.matmul(out, hghi[:, k, :], whi[s][:, k, :], start=k == 0, stop=False)
                                    pe.matmul(out, hghi[:, k, :], wlo[s][:, k, :], start=False, stop=False)
                                    ins = pe.matmul(out, hglo[:, k, :], whi[s][:, k, :], start=False, stop=k == KT - 1)
                                ins.then_inc(sem["w_used"], 1)
                                if c == 0 and not (peeled and q == 0):
                                    turn(b, q - 1, e)
                            if peeled and q == 1:
                                pe.wait_ge(sem["scat_added"], 2 + 4 * e)
                                for c in range(3):
                                    rows = Q if c < NQ else B
                                    ins = pe.transpose(acc[:, 3, c * Q:c * Q + rows], give[0:rows, c, :],
                                                       ident[0:rows, 0:rows])
                                ins.then_inc(sem["gw_turned"], 1)
                        pe.wait_ge(sem["hg_hi"], 1 + e)
                        pe.wait_ge(sem["hg_lo"], 1 + e)
                        pairs(pe, pair)
                        pe.wait_ge(sem["gw_ready"], 1 + e)
                        for d in range(FD):
                            s = (2 * FP + d) % R3
                            wh, wl = (w[s].rearrange("p k c -> p (k c)") for w in (whi, wlo))
                            pe.wait_ge(sem["lo_ready"], NX + 2 * FP + d + 1 + SN * e)
                            pe.wait_ge(sem["gt_lo"], R3 + 1 + d + FP * e)
                            for k in range(DK):
                                for half in range(2):
                                    cols = slice(k * D + half * 512, k * D + half * 512 + 512)
                                    out = acc[:, 2 + half, :]
                                    hi, lo = gthi[:, DK * d + k, :], gtlo[:, DK * d + k, :]
                                    pe.matmul(out, hi, wh[:, cols], start=d == 0 and k == 0, stop=False)
                                    pe.matmul(out, hi, wl[:, cols], start=False, stop=False)
                                    ins = pe.matmul(out, lo, wh[:, cols], start=False, stop=d == FD - 1 and k == DK - 1)
                            ins.then_inc(sem["w_used"], 1)
                            if d == 0:
                                turn(0, FP - 1, e)
                        if not last:
                            gather(e + 1)
                        pe.wait_ge(sem["ys_ready"], 1 + e)
                        for k in range(KT):
                            if k == 4 or k == 6:
                                pe.wait_ge(sem["scat_added"], 4 * e + 3 + (k - 4) // 2)
                            ins = pe.matmul(acc[:, k % 4, 0:T], ys[:, k * P:(k + 1) * P], giveT[:, :], start=True,
                                            stop=True)
                            if k % 2:
                                ins.then_inc(sem["scattered"], 1)
                    with pe.Fori(0, E - 1) as e:
                        picked(e, False)
                    picked(E - 1, True)
                norm(4 * l + 4)

            pe.wait_ge(sem["x_ready"], 3 + 2 * L)
            for c in range(NQ + 1):
                rows = Q if c < NQ else B
                if c >= 2:
                    pe.wait_ge(sem["y_copied"], c - 1)
                for k in range(KT):
                    ins = pe.transpose(ms[0:rows, 2 * (c % 2) + k // 4, (k % 4) * P:(k % 4 + 1) * P],
                                       x[:, k, c * Q:c * Q + rows], ident[:, :])
                ins.then_inc(sem["y_turned"], 1)

        @block.scalar
        def _(act):
            def norm_sq(v, src):
                act.activation(hf[:, :, :], src[:, :, :], ACT.Square).then_inc(sem["sq_ready"], 1)

            def norm_rs(v):
                act.wait_ge(sem["inv_ready"], v)
                act.activation(rs[:, 0, :], rs[:, 0, :], ACT.Sqrt).then_inc(sem["rs_ready"], 1)

            def hi_of_x(v, src):
                act.activation(xhi[:, :, :], src[:, :, :], ACT.Copy).then_inc(sem["xs_hi"], 1)

            act.wait_ge(sem["c_in"], 32)
            act.activation(ctok[0:NC, :], ctok[0:NC, :], ACT.Silu).then_inc(sem["c_silu"], 1)
            act.wait_ge(sem["c_turned"], 1)
            act.wait_ge(sem["cst_zero"], 1)
            act.activation(cst[:, :, 0:NC], ms[:, 0, 0:KT * NC].rearrange("p (k c) -> p k c", k=KT), ACT.Copy) \
                .then_inc(sem["c_hi"], 1)

            def mod_rows(m, c):
                act.wait_ge(sem["w_used"], m + 1)
                if not isinstance(m, int) or m >= R3:
                    act.wait_ge(sem["folded"], m - 2)
                act.activation(mtok[0:CL + NC, c, :], acc[0:CL + NC, c, 0:CW], ACT.Copy).then_inc(sem["mt_ready"], 1)

            NM = N0["xbc", 0]

            def mod_body(i, last=False):
                for c in range(R3):
                    if not (last and c == R3 - 1):
                        s = (c + 1) % R3
                        act.wait_ge(raw_full[s], 16 * ((c + 1) // R3 + 1) + 16 * i)
                        if later(i, 1) or c >= 2:
                            act.wait_ge(sem["w_used"], c - 1 + R3 * i)
                        act.activation(whi[s], raw[s], ACT.Copy).then_inc(sem["hi_ready"], 1)
                    if later(i, 1) or c >= 1:
                        mod_rows(R3 * i + c - 1, (c - 1) % R3)
            act.wait_ge(raw_full[0], 16)
            act.activation(whi[0], raw[0], ACT.Copy).then_inc(sem["hi_ready"], 1)
            mod_body(0)
            mod_body(1)
            with act.Fori(0, NM // R3 - 3) as i:
                mod_body(i + 2)
            mod_body(NM // R3 - 1, True)
            mod_rows(NM - 1, (NM - 1) % R3)
            act.wait_ge(sem["sp_in"], 16 * (4 + L))
            act.activation(expa[:, :], headp[:, 1, :], ACT.Exp).then_inc(sem["a_exp"], 1)

            for l in range(L):
                if l == 0:
                    act.wait_ge(sem["x_ready"], 3)
                    split_hi(act, N0["xbc", 0], 0)
                norm_sq(4 * l + 1, x)
                norm_rs(4 * l + 1)
                act.wait_ge(sem["h_ready"], 2 * l + 1)
                hi_of_x(5 * l + 1, hf)
                S3 = CK - 1
                act_phase(act, ("xbc", l), IN_CHUNKS["xbc"], lambda i, c, banks: act.activation(
                    xrawv[:, bass.ds(4 * i + 2 * c, 2), S3:S3 + T], banks, ACT.Copy))
                split_hi(act, N0["dt", l] + 1, 0)
                act.wait_ge(sem["dt_abs"], l + 1)
                act.activation(dth[:, 3, :], dth[:, 3, :], ACT.Exp, scale=-1.0).then_inc(sem["dt_exp"], 1)

                def gates(name, dst, fn, after=None):
                    act.preload_act_table(fn)
                    act_phase(act, (name, l), IN_CHUNKS[name], lambda i, c, banks: act.activation(
                        dst[:, bass.ds(4 * i + 2 * c, 2), :], banks, fn), after=after)

                def after_z(c):
                    if c == 0:
                        act.wait_ge(sem["spread_ready"], l + 1)
                        act.activation(spx[:, :, :], ms[:, 3, 0:KT * (2 * B + 1)].rearrange("p (k c) -> p k c", k=KT),
                                       ACT.Copy).then_inc(sem["spread_copied"], 1)
                    if c == 1:
                        act.wait_ge(sem["v_centered"], l + 1)
                        act.activation(hf[:, :, :], vb[:, :, :], ACT.Square).then_inc(sem["v_sq"], 1)

                def after_ga(c):
                    if c == 0:
                        act.wait_ge(sem["bc_turned"], l + 1)
                        act.activation(bct[:, :], ms[0:B, 2, :], ACT.Copy).then_inc(sem["bc_ready"], 1)
                gates("v", vb, ACT.Gelu_apprx_tanh)
                act.wait_ge(sem["tail_turned"], l + 1)
                act.activation(tail[0:CK - 1 + B, 0:CD], msf[0:CK - 1 + B, 0:CD], ACT.Copy).then_inc(sem["tail_ready"], 1)
                gates("u", ub, ACT.Gelu_apprx_tanh)
                act.wait_ge(sem["cum_ready"], l + 1)
                act.activation(spin[:, 0:B], dth[:, 2, S:T], ACT.Exp).then_inc(sem["samp_decay"], 1)
                gates("z", zs, ACT.Silu, after_z)
                act.wait_ge(sem["conv_done"], l + 1)
                act.activation(xc[:, :], xc[:, :], ACT.Silu).then_inc(sem["xc_ready"], 1)
                gates("ga", sga, ACT.Sigmoid, after_ga)
                act.wait_ge(sem["v_inv"], l + 1)
                act.activation(rs[:, 0, :], rs[:, 0, :], ACT.Sqrt).then_inc(sem["v_rs"], 1)
                gates("gb", sgb, ACT.Sigmoid)
                act.wait_ge(sem["vs_turned"], l + 1)
                act.activation(vrow, msf[0:B, 0:D], ACT.Copy).then_inc(sem["vs_copied"], 1)
                for c in range(NQ):
                    act.wait_ge(sem["v_tok"], l * NQ + c + 1)
                    act.activation(vtok[:, c, :], msf[:, 0:D], ACT.Copy).then_inc(sem["v_tok_ready"], 1)
                act.wait_ge(sem["sp_bcast"], l + 1)
                act.activation(spc[:, :, :].rearrange("p a b -> p (a b)"), ms[:, 0, 0:2 * KT], ACT.Copy) \
                    .then_inc(sem["sp_bcast_ready"], 1)
                act.wait_ge(sem["sp_taken"], l + 1)
                act.wait_ge(sem["w_used"], N0["cmlp_out", l])
                hi_of_x(5 * l + 2, ub)
                act_phase(act, ("cmlp_out", l), KT // MT)
                for c in range(NQ):
                    v = l * NQ + c
                    act.wait_ge(sem["tok_ready"], v + 1)
                    if c:
                        act.wait_ge(sem["st_part"], v)
                    act.activation(bt[:, :, :], ms[:, 2, 0:G * P].rearrange("p (g n) -> p g n", g=G), ACT.Copy) \
                        .then_inc(sem["bt_ready"], 1)
                    act.wait_ge(sem["wend_arg"], v + 1)
                    act.activation(wend[:, :], wend[:, :], ACT.Exp).then_inc(sem["wend_ready"], 1)
                    act.activation(elast[:, :], lastc[:, :], ACT.Exp).then_inc(sem["last_ready"], 1)
                    act.wait_ge(sem["seg_ready"], v + 1)
                    if c:
                        for s in range(2):
                            act.wait_ge(s_out[s], 8 * (l + 1) * B)
                        act.activation(ce[:, :, :].rearrange("p h q -> p (h q)"), msf, ACT.Exp).then_inc(sem["ce_exp"], 1)
                    act.activation(mix[:, :, :], mix[:, :, :], ACT.Exp).then_inc(sem["mix_exp"], 1)
                    if c == 0:
                        act.wait_ge(sem["st_part"], v + 1)
                        act.activation(hT[:, :], msf[:, 1024:2048], ACT.Copy).then_inc(sem["st_ready"], 1)
                act.wait_ge(sem["st_turned"], l + 1)
                act.activation(hst.rearrange("p k n -> p (k n)"), msf[:, 0:1024], ACT.Copy).then_inc(sem["st_copied"], 1)
                act.wait_ge(sem["samp_done"], l + 1)
                act.activation(zs[:, :, :], hf[:, :, :], ACT.Square).then_inc(sem["gate_sq"], 1)
                act.wait_ge(sem["gate_inv"], l + 1)
                act.activation(rs[:, :, :], rs[:, :, :], ACT.Sqrt).then_inc(sem["gate_rs"], 1)
                act.wait_ge(sem["y_normed"], l + 1)
                act.wait_ge(sem["w_used"], N0["ssd_out", l])
                hi_of_x(5 * l + 3, hf)
                act_phase(act, ("ssd_out", l), KT // MT)
                act.wait_ge(sem["merged"], 1 + l)
                hi_of_x(5 * l + 4, hf)
                act_phase(act, ("w_o", l), KT // MT, lambda i, c, banks: act.activation(
                    zs[:, bass.ds(4 * i + 2 * c, 2), :], banks, ACT.Copy), end=l == L - 1)
                act.wait_ge(acc_free[0], Q0["gu", l] // 2 + Q0["gu", l] % 2)
                act.wait_ge(acc_free[1], Q0["gu", l] // 2)
                norm_sq(4 * l + 2, zs)
                norm_rs(4 * l + 2)
                act.wait_ge(sem["x_ready"], 4 + 2 * l)
                norm_sq(4 * l + 3, x)
                norm_rs(4 * l + 3)
                act.wait_ge(sem["h_ready"], 2 * l + 2)
                hi_of_x(5 * l + 5, hf)
                act.wait_ge(sem["st_out"], 16 * (l + 1))
                if l % 2:
                    act.wait_ge(sem["logits_ready"], 1)
                    act.wait_ge(sem["route_arg"], 1)
                    act.activation(lg[:, :, :], lg[:, :, :], ACT.Exp).then_inc(sem["route_exp"], 1)

                def expert(e, pairs_before, last):
                    n0, q0 = N0["gu", l], Q0["gu", l]

                    def gates(i):
                        split_hi(act, n0 + 1, i, 2, e)
                        act.wait_ge(sem["w_used"], n0 + 1 + 2 * i + EN * e)
                        act.wait_ge(sem["gu_ready"], pairs_before + i + FT // MT * e)
                        act.activation(sg[:, :, :], acc[:, 2 * (q0 % 2):2 * (q0 % 2) + 2, 0:T], ACT.Silu) \
                            .then_inc(acc_free[q0 % 2], 1)
                        split_hi(act, n0 + 2, i, 2, e)
                        act.wait_ge(sem["gu_ready"], pairs_before + 1 + i + FT // MT * e)
                        act.activation(ghi[:, bass.ds(2 * i, 2), :], gu[:, :, :], ACT.Copy).then_inc(sem["g_hi"], 1)

                    with act.Fori(0, FT // MT) as i:
                        gates(i)
                    n1 = N0["wd", l]
                    C = 2 * len(KG)

                    def downs(i, last=False):
                        for c in range(C - (1 if last else 0)):
                            split_hi(act, n1 + c + 1, i, C, e)
                    if last:
                        downs(0)
                        downs(1, True)
                    else:
                        with act.Fori(0, KT // MT // 2) as i:
                            downs(i)

                act.preload_act_table(ACT.Silu)
                if l % 2 == 0:
                    expert(0, 1, False)
                    act.wait_ge(acc_free[0], Q0["wd", l] // 2 + KT // MT // 2 + Q0["wd", l] % 2)
                    act.wait_ge(acc_free[1], Q0["wd", l] // 2 + KT // MT // 2)
                else:
                    with act.If(crowded(act)):
                        act.wait_ge(sem["combine_turned"], 1)
                        act.activation(comb[:, :], ms[0:E, 2, 0:T], ACT.Copy).then_inc(sem["combine_ready"], 1)
                        for e in range(E):
                            act.wait_ge(sem["combine_spread"], e + 1)
                            act.activation(cbc[:, e, :], ms[:, e % 4, 0:T], ACT.Copy) \
                                .then_inc(sem["combine_spread_ready"], 1)
                        split_hi(act, NX, 0)
                        act.preload_act_table(ACT.Silu)
                        with act.Fori(0, E - 1) as e:
                            expert(e, 1 + FT // MT, False)
                        expert(E - 1, 1 + FT // MT, True)
                    with act.Else():
                        for c in range(3):
                            rows = Q if c < NQ else B
                            act.wait_ge(sem["h_turned"], c + 1)
                            act.activation(htokhi[0:rows, c, :], msf[0:rows, (c % 2) * D:(c % 2 + 1) * D], ACT.Copy) \
                                .then_inc(sem["htok_hi"], 1)
                        split_hi3(act, 0, 0)
                        split_hi3(act, 1, 0)
                        act.wait_ge(sem["gathered"], 1)
                        act.activation(hghi[:, :, :].rearrange("p k t -> p (k t)"), msf[:, 0:D], ACT.Copy) \
                            .then_inc(sem["hg_hi"], 1)

                        def picked(e, last):
                            def turned(b, q):
                                act.wait_ge(sem["gu_turned"], q + 2 + R3 * b + FP * e)
                                act.activation(gthi[:, bass.ds(MT * q + MT * R3 * b, MT), :],
                                               ms[:, q % R3, 0:MT * P].rearrange("p (k t) -> p k t", k=MT), ACT.Copy) \
                                    .then_inc(sem["gt_hi"], 1)

                            def pair(b, q):
                                peeled = isinstance(b, int)
                                ahead(2 * q + 2, b)
                                if not (peeled and q == 0):
                                    turned(b, q - 1)
                                ahead(2 * q + 3, b)
                                act.wait_ge(sem["w_used"], NX + 2 * q + 2 + 2 * R3 * b + SN * e)
                                act.wait_ge(sem["gu_done"], R3 + q + R3 * b + FP * e)
                                act.activation(sgs[:, :], acc[:, q % R3, 0:CW], ACT.Silu).then_inc(sem["gate_ready"], 1)
                                if peeled and q == 1:
                                    act.wait_ge(sem["gw_turned"], 1 + e)
                                    act.activation(giveT[:, :], acc[:, 3, 0:T], ACT.Copy).then_inc(sem["gw_ready"], 1)

                            def ahead(j, b):
                                s = j % R3
                                act.wait_ge(raw_full[s], 16 * (FILLS[s] + j // R3 + 1) + 16 * (SN // R3) * e + 32 * b)
                                act.wait_ge(sem["w_used"], NX + j - R3 + 1 + SN * e + 2 * R3 * b)
                                act.activation(whi[s], raw[s], ACT.Copy).then_inc(sem["hi_ready"], 1)
                            pairs(act, pair)
                            for d in range(FD):
                                if not (last and d >= FD - 2):
                                    split_hi3(act, 2 * FP + d + 2, e)
                                if d == 0:
                                    turned(0, FP - 1)
                            act.wait_ge(sem["w_used"], NX + SN + SN * e)
                            act.activation(ys[:, :].rearrange("p (h c) -> p h c", h=2), acc[:, 2:4, :], ACT.Copy) \
                                .then_inc(sem["ys_ready"], 1)
                            if not last:
                                act.wait_ge(sem["gathered"], 2 + e)
                                act.activation(hghi[:, :, :].rearrange("p k t -> p (k t)"), msf[:, 0:D], ACT.Copy) \
                                    .then_inc(sem["hg_hi"], 1)
                        act.preload_act_table(ACT.Silu)
                        with act.Fori(0, E - 1) as e:
                            picked(e, False)
                        picked(E - 1, True)
                    act.wait_ge(sem["moe_done"], 1)
                norm_sq(4 * l + 4, facc)
                norm_rs(4 * l + 4)
                if l < L - 1:
                    act.wait_ge(sem["x_ready"], 5 + 2 * l)

        @block.vector
        def _(dve):
            steps = 0

            def then(ins):
                nonlocal steps
                steps += 1
                ins.then_inc(sem["dve_chain"], 1)
                dve.wait_ge(sem["dve_chain"], steps)

            def mean_inv(out, sums, count, done):
                then(dve.tensor_scalar(out, sums, 1.0 / count, EPS, ALU.mult, ALU.add))
                dve.reciprocal(out, out).then_inc(done, 1)

            def norm_inv(v):
                dve.wait_ge(sem["ssq_ready"], v)
                mean_inv(rs[:, 0, :], ms[:, 0, 0:T], D, sem["inv_ready"])

            def lo_of_x(v, src):
                dve.wait_ge(sem["xs_hi"], v)
                dve.tensor_tensor(xlo[:, :, :], src[:, :, :], xhi[:, :, :].bitcast(F32), ALU.subtract) \
                    .then_inc(sem["xs_lo"], 1)

            def modulated(l, k, v, hv):
                norm_inv(v)
                dve.wait_ge(sem["rs_ready"], v)
                then(dve.tensor_tensor(hf[:, :, :], x[:, :, :], bc(rs[:, 0, :], 1, [P, KT, T]), ALU.mult))
                sh, sc = mod[:, l, 3 * k * KT:(3 * k + 1) * KT, :], mod[:, l, (3 * k + 1) * KT:(3 * k + 2) * KT, :]
                for t in range(KT):
                    dve.tensor_scalar(hf[:, t, 0:S], hf[:, t, 0:S], sc[:, t, 0:1], sh[:, t, 0:1], ALU.mult, ALU.add)
                then(dve.tensor_tensor(hf[:, :, S:T], hf[:, :, S:T], sc[:, :, 1:1 + B], ALU.mult))
                dve.tensor_tensor(hf[:, :, S:T], hf[:, :, S:T], sh[:, :, 1:1 + B], ALU.add).then_inc(sem["h_ready"], 1)

            def add_normed(l, k, v, src):
                norm_inv(v)
                dve.wait_ge(sem["rs_ready"], v)
                then(dve.tensor_tensor(src[:, :, :], src[:, :, :], bc(rs[:, 0, :], 1, [P, KT, T]), ALU.mult))
                g = mod[:, l, (3 * k + 2) * KT:(3 * k + 3) * KT, :]
                for t in range(KT):
                    dve.scalar_tensor_tensor(out=x[:, t, 0:S], in0=src[:, t, 0:S], scalar=g[:, t, 0:1],
                                             in1=x[:, t, 0:S], op0=ALU.mult, op1=ALU.add)
                then(dve.tensor_tensor(src[:, :, S:T], src[:, :, S:T], g[:, :, 1:1 + B], ALU.mult))
                dve.tensor_tensor(x[:, :, S:T], x[:, :, S:T], src[:, :, S:T], ALU.add).then_inc(sem["x_ready"], 1)

            dve.memset(ctok[0:NC, :], 0.0).then_inc(sem["ctok_zero"], 1)
            dve.memset(cst[:, :, :].bitcast(F32), 0.0).then_inc(sem["cst_zero"], 1)
            then(dve.memset(ones[:, :], 1.0))
            dve.wait_ge(sem["c_hi"], 1)
            dve.tensor_tensor(cst[:, :, CL:CL + NC], ms[:, 0, 0:KT * NC].rearrange("p (k c) -> p k c", k=KT),
                              cst[:, :, 0:NC].bitcast(F32), ALU.subtract).then_inc(sem["c_lo"], 1)
            dve.wait_ge(sem["params_turned"], 1)
            dve.tensor_copy(PT[:, :, :].rearrange("p l r -> p (l r)"), ms[:, 1, 0:L * NROW]) \
                .then_inc(sem["params_ready"], 1)
            dve.wait_ge(sem["params_ready"], 1)
            b0 = ROWS["b_mod"][0]
            dve.tensor_copy(bmod.rearrange("p (l r) -> p l r", l=L), PT[:, :, b0:b0 + 6 * KT])
            dve.wait_ge(sem["state_turned"], 1)
            dve.tensor_copy(stT[:, :, :, :].rearrange("p l c r -> p l (c r)"), ms[:, 2:4, 0:CT * B * (CK - 1)]) \
                .then_inc(sem["state_ready"], 1)
            for c in range(NQ + 1):
                rows = Q if c < NQ else B
                dve.wait_ge(sem["x_turned"], c + 1)
                b0 = 2 * (c % 2)
                dve.tensor_copy(x[:, :, c * Q:c * Q + rows].rearrange("p (b k) t -> p b k t", b=2),
                                ms[:, b0:b0 + 2, :].rearrange("p b (k t) -> p b k t", t=P)[:, :, :, 0:rows]) \
                    .then_inc(sem["x_ready"], 1)
            NM = N0["xbc", 0]

            def mod_lo(m, s):
                dve.wait_ge(sem["hi_ready"], m + 1)
                dve.tensor_tensor(wlo[s], raw[s], whi[s].bitcast(F32), ALU.subtract).then_inc(sem["lo_ready"], 1)

            def mod_add(m, s):
                dve.wait_ge(sem["folded"], m + 1)
                c0 = MT * m if isinstance(m, int) else dve.snap(MT * m)
                dve.tensor_tensor(modf[:, bass.ds(c0, MT), :], ms[:, s, 0:MT * NC].rearrange("p (j c) -> p j c", j=MT),
                                  bc(bmod[:, bass.ds(c0, MT)], 2, [P, MT, NC]), ALU.add).then_inc(sem["mod_added"], 1)

            def mod_body(i, last=False):
                for c in range(R3):
                    if not (last and c == R3 - 1):
                        mod_lo(R3 * i + c + 1, (c + 1) % R3)
                    if later(i, 1):
                        mod_add(R3 * i + c - R3, c)
            mod_lo(0, 0)
            mod_body(0)
            with dve.Fori(0, NM // R3 - 2) as i:
                mod_body(i + 1)
            mod_body(NM // R3 - 1, True)
            for m in range(NM - R3, NM):
                mod_add(m, m % R3)
            dve.wait_ge(sem["mod_added"], NM)
            for l in range(L):
                for k, (pre, post) in enumerate((("mix_pre_g", "mix_post_g"), ("ffn_pre_g", "ffn_post_g"))):
                    sc = mod[:, l, (3 * k + 1) * KT:(3 * k + 2) * KT, :]
                    g = mod[:, l, (3 * k + 2) * KT:(3 * k + 3) * KT, :]
                    dve.scalar_tensor_tensor(out=sc, in0=sc, scalar=1.0, in1=bc(row(pre, l), 2, [P, KT, NC]),
                                             op0=ALU.add, op1=ALU.mult)
                    ins = dve.tensor_tensor(g, g, bc(row(post, l), 2, [P, KT, NC]), ALU.mult)
            ins.then_inc(sem["mod_ready"], 1)
            dve.wait_ge(sem["mod_ready"], 1)

            split_lo(dve, N0["xbc", 0], 0)
            for l in range(L):
                modulated(l, 0, 4 * l + 1, 2 * l + 1)
                lo_of_x(5 * l + 1, hf)
                ins = dve.memset(xrawv[:, :, 0:CK - 1], 0.0)
                then(ins)
                dve_phase(dve, ("xbc", l), IN_CHUNKS["xbc"])
                n, q = N0["dt", l], Q0["dt", l]
                split_lo(dve, n + 1, 0)
                dve.wait_ge(sem["w_used"], n + 1)
                dve.tensor_scalar(dth[:, 1, :], acc[0:H, 2 * (q % 2), 0:T], headp[:, 0, l:l + 1], None, ALU.add) \
                    .then_inc(acc_free[q % 2], 1)
                cum, dt, dta, e_, r_, s2, p_, mx = (dth[:, k, :] for k in range(8))
                dve.wait_ge(acc_free[q % 2], q // 2 + 1)
                dve.scalar_tensor_tensor(out=e_, in0=dt, scalar=-1.0, in1=dt, op0=ALU.mult, op1=ALU.max) \
                    .then_inc(sem["dt_abs"], 1)
                dve.tensor_scalar(mx, dt, 0.0, None, ALU.max)

                def after_v(c):
                    if c == 0:
                        dve.wait_ge(sem["dt_exp"], l + 1)
                        then(dve.tensor_scalar(r_, e_, 2.0, None, ALU.add))
                        then(dve.reciprocal(r_, r_))
                        then(dve.tensor_tensor(r_, e_, r_, ALU.mult))
                    if c == 1:
                        then(dve.tensor_tensor(s2, r_, r_, ALU.mult))
                        then(dve.tensor_scalar(p_, s2, 1.0 / 17, None, ALU.mult))
                        for k in range(15, 9, -2):
                            then(dve.scalar_tensor_tensor(out=p_, in0=p_, scalar=1.0 / k, in1=s2, op0=ALU.add, op1=ALU.mult))
                    if c == 2:
                        for k in range(9, 1, -2):
                            then(dve.scalar_tensor_tensor(out=p_, in0=p_, scalar=1.0 / k, in1=s2, op0=ALU.add, op1=ALU.mult))
                        then(dve.scalar_tensor_tensor(out=p_, in0=p_, scalar=1.0, in1=r_, op0=ALU.add, op1=ALU.mult))
                        then(dve.scalar_tensor_tensor(out=dt, in0=p_, scalar=2.0, in1=mx, op0=ALU.mult, op1=ALU.add))
                    if c == 3:
                        dve.wait_ge(sem["a_exp"], 1)
                        then(dve.tensor_scalar(dta, dt, expa[:, l:l + 1], -1.0, ALU.mult, ALU.mult))
                        for k in range(NQ):
                            dve.tensor_tensor_scan(cum[:, k * Q:(k + 1) * Q], ones[0:H, 0:Q], dta[:, k * Q:(k + 1) * Q],
                                                   0.0, ALU.mult, ALU.add)
                        dve.tensor_copy(spin[:, B:2 * B], dt[:, S:T])
                        dve.tensor_copy(spin[:, 2 * B:2 * B + 1], headp[:, 2, l:l + 1]).then_inc(sem["cum_ready"], 1)

                def conv(tiles):
                    for k in range(CK):
                        for t in tiles:
                            src = xrawv[:, t, k:k + S]
                            if k == 0:
                                ins = dve.tensor_scalar(xcv[:, t, 0:S], src, row("conv_w", l, t), row("conv_b", l, t),
                                                        ALU.mult, ALU.add)
                            else:
                                ins = dve.scalar_tensor_tensor(out=xcv[:, t, 0:S], in0=src,
                                                               scalar=row("conv_w", l, k * CT + t),
                                                               in1=xcv[:, t, 0:S], op0=ALU.mult, op1=ALU.add)
                        then(ins)

                def after_u(c):
                    conv(((0, 1), (2, 3), (4,), (5,))[c])

                def after_z(c):
                    if c == 0:
                        dve.wait_ge(sem["v_sum"], l + 1)
                        then(dve.tensor_scalar(rs[:, 1, :], ms[:, 0, 0:T], 1.0 / D, None, ALU.mult))
                        dve.tensor_tensor(vb[:, :, :], vb[:, :, :], bc(rs[:, 1, :], 1, [P, KT, T]), ALU.subtract) \
                            .then_inc(sem["v_centered"], 1)
                    else:
                        conv((2 * c + 4, 2 * c + 5))
                    if c == 3:
                        st = stT[:, l, :, :].rearrange("p c (b k) -> p c b k", k=CK - 1)
                        wk = row("conv_w", l).rearrange("p (k c) -> p k c", k=CK)
                        xs_ = xcv[:, :, S:T]
                        then(dve.tensor_tensor(xs_, xrawv[:, :, CK - 1 + S:CK - 1 + T],
                                               bc(wk[:, CK - 1, :], 2, [P, CT, B]), ALU.mult))
                        for k in range(CK - 1):
                            then(dve.tensor_tensor(tmp[:, :, :], st[:, :, :, k], bc(wk[:, k, :], 2, [P, CT, B]), ALU.mult))
                            then(dve.tensor_tensor(xs_, xs_, tmp[:, :, :], ALU.add))
                        dve.tensor_tensor(xs_, xs_, bc(row("conv_b", l), 2, [P, CT, B]), ALU.add) \
                            .then_inc(sem["conv_done"], 1)

                def sample(b):
                    s = b % 2
                    Sb = sring[:, s]
                    Bb, Cb = (ms[:, 2 + s, g0 * P:(g0 + G) * P].rearrange("p (g n) -> p g n", g=G) for g0 in (0, G))
                    dve.wait_ge(sem["bc_spread"], l * B + b + 1)
                    if b:
                        dve.wait_ge(sem["samp_used"], l * B + b)
                    then(dve.tensor_tensor(sprod.rearrange("p (g k) n -> p g k n", g=G),
                                           Bb.unsqueeze(2).to_broadcast([P, G, KT // G, P]),
                                           bc(dtx[:, :, b], 2, [P, KT, P]).rearrange("p (g k) n -> p g k n", g=G), ALU.mult))
                    dve.wait_ge(s_in[s], 16 * (l * B // 2 + b // 2 + 1))
                    for k in range(KT):
                        ins = dve.scalar_tensor_tensor(out=Sb[:, k, :], in0=Sb[:, k, :], scalar=spx[:, k, b:b + 1],
                                                       in1=sprod[:, k, :], op0=ALU.mult, op1=ALU.add)
                    ins.then_inc(sem["s_new"], 1)
                    dve.wait_ge(sem["s_new"], l * B + b + 1)
                    for k in range(KT):
                        ins = dve.tensor_tensor_reduce(sprod[:, k, :], Sb[:, k, :], Cb[:, k * G // KT, :], 1.0, 0.0,
                                                       ALU.mult, ALU.add, accum_out=ysm[:, k, b:b + 1])
                    ins.then_inc(sem["samp_used"], 1)

                def after_ga(c):
                    if c == 0:
                        dve.wait_ge(sem["xc_ready"], l + 1)
                        dve.wait_ge(sem["spread_copied"], l + 1)
                        then(dve.tensor_tensor(dtx[:, :, :], xcv[:, 0:KT, S:T], spx[:, :, B:2 * B], ALU.mult))
                        dve.wait_ge(sem["v_ssq"], l + 1)
                        mean_inv(rs[:, 0, :], ms[:, 1, 0:T], D, sem["v_inv"])
                    sample(c)

                def after_gb(c):
                    sample(B // 2 + c)
                    if c == 0:
                        dve.wait_ge(sem["v_rs"], l + 1)
                        then(dve.tensor_tensor(vb[:, :, :], vb[:, :, :], bc(rs[:, 0, :], 1, [P, KT, T]), ALU.mult))
                    if c == 1:
                        for t in range(KT):
                            ins = dve.tensor_scalar(vb[:, t, :], vb[:, t, :], row("cmlp_ln_g", l, t),
                                                    row("cmlp_ln_b", l, t), ALU.mult, ALU.add)
                        ins.then_inc(sem["v_normed"], 1)
                dve_phase(dve, ("v", l), IN_CHUNKS["v"], after=after_v)
                for p in range(2):
                    dve.wait_ge(acc_free[p], (Q0["dt", l] + 1 - p) // 2)
                dve_phase(dve, ("u", l), IN_CHUNKS["u"], after=after_u)
                dve_phase(dve, ("z", l), IN_CHUNKS["z"], after=after_z)
                dve_phase(dve, ("ga", l), IN_CHUNKS["ga"], after=after_ga)
                dve_phase(dve, ("gb", l), IN_CHUNKS["gb"], after=after_gb)
                dve.wait_ge(sem["sp_in"], 16 * (4 + L))
                dve.tensor_scalar(diag[:, 0, :], ident[0:KT, 0:KT], w00[:, l:l + 1], None, ALU.mult)
                dve.tensor_scalar(diag[:, 1, :], ident[0:KT, 0:KT], spb[:, l, 0:1], None, ALU.mult) \
                    .then_inc(sem["diag_ready"], 1)
                dve.wait_ge(sem["w_turned"], l + 1)
                dve.tensor_tensor(wT, msf[:, 1024:2048].rearrange("p (g q) -> p g q", g=KT),
                                  bc(tri[:, :], 1, [P, KT, Q]), ALU.mult).then_inc(sem["w_ready"], 1)
                dve.wait_ge(sem["v_normed"], l + 1)
                dve.wait_ge(sem["sp_bcast_ready"], l + 1)
                g0 = tmp[:, 0:KT, :]
                then(dve.tensor_tensor(g0, vb[:, :, S:T], bc(spc[:, 0, :], 2, [P, KT, B]), ALU.mult))
                then(dve.tensor_tensor(g0, g0, bc(spc[:, 1, :], 2, [P, KT, B]), ALU.add))
                dve.tensor_tensor(ub[:, :, S:T], ub[:, :, S:T], g0, ALU.mult)
                for c in range(NQ):
                    dve.wait_ge(sem["sp_out"], l * NQ + c + 1)
                    ins = dve.tensor_tensor(ub[:, :, c * Q:(c + 1) * Q], ub[:, :, c * Q:(c + 1) * Q],
                                            msf[:, c * 1024:(c + 1) * 1024].rearrange("p (k q) -> p k q", k=KT), ALU.mult)
                ins.then_inc(sem["sp_taken"], 1)
                lo_of_x(5 * l + 2, ub)
                dve_phase(dve, ("cmlp_out", l), KT // MT, lambda i, c, banks: dve.tensor_tensor(
                    sgb[:, bass.ds(4 * i + 2 * c, 2), :], sgb[:, bass.ds(4 * i + 2 * c, 2), :], banks, ALU.mult))
                for c in range(NQ):
                    v = l * NQ + c
                    toks = slice(c * Q, (c + 1) * Q)
                    dve.wait_ge(sem["b_tok"], v + 1)
                    dve.tensor_copy(tokp[:, :, :].rearrange("p a h -> p (a h)"), ms[:, 2, 2 * P:2 * P + 2 * H]) \
                        .then_inc(sem["tok_ready"], 1)
                    dve.wait_ge(sem["tok_ready"], v + 1)
                    dve.tensor_tensor(xdt[:, :].rearrange("p (h d) -> p h d", h=H),
                                      msf[:, 0:D].rearrange("p (h d) -> p h d", h=H),
                                      bc(tokp[:, 1, :], 2, [P, H, HD]), ALU.mult).then_inc(sem["xdt_ready"], 1)
                    dve.wait_ge(sem["cb_ready"], v + 1)
                    dve.tensor_tensor(cbm[:, :, :], ms[:, 3, 0:G * Q].rearrange("p (g q) -> p g q", g=G),
                                      bc(tri[:, :], 1, [P, G, Q]), ALU.mult).then_inc(sem["cbm_ready"], 1)
                    dve.wait_ge(sem["cumb_ready"], v + 1)
                    last = ms[:, :, :].rearrange("p b (h q) -> p (b h) q", q=Q)[:, :, Q - 1]
                    then(dve.tensor_copy(lastc[:, :], last))
                    dve.tensor_tensor(wend[:, :], lastc[:, :], tokp[:, 0, :], ALU.subtract).then_inc(sem["wend_arg"], 1)
                    for h in range(H):
                        cs = tokp[:, 0, h:h + 1]
                        ins = dve.tensor_scalar(mix[:, h, :], ms[:, h // 4, (h % 4) * Q:(h % 4 + 1) * Q], cs, cs,
                                                ALU.min, ALU.subtract)
                    ins.then_inc(sem["seg_ready"], 1)
                    dve.wait_ge(sem["wend_ready"], v + 1)
                    dve.tensor_tensor(xw[:, :].rearrange("p (h d) -> p h d", h=H),
                                      xdt[:, :].rearrange("p (h d) -> p h d", h=H),
                                      bc(wend[:, :], 2, [P, H, HD]), ALU.mult).then_inc(sem["xw_ready"], 1)
                    if c:
                        dve.wait_ge(sem["ce_exp"], l + 1)
                        for g in range(G):
                            ins = dve.tensor_tensor(ce[:, g * R:(g + 1) * R, :], ce[:, g * R:(g + 1) * R, :],
                                                    bc(xcv[:, KT + G + g, toks], 1, [P, R, Q]), ALU.mult)
                        ins.then_inc(sem["ce_ready"], 1)
                    dve.wait_ge(sem["mix_exp"], v + 1)
                    for g in range(G):
                        ins = dve.tensor_tensor(mix[:, g * R:(g + 1) * R, :], mix[:, g * R:(g + 1) * R, :],
                                                bc(cbm[:, g, :], 1, [P, R, Q]), ALU.mult)
                    ins.then_inc(sem["mix_ready"], 1)
                    dve.wait_ge(sem["y_part"], v + 1)
                    dve.wait_ge(sem["vs_out"], 16 * (l + 1))
                    for t in range(KT):
                        ins = dve.scalar_tensor_tensor(out=hf[:, t, toks], in0=xcv[:, t, toks],
                                                       scalar=spx[:, t, 2 * B:2 * B + 1],
                                                       in1=ms[:, t // 4, (t % 4) * Q:(t % 4 + 1) * Q],
                                                       op0=ALU.mult, op1=ALU.add)
                    ins.then_inc(sem["y_taken"], 1)
                    if c:
                        dve.wait_ge(sem["last_ready"], v + 1)
                        hv = hT[:, :].rearrange("p (h d) -> p h d", h=H)
                        then(dve.tensor_tensor(hv, hv, bc(elast[:, :], 2, [P, H, HD]), ALU.mult))
                        dve.wait_ge(sem["st_part"], v + 1)
                        dve.tensor_tensor(hT[:, :], hT[:, :], msf[:, 1024:2048], ALU.add).then_inc(sem["st_ready"], 1)

                dve.wait_ge(sem["samp_used"], (l + 1) * B)
                then(dve.tensor_tensor(hf[:, :, S:T], xcv[:, 0:KT, S:T],
                                       spx[:, :, 2 * B:2 * B + 1].to_broadcast([P, KT, B]), ALU.mult))
                then(dve.tensor_tensor(hf[:, :, S:T], hf[:, :, S:T], ysm[:, :, :], ALU.add))
                dve.tensor_tensor(hf[:, :, :], hf[:, :, :], zs[:, :, :], ALU.mult).then_inc(sem["samp_done"], 1)
                dve.wait_ge(sem["gate_ssq"], l + 1)
                mean_inv(rs[:, :, :], ms[:, 2:4, 0:T], D // G, sem["gate_inv"])
                dve.wait_ge(sem["gate_rs"], l + 1)
                for g in range(G):
                    k0, k1 = g * KT // G, (g + 1) * KT // G
                    ins = dve.tensor_tensor(hf[:, k0:k1, :], hf[:, k0:k1, :], bc(rs[:, g, :], 1, [P, KT // G, T]),
                                            ALU.mult)
                then(ins)
                dve.tensor_tensor(hf[:, :, :], hf[:, :, :], bc(row("ssm_norm_g", l), 2, [P, KT, T]), ALU.mult) \
                    .then_inc(sem["y_normed"], 1)
                lo_of_x(5 * l + 3, hf)
                dve_phase(dve, ("ssd_out", l), KT // MT, lambda i, c, banks: dve.tensor_tensor(
                    sga[:, bass.ds(4 * i + 2 * c, 2), :], sga[:, bass.ds(4 * i + 2 * c, 2), :], banks, ALU.mult))

                for p in range(2):
                    dve.wait_ge(acc_free[p], (Q0["w_o", l] + 1 - p) // 2)
                dve.tensor_tensor(hf[:, :, :], sga[:, :, :], sgb[:, :, :], ALU.add).then_inc(sem["merged"], 1)
                lo_of_x(5 * l + 4, hf)
                dve_phase(dve, ("w_o", l), KT // MT, end=l == L - 1)
                add_normed(l, 0, 4 * l + 2, zs)
                dve.wait_ge(sem["x_ready"], 4 + 2 * l)
                modulated(l, 1, 4 * l + 3, 2 * l + 2)
                lo_of_x(5 * l + 5, hf)
                dve.wait_ge(sem["st_out"], 16 * (l + 1))

                if l % 2:
                    dve.wait_ge(sem["logits_ready"], 1)
                    then(dve.memset(lg[:, :, :], 0.0))
                    then(dve.tensor_copy(lg[:, 0:NQ, :], ms[:, 1, 0:NQ * E].rearrange("p (c e) -> p c e", e=E)))
                    then(dve.tensor_copy(lg[0:B, NQ, :], ms[0:B, 1, NQ * E:(NQ + 1) * E]))
                    for c in range(3):
                        mine, other = bc(lg[:, c, :], 2, [P, E, E]), bc(lg[:, c, :], 1, [P, E, E])
                        dve.tensor_reduce(top[:, c, 0:1], lg[:, c, :], AX.X, ALU.max)
                        then(dve.tensor_tensor(eqm[:, :, :], other, mine, ALU.is_equal))
                        then(dve.tensor_tensor(eqm[:, :, :], eqm[:, :, :], earlier[:, :, :], ALU.mult))
                        then(dve.tensor_tensor(cmp_[:, :, :], other, mine, ALU.is_gt))
                        then(dve.tensor_tensor(cmp_[:, :, :], cmp_[:, :, :], eqm[:, :, :], ALU.add))
                        then(dve.tensor_reduce(rank[:, c, :], cmp_[:, :, :], AX.X, ALU.add))
                    then(dve.tensor_scalar(rank[:, :, :], rank[:, :, :], 1.5, None, ALU.is_lt))
                    then(dve.memset(sel[:, :, :], 0.0))
                    dve.tensor_copy(sel[:, 0:NQ, :], rank[:, 0:NQ, :])
                    dve.tensor_copy(sel[0:B, NQ, :], rank[0:B, NQ, :]).then_inc(sem["sel_ready"], 1)
                    dve.tensor_tensor(lg[:, :, :], lg[:, :, :], top[:, :, 0:1].to_broadcast([P, 3, E]), ALU.subtract) \
                        .then_inc(sem["route_arg"], 1)
                    dve.wait_ge(sem["route_exp"], 1)
                    then(dve.tensor_tensor(rank[:, :, :], rank[:, :, :], lg[:, :, :], ALU.mult))
                    then(dve.tensor_reduce(rsum[:, :], rank[:, :, :], AX.X, ALU.add))
                    then(dve.reciprocal(rsum[:, :], rsum[:, :]))
                    dve.tensor_tensor(rank[:, :, :], rank[:, :, :], bc(rsum[:, :], 2, [P, 3, E]), ALU.mult) \
                        .then_inc(sem["route_done"], 1)
                    dve.wait_ge(sem["counted"], 1)
                    then(dve.tensor_copy(place[:, :, :].rearrange("p c e -> p (c e)"), ms[:, 3, 0:4 * E]))
                    then(dve.tensor_reduce(most[:, :], place[:, 3, :], AX.X, ALU.max))
                    dve.tensor_scalar(flag[:, :], most[:, :], float(P), None, ALU.is_gt).then_inc(sem["flag_ready"], 1)
                if l == 0:
                    dve.memset(facc[:, :, :], 0.0).then_inc(sem["gu_ready"], 1)
                    dve.wait_ge(sem["gu_ready"], 1)
                else:
                    then(dve.memset(facc[:, :, :], 0.0))

                def expert(e, gated, last):
                    n0, q0 = N0["gu", l], Q0["gu", l]
                    gb = 0 if l % 2 == 0 else FT // MT

                    def gates(i):
                        split_lo(dve, n0 + 1, i, 2, e)
                        pair = (q0 + 1) % 2
                        split_lo(dve, n0 + 2, i, 2, e)
                        dve.wait_ge(sem["w_used"], n0 + 2 + 2 * i + EN * e)
                        dve.wait_ge(acc_free[q0 % 2], q0 // 2 + 1 + i + EQ // 2 * e)
                        up = acc[:, 2 * pair:2 * pair + 2, 0:T]
                        if gated:
                            dve.tensor_tensor(sg[:, :, :], sg[:, :, :], cbc[:, bass.ds(e, 1), :].to_broadcast([P, MT, T]),
                                              ALU.mult).then_inc(sem["sg_ready"], 1)
                            dve.wait_ge(sem["sg_ready"], 1 + i + FT // MT * e)
                        dve.tensor_tensor(gu[:, :, :], sg[:, :, :], up, ALU.mult).then_inc(sem["gu_ready"], 1)
                        dve.wait_ge(sem["g_hi"], gb + 1 + i + FT // MT * e)
                        dve.tensor_tensor(glo[:, bass.ds(2 * i, 2), :], gu[:, :, :],
                                          ghi[:, bass.ds(2 * i, 2), :].bitcast(F32), ALU.subtract) \
                            .then_inc(acc_free[pair], 1)
                    with dve.Fori(0, FT // MT) as i:
                        gates(i)
                    n1, q1 = N0["wd", l], Q0["wd", l]
                    C = 2 * len(KG)

                    def downs(i, last=False):
                        for g in range(2):
                            for s in range(len(KG)):
                                c = g * len(KG) + s
                                if not (last and c == C - 1):
                                    split_lo(dve, n1 + c + 1, i, C, e)
                            dve.wait_ge(sem["w_used"], n1 + g * len(KG) + len(KG) + C * i + EN * e)
                            pair = (q1 + g) % 2
                            f = facc[:, bass.ds(4 * i + 2 * g, 2), :]
                            dve.tensor_tensor(f, f, acc[:, 2 * pair:2 * pair + 2, 0:T], ALU.add) \
                                .then_inc(acc_free[pair], 1)
                    if last:
                        downs(0)
                        downs(1, True)
                    else:
                        with dve.Fori(0, KT // MT // 2) as i:
                            downs(i)

                if l % 2 == 0:
                    expert(0, False, False)
                else:
                    crowd = crowded(dve)
                    with dve.If(crowd):
                        dve.wait_ge(sem["combine_spread_ready"], E)
                        split_lo(dve, NX, 0)
                        with dve.Fori(0, E - 1) as e:
                            expert(e, True, False)
                        expert(E - 1, True, True)
                    with dve.Else():
                        for c in range(3):
                            rows = Q if c < NQ else B
                            dve.wait_ge(sem["htok_hi"], c + 1)
                            dve.tensor_tensor(htoklo[0:rows, c, :], msf[0:rows, (c % 2) * D:(c % 2 + 1) * D],
                                              htokhi[0:rows, c, :].bitcast(F32), ALU.subtract).then_inc(sem["htok_lo"], 1)
                        dve.memset(sgs[:, :], 0.0).then_inc(sem["gu_done"], R3)
                        dve.memset(gus[:, :], 0.0).then_inc(sem["gt_lo"], R3)
                        dve.memset(ys[:, :], 0.0).then_inc(sem["scat_added"], 2)
                        dve.memset(giveT[:, :], 0.0).then_inc(sem["gu_turned"], 1)
                        dve.tensor_tensor_scan(count[:, :], ones[:, :], ones[:, :], 0.0, ALU.mult, ALU.add) \
                            .then_inc(sem["counted"], 1)
                        dve.wait_ge(sem["counted"], 2)

                        def build(e):
                            col = bass.ds(e, 1)
                            for c in range(3):
                                rows = Q if c < NQ else B
                                dve.tensor_scalar(pick[0:rows, c, :], count[0:rows, :], place[0:rows, c, col],
                                                  sel[0:rows, c, col], ALU.is_equal, ALU.mult)
                            for c in range(3):
                                rows = Q if c < NQ else B
                                ins = dve.tensor_scalar(give[0:rows, c, :], count[0:rows, :], place[0:rows, c, col],
                                                        rank[0:rows, c, col], ALU.is_equal, ALU.mult)
                            ins.then_inc(sem["g_built"], 1)

                        def gathered_lo(e):
                            dve.wait_ge(sem["gathered"], 1 + e)
                            dve.tensor_copy(hglo[:, :, :].rearrange("p k t -> p (k t)"), msf[:, D:2 * D]) \
                                .then_inc(sem["hg_lo"], 1)
                        build(0)
                        split_lo3(dve, 0, 0)
                        split_lo3(dve, 1, 0)
                        gathered_lo(0)

                        def picked(e, last):
                            def turned(b, q):
                                dve.wait_ge(sem["gt_hi"], q + 1 + R3 * b + FP * e)
                                dst = bass.ds(MT * q + MT * R3 * b, MT)
                                dve.tensor_tensor(gtlo[:, dst, :],
                                                  ms[:, q % R3, 0:MT * P].rearrange("p (k t) -> p k t", k=MT),
                                                  gthi[:, dst, :].bitcast(F32), ALU.subtract).then_inc(sem["gt_lo"], 1)

                            def ahead(j, b):
                                dve.wait_ge(sem["hi_ready"], NX + j + 1 + SN * e + 2 * R3 * b)
                                dve.tensor_tensor(wlo[j % R3], raw[j % R3], whi[j % R3].bitcast(F32), ALU.subtract) \
                                    .then_inc(sem["lo_ready"], 1)

                            def pair(b, q):
                                ahead(2 * q + 2, b)
                                if not (isinstance(b, int) and q == 0):
                                    turned(b, q - 1)
                                ahead(2 * q + 3, b)
                                dve.wait_ge(sem["gate_ready"], q + 1 + R3 * b + FP * e)
                                dve.wait_ge(sem["gu_turned"], q + 1 + R3 * b + FP * e)
                                dve.tensor_tensor(gus[:, :], sgs[:, :], acc[:, q % R3, CW:2 * CW], ALU.mult) \
                                    .then_inc(sem["gu_done"], 1)
                            pairs(dve, pair)
                            for d in range(FD):
                                if not (last and d >= FD - 2):
                                    split_lo3(dve, 2 * FP + d + 2, e)
                                if d == 0:
                                    turned(0, FP - 1)
                                if d == 2 and not last:
                                    dve.wait_ge(sem["gathered"], 1 + e)
                                    dve.wait_ge(sem["gw_turned"], 1 + e)
                                    build(e + 1)
                            if not last:
                                gathered_lo(e + 1)
                            for k in range(4):
                                dve.wait_ge(sem["scattered"], k + 1 + 4 * e)
                                b0 = 2 * (k % 2)
                                f = facc[:, 2 * k:2 * k + 2, :]
                                dve.tensor_tensor(f, f, acc[:, b0:b0 + 2, 0:T], ALU.add).then_inc(sem["scat_added"], 1)
                        with dve.Fori(0, E - 1) as e:
                            picked(e, False)
                        picked(E - 1, True)
                    dve.drain().then_inc(sem["moe_done"], 1)
                add_normed(l, 1, 4 * l + 4, facc)
                dve.wait_ge(sem["x_ready"], 5 + 2 * l)

            for c in range(NQ + 1):
                rows = Q if c < NQ else B
                dve.wait_ge(sem["y_turned"], c + 1)
                dve.tensor_copy(xtok[0:rows, c * D:(c + 1) * D], msf[0:rows, (c % 2) * D:(c % 2 + 1) * D]) \
                    .then_inc(sem["y_copied"], 1)


_VECTORS = ["b_mod", "mix_pre_g", "mix_post_g", "ffn_pre_g", "ffn_post_g", "conv_b", "ssm_norm_g", "cmlp_ln_g",
            "cmlp_ln_b"]


def kernel(**inputs):
    import numpy as _np
    import concourse.bacc as _bacc
    from concourse import mybir as _mybir
    from concourse.bass_utils import run_bass_kernel_spmd as _run

    nc = _bacc.Bacc("TRN2", target_bir_lowering=False, num_devices=1)
    arrays, args = {}, {}
    for name, a in inputs.items():
        a = _np.ascontiguousarray(a)
        arrays[f"in_{name}_dram"] = a
        args[name] = nc.dram_tensor(f"in_{name}_dram", a.shape, _mybir.dt.from_np(a.dtype), kind="ExternalInput").ap()
    depth, samples, heads, head_dim, states = inputs["state_ssm"].shape
    _, _, rows, conv_dim = inputs["state_conv"].shape
    batch, seq, width = inputs["x_prompt"].shape
    outs = {
        "y_p": (batch, seq, width), "y_s": tuple(inputs["x_sample"].shape),
        "ssm_p": (depth, batch, heads, head_dim, states), "conv_p": (depth, batch, rows, conv_dim),
        "ssm_s": (depth, samples, heads, head_dim, states), "conv_s": (depth, samples, rows, conv_dim),
        "v_s": (depth, samples, 1, width),
    }
    handles = {name: nc.dram_tensor(f"out_{name}_dram", shape, _mybir.dt.float32, kind="ExternalOutput").ap()
               for name, shape in outs.items()}
    args["vectors"] = {name: args[name] for name in _VECTORS}
    hybrid_ssd_chunkmlp_moe_step(nc, args, handles)
    r = _run(nc, [arrays], core_ids=[0])
    return tuple(r.results[0][f"out_{name}_dram"] for name in outs)
```

```python
from contextlib import ExitStack

import concourse.bass as bass
from concourse import mybir

F32 = mybir.dt.float32
F32R = mybir.dt.float32r
ALU = mybir.AluOpType
ACT = mybir.ActivationFunctionType
AX = mybir.AxisListType

P = 128
MT = 2
CW = MT * P

SEMAPHORES = """params_in ctok_zero c_in x_in states_in ident_zero consts
c_silu c_turned cst_zero c_hi c_lo mt_ready folded mod_added aux_turned aux_copied x_ready
raw_full0 raw_full1 raw_full2 raw_full3 raw_full4 raw_full5 hi_ready lo_ready w_used acc_free0 acc_free1
sq_ready sq_folded ssq_ready root_ready h_ready xs_hi xs_lo mod_ready a_exp
conv_part conv_done xc_ready tail_turned tail_ready tail_out
dt_abs dt_exp cum_ready samp_decay spread_ready spread_copied
tok_ready x_tok b_tok xdt_ready bt_ready cb_ready cbm_ready cumb_ready seg_ready seg_act ce_exp
last_ready wend_arg wend_ready mix_exp mix_ready ce_ready xw_ready y_part y_taken st_part st_ready
st_turned st_copied st_out
bc_turned bc_ready bc_spread dtx_ready outer_ready samp_scaled s_in0 s_in1 s_new s_out0 s_out1 samp_used samp_done
gate_sq gate_folded gate_ssq gate_root
v_sum v_centered v_sq v_ssq v_inv v_rs v_normed vs_turned vs_copied vs_out v_tok v_tok_ready
w_sp_in w_turned w_ready sp_in diag_ready sp_bcast sp_bcast_ready sp_out sp_taken
sg_ready gu_ready g_hi route_in logits_ready route_exp route_done combine_turned combine_ready
combine_spread combine_spread_ready facc_zero sel_ready counted flag_ready
h_turned htok_hi htok_lo g_built gathered_hi gathered_lo hg_hi hg_lo gw_turned gw_ready gate_ready gu_done gu_turned gt_hi gt_lo
ys_hi ys_ready scattered scat_added moe_done
route_arg y_normed merged y_turned y_copied y_out conv_keep dve_chain""".split()


def hybrid_ssd_chunkmlp_moe_step(nc, A, O):
    D = A["x_prompt"].shape[2]
    S = A["x_prompt"].shape[1]
    B = A["x_sample"].shape[0]
    L = A["w_in"].shape[0]
    T = S + B
    KT = D // P
    H = A["a_log"].shape[1]
    HD = D // H
    NS = A["state_ssm"].shape[-1]
    CD = A["conv_w"].shape[2]
    CT = CD // P
    CK = A["conv_w"].shape[1]
    G = (CD - D) // (2 * NS)
    R = H // G
    F = A["ffn_wg"].shape[2]
    FT = F // P
    E = A["exp_wg"].shape[1]
    Q = 128
    NQ = S // Q
    EPS = 1e-6
    NC = B + 2
    CL = 32
    R3 = 3
    assert D == 1024 and T % 2 == 0 and NS == P and 2 * HD == P and F % CW == 0 and NQ == 2 and B == E == 8

    IN_COL = {"xbc": D, "z": 0}
    at = D + CD + H
    for name in ("u", "v", "ga", "gb"):
        IN_COL[name] = at
        at += D
    IN_CHUNKS = {"xbc": CD // CW, "z": D // CW, "u": D // CW, "v": D // CW, "ga": D // CW, "gb": D // CW}
    KG = [(k, min(KT, FT - k)) for k in range(0, FT, KT)]

    N0, Q0 = {}, {}
    n = q = 0

    def phase(key, chunks, groups):
        nonlocal n, q
        N0[key], Q0[key] = n, q
        n += chunks
        q += groups

    phase("mod", L * 6 * KT // MT, 0)
    R6 = 2 * R3
    M6 = n // R6
    for l in range(L):
        for name in ("xbc", "dt", "v", "u", "z", "ga", "gb"):
            k = IN_CHUNKS.get(name, 1)
            phase((name, l), k, k)
        for name in ("cmlp_out", "ssd_out", "w_o"):
            phase((name, l), KT // MT, KT // MT)
        phase(("gu", l), 2 * FT // MT, 2 * FT // MT)
        phase(("wd", l), len(KG) * KT // MT, KT // MT)
    EN = 2 * FT // MT + len(KG) * KT // MT
    EQ = 2 * FT // MT + KT // MT

    FP = FT // MT
    DK = KT * CW // D
    FD = FT // DK
    SN = 2 * FP + FD
    assert L == 2 and N0["xbc", 0] % R6 == 0 and SN % R3 == 0 and SN % R6 == R3 and FP == FD and FP % R3 == 2 and E % 2 == 0

    ROWS = {}
    at = 0
    for name, rows in (("b_mod", 6 * KT), ("mix_pre_g", KT), ("mix_post_g", KT), ("ffn_pre_g", KT),
                       ("ffn_post_g", KT), ("conv_w", CK * CT), ("conv_b", CT), ("ssm_norm_g", KT),
                       ("cmlp_ln_g", KT), ("cmlp_ln_b", KT)):
        ROWS[name] = (at, rows)
        at += rows
    NROW = at
    RT = -(-NROW // P)
    assert ROWS["conv_b"][0] == P

    ctx = ExitStack()
    with ctx:
        def sb(name, shape, dt=F32, where=ctx):
            return where.enter_context(nc.sbuf_tensor(name, shape, dt))

        raw01 = sb("raw01", [P, 2, KT, CW])
        whi01 = sb("whi01", [P, 2, KT, CW], F32R)
        wlo01 = sb("wlo01", [P, 2, KT, CW], F32R)
        x = sb("x", [P, KT, T])
        hf = sb("hf", [P, KT, T])
        rs = sb("rs", [P, 2, T])
        ident = sb("ident", [P, P])
        eps = sb("eps", [P, 1])
        ones = sb("ones", [P, P])
        tri = sb("tri", [P, P])
        earlier = sb("earlier", [P, E, E])
        spread = sb("spread", [H, D])
        PT = sb("PT", [P, L, NROW])
        mod = sb("mod", [P, L, 6 * KT, NC])
        fold = sb("fold", [CL + NC, NC])
        stT = sb("stT", [P, L, CT, B * (CK - 1)])
        headp = sb("headp", [H, 3, L])
        expa = sb("expa", [H, L])
        rw = sb("rw", [P, KT, E])
        rb = sb("rb", [1, E])
        spb = sb("spb", [KT, L, Q])
        w00 = sb("w00", [KT, L])

        split = ExitStack()
        xhi = sb("xhi", [P, KT, T], F32R, split)
        xlo = sb("xlo", [P, KT, T], F32R, split)

        mixer = ExitStack()
        zs = sb("zs", [P, KT, T], F32, mixer)
        ub = sb("ub", [P, KT, T], F32, mixer)
        vb = sb("vb", [P, KT, T], F32, mixer)
        sga = sb("sga", [P, KT, T], F32, mixer)
        sgb = sb("sgb", [P, KT, T], F32, mixer)
        xraw = sb("xraw", [P, CT * (CK - 1 + T)], F32, mixer)
        xrawv = xraw[:, :].rearrange("p (c t) -> p c t", c=CT)
        xc = sb("xc", [P, CT * T], F32, mixer)
        xcv = xc[:, :].rearrange("p (c t) -> p c t", c=CT)
        xdt = sb("xdt", [P, D], F32, mixer)
        xw = sb("xw", [P, D], F32, mixer)
        mix = sb("mix", [P, H, Q], F32, mixer)
        ce = sb("ce", [P, H, Q], F32, mixer)
        hT = sb("hT", [P, D], F32, mixer)
        bt = sb("bt", [P, G, Q], F32, mixer)
        cbm = sb("cbm", [P, G, Q], F32, mixer)
        dth = sb("dth", [H, 8, T], F32, mixer)
        spin = sb("spin", [H, 2 * B + 1], F32, mixer)
        spx = sb("spx", [P, KT, 2 * B + 1], F32, mixer)
        tokp = sb("tokp", [P, 2, H], F32, mixer)
        lastc = sb("lastc", [P, H], F32, mixer)
        wend = sb("wend", [P, H], F32, mixer)
        elast = sb("elast", [P, H], F32, mixer)
        bct = sb("bct", [B, 4 * P], F32, mixer)
        dtx = sb("dtx", [P, KT, B], F32, mixer)
        ysm = sb("ysm", [P, KT, B], F32, mixer)
        tmp = sb("tmp", [P, CT, B], F32, mixer)
        diag = sb("diag", [KT, 2, KT], F32, mixer)
        spc = sb("spc", [P, 2, KT], F32, mixer)
        mixer.close()
        ffn = ExitStack()
        raw2 = sb("raw2", [P, KT, CW], F32, ffn)
        whi2 = sb("whi2", [P, KT, CW], F32R, ffn)
        wlo2 = sb("wlo2", [P, KT, CW], F32R, ffn)
        cst = sb("cst", [P, KT, P], F32R, ffn)
        facc = sb("facc", [P, KT, T], F32, ffn)
        lg = sb("lg", [P, 3, E], F32, ffn)
        cmp_ = sb("cmp_", [P, E, E], F32, ffn)
        eqm = sb("eqm", [P, E, E], F32, ffn)
        rank = sb("rank", [P, 3, E], F32, ffn)
        top = sb("top", [P, 3, 8], F32, ffn)
        rsum = sb("rsum", [P, 3], F32, ffn)
        sel = sb("sel", [P, 3, E], F32, ffn)
        place = sb("place", [P, 4, E], F32, ffn)
        most = sb("most", [P, 1], F32, ffn)
        flag = sb("flag", [P, 1], mybir.dt.int32, ffn)
        dense = ExitStack()
        ghi = sb("ghi", [P, FT, T], F32R, dense)
        glo = sb("glo", [P, FT, T], F32R, dense)
        sg = sb("sg", [P, MT, T], F32, dense)
        gu = sb("gu", [P, MT, T], F32, dense)
        cbc = sb("cbc", [P, E, T], F32, dense)
        comb = sb("comb", [E, T], F32, dense)
        dense.close()
        sparse = ExitStack()
        htokhi = sb("htokhi", [P, 3, D], F32R, sparse)
        htoklo = sb("htoklo", [P, 3, D], F32R, sparse)
        hghi = sb("hghi", [P, KT, P], F32R, sparse)
        hglo = sb("hglo", [P, KT, P], F32R, sparse)
        gthi = sb("gthi", [P, FT, P], F32R, sparse)
        gtlo = sb("gtlo", [P, FT, P], F32R, sparse)
        pick = sb("pick", [P, 3, P], F32R, sparse)
        pickT = sb("pickT", [P, T], F32R, sparse)
        weight = sb("weight", [P, 1], F32, sparse)
        yshi = sb("yshi", [P, D], F32R, sparse)
        yslo = sb("yslo", [P, D], F32R, sparse)
        sgs = sb("sgs", [P, CW], F32, sparse)
        gus = sb("gus", [P, CW], F32, sparse)
        count = sb("count", [P, P], F32, sparse)
        sparse.close()
        ffn.close()
        split.close()
        raw45 = sb("raw45", [P, 2, KT * T])
        raw = [raw01[:, 0], raw01[:, 1], raw2[:, :, :]]
        whi = [whi01[:, 0], whi01[:, 1], whi2[:, :, :]]
        wlo = [wlo01[:, 0], wlo01[:, 1], wlo2[:, :, :]]
        raw6 = raw + [b[:, 0:KT * CW].rearrange("p (k c) -> p k c", k=KT)
                      for b in (hf[:, :, :].rearrange("p k t -> p (k t)"), raw45[:, 0], raw45[:, 1])]
        ctok = xdt
        sq1 = xraw[:, 0:KT * T].rearrange("p (k t) -> p k t", k=KT)
        mtok = sgb[:, :, :].rearrange("p k t -> p (k t)")[:, 0:R3 * CW].rearrange("p (s c) -> p s c", s=R3)
        modf = mod[:, :, :, :].rearrange("p l r c -> p (l r) c")
        ptok = mix[:, :, :].rearrange("p h q -> p (h q)")
        stok = xc
        xtok = xraw
        tail = ce[:, :, :].rearrange("p h q -> p (h q)")
        sring = ce[:, :, :].rearrange("p (s k) n -> p s k n", s=2)
        sprod = [b[:, :].rearrange("p (k n) -> p k n", k=KT) for b in (xw, xdt)]
        hst = mix[:, 0:KT, :]
        vtok = mix[:, :, :].rearrange("p (c g) q -> p c (g q)", c=NQ)
        wsp = hT[:, :].rearrange("p (g q) -> p g q", g=KT)
        vrow = hf[0:B, :, :].rearrange("b k t -> b (k t)")[:, 0:D]
        wT = xdt[:, :].rearrange("p (g q) -> p g q", g=KT)

        acc = ctx.enter_context(nc.psum_tensor("acc", [P, 4, 512], F32))
        ms = ctx.enter_context(nc.psum_tensor("ms", [P, 4, 512], F32))
        msf = ms[:, :, :].rearrange("p b n -> p (b n)")
        accf = acc[:, :, :].rearrange("p b n -> p (b n)")

        sem = {s: ctx.enter_context(nc.semaphore(s)) for s in SEMAPHORES}
        raw_full = [sem[f"raw_full{s}"] for s in range(R6)]
        acc_free = [sem["acc_free0"], sem["acc_free1"]]
        s_in = [sem["s_in0"], sem["s_in1"]]
        s_out = [sem["s_out0"], sem["s_out1"]]
        block = ctx.enter_context(nc.Block())

        def row(name, l, k=None):
            r0, rows = ROWS[name]
            return PT[:, l, r0:r0 + rows] if k is None else PT[:, l, r0 + k:r0 + k + 1]

        def bc(ap, axis, shape):
            return ap.unsqueeze(axis).to_broadcast(shape)

        def later(i, n):
            return not isinstance(i, int) or i >= n

        def loop(eng, count, body, peel=0):
            for i in range(peel):
                body(i)
            if count > peel:
                with eng.Fori(0, count - peel) as i:
                    body(i + peel)

        def load(sp, n, slot, dst_cols, src, nk=KT):
            sp.wait_ge(sem["lo_ready"], n - 1)
            sp.dma_start(raw[slot][:, 0:nk, 0:dst_cols], src).then_inc(raw_full[slot], 16)

        def landed(base):
            return 16 * (M6 + (base - N0["xbc", 0]) // 2 + 1)

        def load_phase(sp, key, w, col0, count):
            n0 = N0[key]
            wv = w.rearrange("(k p) m -> p k m", p=P)

            def body(i):
                for c in range(2):
                    a = sp.snap(col0 + CW * c + 2 * CW * i)
                    load(sp, n0 + c + 2 * i, (n0 + c) % 2, CW, wv[:, :, bass.ds(a, CW)])
            loop(sp, count // 2, body)

        def split_hi(act, base, i, step=2, e=0):
            slot = base % 2
            act.wait_ge(raw_full[slot], landed(base) + 8 * step * i + 8 * EN * e)
            act.wait_ge(sem["w_used"], base - 1 + step * i + EN * e)
            act.activation(whi[slot], raw[slot], ACT.Copy).then_inc(sem["hi_ready"], 1)

        def split_lo(dve, base, i, step=2, e=0):
            slot = base % 2
            dve.wait_ge(sem["hi_ready"], base + 1 + step * i + EN * e)
            dve.tensor_tensor(wlo[slot], raw[slot], whi[slot].bitcast(F32), ALU.subtract) \
                .then_inc(sem["lo_ready"], 1)

        NX = N0["gu", L - 1]
        FILLS = [M6 + sum(m % 2 == s for m in range(N0["xbc", 0], NX)) for s in range(2)] + [M6] * (R6 - 2)

        def in_ring(j, half):
            return (SN * half + j) % R6, (SN * half + j) // R6

        def split_hi3(act, j, half, pair, b=0):
            slot, turn = in_ring(j, half)
            act.wait_ge(raw_full[slot], 16 * (FILLS[slot] + turn + 1) + 16 * (2 * SN // R6) * pair + 16 * b)
            act.wait_ge(sem["w_used"], NX + j - R3 + 1 + SN * half + 2 * SN * pair + R6 * b)
            act.activation(whi[j % R3], raw6[slot], ACT.Copy).then_inc(sem["hi_ready"], 1)

        def split_lo3(dve, j, half, pair, b=0):
            slot, _ = in_ring(j, half)
            dve.wait_ge(sem["hi_ready"], NX + j + 1 + SN * half + 2 * SN * pair + R6 * b)
            dve.tensor_tensor(wlo[j % R3], raw6[slot], whi[j % R3].bitcast(F32), ALU.subtract) \
                .then_inc(sem["lo_ready"], 1)

        def by_twos(eng, expert):
            with eng.Fori(0, E // 2 - 1) as pair:
                for half in range(2):
                    expert(half, pair, False)
            for half in range(2):
                expert(half, E // 2 - 1, half == 1)

        def crowded(eng):
            eng.wait_ge(sem["flag_ready"], 1)
            return eng.value_load(flag[0:1, 0:1]) > 0

        def pairs(eng, pair):
            for q in range(2):
                pair(0, q)
            with eng.Fori(0, FP // R3) as b:
                for q in range(2, 2 + R3):
                    pair(b, q)

        def products(pe, n, slot, pair, first, last, hi, lo, cols, nk=KT, tiles=MT, ready=None):
            pe.wait_ge(sem["lo_ready"], n + 1)
            for j in range(tiles):
                out = acc[:, 2 * pair + j, 0:cols]
                for k in range(nk):
                    if ready and j == 0 and k % HT == 0:
                        pe.wait_ge(sem["xs_lo"], 2 * ready - 1 + k // HT)
                    a = whi[slot][:, k, j * P:(j + 1) * P]
                    b = wlo[slot][:, k, j * P:(j + 1) * P]
                    pe.matmul(out, a, hi(k), start=first and k == 0, stop=False)
                    pe.matmul(out, a, lo(k), start=False, stop=False)
                    ins = pe.matmul(out, b, hi(k), start=False, stop=last and k == nk - 1)
            ins.then_inc(sem["w_used"], 1)

        def pe_phase(pe, key, count, hi, lo, cols, ready=None, after=None):
            n0, q0 = N0[key], Q0[key]

            def body(i):
                for c in range(2):
                    if not (isinstance(i, int) and q0 + c + 2 * i < 2):
                        pe.wait_ge(acc_free[(q0 + c) % 2], (q0 + c) // 2 + i)
                    products(pe, n0 + c + 2 * i, (n0 + c) % 2, (q0 + c) % 2, True, True, hi, lo, cols,
                             ready=ready if isinstance(i, int) and i + c == 0 else None)
                    if after:
                        after(c + 2 * i)
            loop(pe, count // 2, body, count // 2 if after else 1 if ready else 0)

        def act_phase(act, key, count, epilogue=None, peel=0, end=False, after=None):
            n0, q0 = N0[key], Q0[key]

            def body(i):
                for c in range(2):
                    if not (end and c + 1 + 2 * i == count):
                        split_hi(act, n0 + c + 1, i)
                    if epilogue:
                        act.wait_ge(sem["w_used"], n0 + c + 1 + 2 * i)
                        pair = (q0 + c) % 2
                        epilogue(i, c, acc[:, 2 * pair:2 * pair + 2, 0:T]).then_inc(acc_free[pair], 1)
                    if after:
                        after(c + 2 * i)
            loop(act, count // 2, body, count // 2 if end or after else peel)

        def dve_phase(dve, key, count, epilogue=None, peel=0, cols=T, end=False, after=None):
            n0, q0 = N0[key], Q0[key]

            def body(i):
                for c in range(2):
                    if not (end and c + 1 + 2 * i == count):
                        split_lo(dve, n0 + c + 1, i)
                    if epilogue:
                        dve.wait_ge(sem["w_used"], n0 + c + 1 + 2 * i)
                        pair = (q0 + c) % 2
                        epilogue(i, c, acc[:, 2 * pair:2 * pair + 2, 0:cols]).then_inc(acc_free[pair], 1)
                    if after:
                        after(c + 2 * i)
            loop(dve, count // 2, body, count // 2 if end or after else peel)

        def xs(part):
            return lambda k: part[:, k, :]

        HT = KT // 2
        HALVES = (slice(0, HT), slice(HT, KT))

        def squares(v):
            l, k = divmod(v - 1, 4)
            return (2 * 3 + KT // MT) * l + (0, 2, 2 + KT // MT, 4 + KT // MT)[k]

        def folds(v):
            return 2 * (v - 3 - (v - 3) // 4)

        SR = B * (CK - 1)
        TURNS = [("params", 0, 0)] + [("state", l, 0) for l in range(L)] \
            + [("x", c, h) for c in range(NQ) for h in range(2)] + [("x", NQ, 0)]
        TURNS_AFTER = {3: range(0, 3), 4: range(3, 6), 5: range(6, 8)}
        MOD_PEEL = 8
        assert len(TURNS) == 8

        def turn_bank(p):
            return acc[:, 3, :] if p % 2 else ms[:, 3, :]

        @block.sync
        def _(sp):
            sp.wait_ge(sem["ctok_zero"], 1)
            sp.dma_start(ctok[0:1, :], A["c_prompt"]).then_inc(sem["c_in"], 16)
            sp.dma_start(ctok[1:1 + B, :], A["c_sample"]).then_inc(sem["c_in"], 16)
            per = 6 * KT // MT
            for l in range(L):
                wv = A["w_mod"][l].rearrange("(k p) m -> p k m", p=P)

                def body(i):
                    for c in range(R6):
                        a = sp.snap(R6 * CW * i + CW * c)
                        if not (isinstance(i, int) and l == 0):
                            sp.wait_ge(sem["lo_ready"], l * per + c - R6 + 1 + R6 * i)
                        sp.dma_start(raw6[c], wv[:, :, bass.ds(a, CW)]).then_inc(raw_full[c], 16)
                loop(sp, per // R6, body, 1 if l == 0 else 0)
            for l in range(L):
                load_phase(sp, ("xbc", l), A["w_in"][l], IN_COL["xbc"], IN_CHUNKS["xbc"])
                n = N0["dt", l]
                load(sp, n, n % 2, H, A["w_in"][l].rearrange("(k p) m -> p k m", p=P)[:, :, D + CD:D + CD + H])
                for name in ("v", "u", "z", "ga", "gb"):
                    load_phase(sp, (name, l), A["w_in"][l], IN_COL[name], IN_CHUNKS[name])
                for name, w in (("cmlp_out", A["w_cmlp_out"]), ("ssd_out", A["w_ssd_out"]), ("w_o", A["w_o"])):
                    load_phase(sp, (name, l), w[l], 0, KT // MT)

                def expert(e, wg, wu, wd):
                    n0 = N0["gu", l]
                    gv, uv = (w.rearrange("(k p) m -> p k m", p=P) for w in (wg, wu))
                    dv = wd.rearrange("(k p) m -> p k m", p=P)

                    def gates(i):
                        a = sp.snap(CW * i)
                        for c, w in enumerate((gv, uv)):
                            load(sp, n0 + c + 2 * i + EN * e, (n0 + c) % 2, CW, w[:, :, bass.ds(a, CW)])
                    with sp.Fori(0, FT // MT) as i:
                        gates(i)
                    n1 = N0["wd", l]

                    def downs(i):
                        for g in range(2):
                            a = sp.snap(2 * CW * i + g * CW)
                            for s, (k0, nk) in enumerate(KG):
                                c = g * len(KG) + s
                                load(sp, n1 + c + 2 * len(KG) * i + EN * e, (n1 + c) % 2, CW,
                                     dv[:, k0:k0 + nk, bass.ds(a, CW)], nk)
                    with sp.Fori(0, KT // MT // 2) as i:
                        downs(i)

                if l % 2 == 0:
                    expert(0, A["ffn_wg"][l // 2], A["ffn_wu"][l // 2], A["ffn_wd"][l // 2])
                    continue
                with sp.If(crowded(sp)):
                    with sp.Fori(0, E) as e:
                        expert(e, A["exp_wg"][l // 2, e], A["exp_wu"][l // 2, e], A["exp_wd"][l // 2, e])
                with sp.Else():
                    def fetch_expert(half, two, last):
                        e = sp.snap(2 * two + half)
                        gv, uv = (w[l // 2, e].rearrange("(k p) m -> p k m", p=P) for w in (A["exp_wg"], A["exp_wu"]))
                        dv = A["exp_wd"][l // 2, e].rearrange("(d k p) m -> d p k m", k=DK, p=P)

                        def fetch(j, b, src, shape=lambda raw: raw):
                            slot, turn = in_ring(j, half)
                            if turn == 0 and slot == R3:
                                sp.wait_ge(sem["h_turned"], 3)
                            sp.wait_ge(sem["lo_ready"], NX + j - R6 + 1 + SN * half + 2 * SN * two + R6 * b)
                            sp.dma_start(shape(raw6[slot]), src).then_inc(raw_full[slot], 16)

                        def pair(b, q):
                            a = sp.snap(CW * R3 * b + CW * q)
                            for c, w in enumerate((gv, uv)):
                                fetch(2 * q + c, b, w[:, :, bass.ds(a, CW)])
                        pairs(sp, pair)
                        for d in range(FD):
                            fetch(2 * FP + d, 0, dv[d], lambda raw: raw.rearrange("p k c -> p (k c)").rearrange(
                                "p (k m) -> p k m", k=DK))
                    by_twos(sp, fetch_expert)

        @block.gpsimd
        def _(pool):
            pool.memset(ident[:, :], 0.0).then_inc(sem["ident_zero"], 1)
            pool.memset(tri[:, :], 1.0).then_inc(sem["ident_zero"], 1)
            pool.memset(spread[:, :], 1.0).then_inc(sem["ident_zero"], 1)
            pool.memset(earlier[:, :, :], 1.0).then_inc(sem["ident_zero"], 1)
            pool.memset(fold[:, :], 0.0).then_inc(sem["ident_zero"], 1)
            pool.wait_ge(sem["ident_zero"], 5)
            pool.affine_select(out=ident[:, :], in_=ident[:, :], compare_op=ALU.not_equal, fill=1.0, base=0,
                               pattern=[[-1, P]], channel_multiplier=1).then_inc(sem["consts"], 1)
            pool.affine_select(out=tri[:, :], in_=tri[:, :], compare_op=ALU.is_ge, fill=0.0, base=0,
                               pattern=[[1, P]], channel_multiplier=-1).then_inc(sem["consts"], 1)
            pool.affine_select(out=spread[:, :], in_=spread[:, :], compare_op=ALU.is_ge, fill=0.0, base=0,
                               pattern=[[1, D]], channel_multiplier=-HD).then_inc(sem["consts"], 1)
            pool.wait_ge(sem["consts"], 3)
            pool.affine_select(out=spread[:, :], in_=spread[:, :], compare_op=ALU.is_ge, fill=0.0, base=HD - 1,
                               pattern=[[-1, D]], channel_multiplier=HD).then_inc(sem["consts"], 1)
            pool.affine_select(out=earlier[:, :, :], in_=earlier[:, :, :], compare_op=ALU.is_gt, fill=0.0, base=0,
                               pattern=[[1, E], [-1, E]], channel_multiplier=0).then_inc(sem["consts"], 1)
            pool.wait_ge(sem["consts"], 5)
            pool.tensor_copy(fold[0:NC, :], ident[0:NC, 0:NC]).then_inc(sem["consts"], 1)
            pool.tensor_copy(fold[CL:CL + NC, :], ident[CL:CL + NC, CL:CL + NC]).then_inc(sem["consts"], 1)
            for l in range(L):
                for name, (r0, rows) in ROWS.items():
                    src = (A["conv_w"][l].rearrange("k (c p) -> (k c) p", p=P) if name == "conv_w"
                           else A["vectors"][name][l].rearrange("(c p) -> c p", p=P))
                    c0 = (l * RT + r0 // P) * P
                    pool.dma_start(ptok[r0 % P:r0 % P + rows, c0:c0 + P], src).then_inc(sem["params_in"], 16)
            for l in range(L):
                pool.dma_start(stok[0:B * (CK - 1), l * CD:(l + 1) * CD],
                               A["state_conv"][l].rearrange("b k c -> (b k) c")).then_inc(sem["states_in"], 16)
            for c in range(NQ):
                pool.dma_start(xtok[:, c * D:(c + 1) * D], A["x_prompt"][0, c * Q:(c + 1) * Q, :]).then_inc(sem["x_in"], 16)
            pool.dma_start(xtok[0:B, NQ * D:(NQ + 1) * D], A["x_sample"][:, 0, :]).then_inc(sem["x_in"], 16)
            for k, v in enumerate((A["dt_bias"], A["a_log"], A["d_skip"])):
                pool.dma_start(headp[:, k, :], v.rearrange("l h -> h l"), allow_slow_non_contiguous=True).then_inc(sem["sp_in"], 16)
            pool.dma_start(spb[:, :, :], A["b_spatial"].rearrange("l g q -> g l q")).then_inc(sem["sp_in"], 16)
            for l in range(L):
                pool.dma_start(w00[:, l:l + 1], A["w_spatial"][l, :, 0, 0:1], allow_slow_non_contiguous=True).then_inc(sem["sp_in"], 16)
            pool.dma_start(rw[:, :, :], A["router_w"][0].rearrange("(k p) e -> p k e", p=P)).then_inc(sem["route_in"], 16)
            pool.dma_start(rb[:, :], A["router_b"]).then_inc(sem["route_in"], 16)
            pool.dma_start(O["conv_s"][:, :, 0:CK - 2, :], A["state_conv"][:, :, 1:CK - 1, :]).then_inc(sem["conv_keep"], 16)

            for l in range(L):
                pool.wait_ge(sem["tail_ready"], l + 1)
                pool.dma_start(O["conv_p"][l, 0], tail[0:CK - 1, 0:CD]).then_inc(sem["tail_out"], 16)
                pool.dma_start(O["conv_s"][l, :, CK - 2, :], tail[CK - 1:CK - 1 + B, 0:CD]).then_inc(sem["tail_out"], 16)
                pool.dma_start(wsp, A["w_spatial"][l].rearrange("g t s -> t g s")).then_inc(sem["w_sp_in"], 16)
                state = A["state_ssm"][l].rearrange("b (k j) p n -> b (j p) k n", j=2)
                new = O["ssm_s"][l].rearrange("b (k j) p n -> b (j p) k n", j=2)
                pool.wait_ge(sem["tail_out"], 32 * (l + 1))
                for b in range(B):
                    s = b % 2
                    if b >= 2:
                        pool.wait_ge(s_out[s], 16 * (l * B // 2 + b // 2))
                        pool.wait_ge(sem["samp_used"], l * B + b - 1)
                    pool.dma_start(sring[:, s], state[b]).then_inc(s_in[s], 16)
                    if b >= 1:
                        pool.wait_ge(sem["s_new"], l * B + b)
                        pool.dma_start(new[b - 1], sring[:, 1 - s]).then_inc(s_out[1 - s], 16)
                pool.wait_ge(sem["s_new"], (l + 1) * B)
                pool.dma_start(new[B - 1], sring[:, (B - 1) % 2]).then_inc(s_out[(B - 1) % 2], 16)
                pool.wait_ge(sem["vs_copied"], l + 1)
                pool.dma_start(O["v_s"][l, :, 0, :], vrow).then_inc(sem["vs_out"], 16)
                pool.wait_ge(sem["st_copied"], l + 1)
                pool.dma_start(O["ssm_p"][l, 0].rearrange("(k j) p n -> (j p) k n", j=2), hst).then_inc(sem["st_out"], 16)
                pool.wait_ge(sem["merged"], 2 * (l + 1))
                pool.memset(facc[:, :, :], 0.0).then_inc(sem["facc_zero"], 1)
            pool.wait_ge(sem["y_copied"], 3)
            for c in range(NQ):
                pool.dma_start(O["y_p"][0, c * Q:(c + 1) * Q, :], xtok[:, c * D:(c + 1) * D]).then_inc(sem["y_out"], 16)
            pool.dma_start(O["y_s"][:, 0, :], xtok[0:B, NQ * D:(NQ + 1) * D]).then_inc(sem["y_out"], 16)
            pool.wait_ge(sem["y_out"], 16 * (NQ + 1))
            pool.wait_ge(sem["conv_keep"], 16)
            pool.wait_ge(sem["tail_out"], 32 * L)
            pool.wait_ge(sem["st_out"], 16 * L)
            for s in range(2):
                pool.wait_ge(s_out[s], 8 * L * B)
            pool.wait_ge(sem["vs_out"], 16 * L)

        @block.tensor
        def _(pe):
            def sum_tiles(src, out, k0=0, k1=KT, first=0, last=KT):
                for k in range(k0, k1):
                    ins = pe.matmul(out, ones[:, :], src[:, k, :], start=k == first, stop=k == last - 1)
                return ins

            def norm(v):
                for c in range(2):
                    if v == 1:
                        pe.wait_ge(sem["sq_ready"], squares(v) + c + 1)
                        ins = sum_tiles(sq1, ms[:, 3, 0:T], HT * c, HT * (c + 1))
                    else:
                        pe.wait_ge(sem["sq_folded"], folds(v) + c + 1)
                        ins = sum_tiles(hf, ms[:, 0, 0:T], HT * c, HT * c + HT // 2, last=HT + HT // 2)
                ins.then_inc(sem["ssq_ready"], 1)

            pe.wait_ge(sem["consts"], 7)
            pe.wait_ge(sem["c_silu"], 1)
            for k in range(KT):
                ins = pe.transpose(ms[:, 0, NC * k:NC * (k + 1)], ctok[0:NC, k * P:(k + 1) * P], ident[0:NC, 0:NC])
            ins.then_inc(sem["c_turned"], 1)

            def turn(p):
                what, c, h = TURNS[p]
                bank = turn_bank(p)
                if p >= 2:
                    pe.wait_ge(sem["aux_copied"], p - 1)
                if what == "params":
                    pe.wait_ge(sem["params_in"], 16 * L * len(ROWS))
                    for l in range(L):
                        for r in range(RT):
                            rows = min(P, NROW - r * P)
                            c0 = (l * RT + r) * P
                            ins = pe.transpose(bank[:, l * NROW + r * P:l * NROW + r * P + rows],
                                               ptok[0:rows, c0:c0 + P], ident[0:rows, 0:rows])
                elif what == "state":
                    pe.wait_ge(sem["states_in"], 16 * L)
                    for k in range(CT):
                        ins = pe.transpose(bank[:, k * SR:(k + 1) * SR], stok[0:SR, c * CD + k * P:c * CD + (k + 1) * P],
                                           ident[0:SR, 0:SR])
                else:
                    pe.wait_ge(sem["x_in"], 16 * (NQ + 1))
                    rows = Q if c < NQ else B
                    for k in range(4 if c < NQ else KT):
                        f0 = c * D + (4 * h + k) * P
                        ins = pe.transpose(bank[:, k * rows:(k + 1) * rows], xtok[0:rows, f0:f0 + P],
                                           ident[0:rows, 0:rows])
                ins.then_inc(sem["aux_turned"], 1)

            def fold_chunk(m, c):
                pe.wait_ge(sem["mt_ready"], m + 1)
                if not isinstance(m, int) or m >= R3:
                    pe.wait_ge(sem["mod_added"], m - 2)
                for j in range(MT):
                    ins = pe.matmul(ms[:, c, j * NC:(j + 1) * NC], mtok[0:CL + NC, c, j * P:(j + 1) * P], fold[:, :],
                                    start=True, stop=True)
                ins.then_inc(sem["folded"], 1)

            def mod_body(i):
                for c in range(R3):
                    pe.wait_ge(sem["lo_ready"], c + 1 + R3 * i)
                    if later(i, 1):
                        pe.wait_ge(sem["mt_ready"], c - 2 + R3 * i)
                    for k in range(KT):
                        pe.matmul(acc[:, c, 0:CW], cst[:, k, :], whi[c][:, k, :], start=k == 0, stop=False)
                        ins = pe.matmul(acc[:, c, 0:CW], cst[:, k, :], wlo[c][:, k, :], start=False, stop=k == KT - 1)
                    ins.then_inc(sem["w_used"], 1)
                    if later(i, 1) or c >= 2:
                        fold_chunk(R3 * i + c - 2, (c - 2) % R3)
            pe.wait_ge(sem["c_lo"], 1)
            for i in range(MOD_PEEL):
                mod_body(i)
                for p in TURNS_AFTER.get(i, ()):
                    turn(p)
                if i == 6:
                    norm(1)
            with pe.Fori(0, N0["xbc", 0] // R3 - MOD_PEEL) as i:
                mod_body(i + MOD_PEEL)
            for m in (N0["xbc", 0] - 2, N0["xbc", 0] - 1):
                fold_chunk(m, m % R3)
            pe.wait_ge(sem["mod_added"], N0["xbc", 0])

            for l in range(L):
                if l:
                    norm(4 * l + 1)
                pe_phase(pe, ("xbc", l), IN_CHUNKS["xbc"], xs(xhi), xs(xlo), T, ready=5 * l + 1)
                n, q = N0["dt", l], Q0["dt", l]
                pe.wait_ge(acc_free[q % 2], q // 2)
                products(pe, n, n % 2, q % 2, True, True, xs(xhi), xs(xlo), T, tiles=1)
                pe_phase(pe, ("v", l), IN_CHUNKS["v"], xs(xhi), xs(xlo), T)
                for k in range(CT):
                    ins = pe.transpose(ms[0:CK - 1 + B, k // 4, (k % 4) * P:(k % 4 + 1) * P],
                                       xrawv[:, k, S:S + CK - 1 + B], ident[:, :])
                ins.then_inc(sem["tail_turned"], 1)
                pe_phase(pe, ("u", l), IN_CHUNKS["u"], xs(xhi), xs(xlo), T)
                pe.wait_ge(sem["tail_ready"], l + 1)
                sum_tiles(vb, ms[:, 0, 0:T]).then_inc(sem["v_sum"], 1)
                pe.wait_ge(sem["samp_decay"], l + 1)
                for k in range(KT):
                    ins = pe.matmul(ms[:, 3, k * (2 * B + 1):(k + 1) * (2 * B + 1)], spread[:, k * P:(k + 1) * P],
                                    spin[:, :], start=True, stop=True)
                ins.then_inc(sem["spread_ready"], 1)
                pe_phase(pe, ("z", l), IN_CHUNKS["z"], xs(xhi), xs(xlo), T)

                def sample_rows(b):
                    if b == 1:
                        pe.wait_ge(sem["v_inv"], l + 1)
                    if b >= 2:
                        pe.wait_ge(sem["samp_used"], l * B + b - 1)
                    for bank, g0 in ((b % 2, 0), (2 + b % 2, G * P)):
                        ins = pe.matmul(ms[:, bank, 0:G * P], ident[0:B, b:b + 1].to_broadcast([B, P]),
                                        bct[:, g0:g0 + G * P], start=True, stop=True)
                    ins.then_inc(sem["bc_spread"], 1)

                def after_ga(c):
                    if c == 0:
                        pe.wait_ge(sem["xc_ready"], l + 1)
                        for k in range(2 * G):
                            ins = pe.transpose(ms[0:B, 2, k * P:(k + 1) * P], xcv[:, KT + k, S:T], ident[:, :])
                        ins.then_inc(sem["bc_turned"], 1)
                        pe.wait_ge(sem["bc_ready"], l + 1)
                        pe.wait_ge(sem["spread_copied"], l + 1)
                        sample_rows(0)
                    sample_rows(c + 1)

                def after_gb(c):
                    if B // 2 + c + 1 < B:
                        sample_rows(B // 2 + c + 1)
                pe.wait_ge(sem["v_sq"], l + 1)
                sum_tiles(hf, ms[:, 1, 0:T]).then_inc(sem["v_ssq"], 1)
                pe_phase(pe, ("ga", l), IN_CHUNKS["ga"], xs(xhi), xs(xlo), T, after=after_ga)
                pe_phase(pe, ("gb", l), IN_CHUNKS["gb"], xs(xhi), xs(xlo), T, after=after_gb)

                pe.wait_ge(sem["v_normed"], l + 1)
                pe.wait_ge(sem["outer_ready"], (l + 1) * B)
                for k in range(KT):
                    ins = pe.transpose(ms[0:B, k // 4, (k % 4) * P:(k % 4 + 1) * P], vb[:, k, S:T], ident[:, :])
                ins.then_inc(sem["vs_turned"], 1)
                pe.wait_ge(sem["vs_copied"], l + 1)
                for c in range(NQ):
                    if c:
                        pe.wait_ge(sem["w_sp_in"], 16 * (l + 1))
                        pe.wait_ge(sem["samp_used"], (l + 1) * B)
                        for k in range(KT):
                            ins = pe.transpose(ms[:, 2 + k // 4, (k % 4) * P:(k % 4 + 1) * P], wsp[:, k, :], ident[:, :])
                        ins.then_inc(sem["w_turned"], 1)
                        pe.wait_ge(sem["v_tok_ready"], l * NQ + c)
                    for k in range(KT):
                        ins = pe.transpose(ms[:, k // 4, (k % 4) * P:(k % 4 + 1) * P], vb[:, k, c * Q:(c + 1) * Q],
                                           ident[:, :])
                    ins.then_inc(sem["v_tok"], 1)
                pe.wait_ge(sem["diag_ready"], l + 1)
                pe.wait_ge(sem["v_tok_ready"], (l + 1) * NQ)
                pe.wait_ge(sem["w_ready"], l + 1)
                pe.matmul(ms[:, 0, 0:2 * KT], ones[0:KT, :], diag[:, :, :].rearrange("g a b -> g (a b)"), start=True,
                          stop=True).then_inc(sem["sp_bcast"], 1)
                pe.wait_ge(sem["sp_bcast_ready"], l + 1)
                for c in range(NQ):
                    for k in range(KT):
                        out = ms[:, 2 * c + k // 4, (k % 4) * Q:(k % 4 + 1) * Q]
                        pe.matmul(out, vtok[:, c, k * P:(k + 1) * P], wT[:, k, :], start=True, stop=False)
                        ins = pe.matmul(out, ident[0:KT, k:k + 1].to_broadcast([KT, P]), spb[:, l, :], start=False,
                                        stop=True)
                    ins.then_inc(sem["sp_out"], 1)
                def cmlp_chunk(c):
                    n, q = N0["cmlp_out", l] + c, Q0["cmlp_out", l] + c
                    pe.wait_ge(acc_free[q % 2], q // 2)
                    products(pe, n, n % 2, q % 2, True, True, xs(xhi), xs(xlo), T, ready=None if c else 5 * l + 2)

                pe.wait_ge(sem["sp_taken"], l + 1)
                for c in range(NQ):
                    v = l * NQ + c
                    toks = slice(c * Q, (c + 1) * Q)
                    if c:
                        pe.wait_ge(sem["y_taken"], v)
                        pe.wait_ge(sem["st_ready"], v)
                    for k in range(KT):
                        ins = pe.transpose(ms[:, k // 4, (k % 4) * P:(k % 4 + 1) * P], xcv[:, k, toks], ident[:, :])
                    ins.then_inc(sem["x_tok"], 1)
                    for g in range(G):
                        pe.transpose(ms[:, 2, g * P:(g + 1) * P], xcv[:, KT + g, toks], ident[:, :])
                    pe.transpose(ms[:, 2, 2 * P:2 * P + H], dth[:, 0, toks], ident[0:H, 0:H])
                    pe.transpose(ms[:, 2, 2 * P + H:2 * P + 2 * H], dth[:, 1, toks], ident[0:H, 0:H]) \
                        .then_inc(sem["b_tok"], 1)
                    for g in range(G):
                        ins = pe.matmul(ms[:, 3, g * Q:(g + 1) * Q], xcv[:, KT + g, toks], xcv[:, KT + G + g, toks],
                                        start=True, stop=True)
                    ins.then_inc(sem["cb_ready"], 1)
                    cmlp_chunk(2 * c)
                    pe.wait_ge(sem["xdt_ready"], v + 1)
                    pe.wait_ge(sem["bt_ready"], v + 1)
                    pe.wait_ge(sem["tok_ready"], v + 1)
                    pe.wait_ge(sem["cbm_ready"], v + 1)
                    for h in range(H):
                        ins = pe.matmul(ms[:, h // 4, (h % 4) * Q:(h % 4 + 1) * Q], ident[0:H, h:h + 1].to_broadcast([H, P]),
                                        dth[:, 0, toks], start=True, stop=True)
                    ins.then_inc(sem["cumb_ready"], 1)
                    cmlp_chunk(2 * c + 1)
                    pe.wait_ge(sem["mix_ready"], v + 1)
                    pe.wait_ge(sem["wend_ready"], v + 1)
                    if c:
                        pe.wait_ge(sem["ce_ready"], l + 1)
                    for h in range(H):
                        out = ms[(h % 2) * HD:(h % 2 + 1) * HD, h // 8, (h // 2 % 4) * Q:(h // 2 % 4 + 1) * Q]
                        ins = pe.matmul(out, xdt[:, h * HD:(h + 1) * HD], mix[:, h, :], start=True, stop=c == 0)
                        if c:
                            ins = pe.matmul(out, hT[:, h * HD:(h + 1) * HD], ce[:, h, :], start=False, stop=True)
                    ins.then_inc(sem["y_part"], 1)
                    pe.wait_ge(sem["xw_ready"], v + 1)
                    for g in range(G):
                        ins = pe.matmul(ms[:, 2 + g, :], bt[:, g, :], xw[:, g * 512:(g + 1) * 512], start=True, stop=True)
                    ins.then_inc(sem["st_part"], 1)
                for g in range(G):
                    pe.wait_ge(sem["gate_folded"], G * l + g + 1)
                    sum_tiles(zs, ms[:, g, 0:T], HT * g, HT * g + HT // 2, HT * g, HT * g + HT // 2) \
                        .then_inc(sem["gate_ssq"], 1)
                pe.wait_ge(sem["st_ready"], (l + 1) * NQ)
                for k in range(KT):
                    ins = pe.transpose(ms[:, 2 + k // 4, (k % 4) * P:(k % 4 + 1) * P], hT[:, k * P:(k + 1) * P],
                                       ident[:, :])
                ins.then_inc(sem["st_turned"], 1)
                pe_phase(pe, ("ssd_out", l), KT // MT, xs(xhi), xs(xlo), T, ready=5 * l + 3)


                def add_squares(c):
                    pe.wait_ge(sem["sq_ready"], squares(4 * l + 2) + c + 1)
                    return sum_tiles(hf, ms[:, 0, 0:T], MT * c, MT * (c + 1))
                pe_phase(pe, ("w_o", l), KT // MT, xs(xhi), xs(xlo), T, ready=5 * l + 4,
                         after=lambda c: add_squares(c - 1) if c else None)
                add_squares(KT // MT - 1).then_inc(sem["ssq_ready"], 1)
                norm(4 * l + 3)

                if l % 2:
                    for half, ks in enumerate(HALVES):
                        pe.wait_ge(sem["h_ready"], 2 * (2 * l + 2) - 1 + half)
                        for c in range(3):
                            rows = Q if c < NQ else B
                            for k in range(KT)[ks]:
                                pe.matmul(ms[0:rows, 1 + c, 0:E], hf[:, k, c * Q:c * Q + rows], rw[:, k, :],
                                          start=k == 0, stop=False)
                    for c in range(3):
                        rows = Q if c < NQ else B
                        ins = pe.matmul(ms[0:rows, 1 + c, 0:E], ones[0:1, 0:rows], rb[:, :], start=False, stop=True)
                    ins.then_inc(sem["logits_ready"], 1)

                    def turn_h(c):
                        rows = Q if c < NQ else B
                        for k in range(KT):
                            ins = pe.transpose(acc[0:rows, 2 * (c % 2) + k // 4, (k % 4) * P:(k % 4 + 1) * P],
                                               hf[:, k, c * Q:c * Q + rows], ident[:, :])
                        ins.then_inc(sem["h_turned"], 1)
                    turn_h(0)
                    turn_h(1)
                    pe.wait_ge(sem["sel_ready"], 1)
                    for c in range(4):
                        for d in range(min(c, 2) + 1):
                            ins = pe.matmul(ms[:, 3, c * E:(c + 1) * E], tri[:, :] if d == c else ones[:, :],
                                            sel[:, d, :], start=d == 0, stop=d == min(c, 2))
                    ins.then_inc(sem["counted"], 1)
                    pe.wait_ge(sem["htok_lo"], 1)
                    turn_h(2)
                    pe.wait_ge(sem["xs_lo"], 2 * (5 * l + 5))
                    pe.wait_ge(sem["htok_lo"], 3)

                def all_tokens(pe, expert):
                    pe.wait_ge(sem["route_done"], 1)
                    for c in range(3):
                        rows = Q if c < NQ else B
                        ins = pe.transpose(ms[0:E, 2, c * Q:c * Q + rows], rank[0:rows, c, :], ident[0:rows, 0:rows])
                    ins.then_inc(sem["combine_turned"], 1)
                    pe.wait_ge(sem["combine_ready"], 1)
                    for e in range(E):
                        if e >= 4:
                            pe.wait_ge(sem["combine_spread_ready"], e - 3)
                        pe.matmul(ms[:, e % 4, 0:T], ident[0:E, e:e + 1].to_broadcast([E, P]), comb[:, :], start=True,
                                  stop=True).then_inc(sem["combine_spread"], 1)
                    with pe.Fori(0, E) as e:
                        expert(e)

                def expert(e):
                    n0, q0 = N0["gu", l], Q0["gu", l]

                    def gates(i):
                        for c in range(2):
                            pe.wait_ge(acc_free[(q0 + c) % 2], (q0 + c) // 2 + i + EQ // 2 * e)
                            products(pe, n0 + c + 2 * i + EN * e, (n0 + c) % 2, (q0 + c) % 2, True, True, xs(xhi),
                                     xs(xlo), T, ready=5 if l == 0 and isinstance(i, int) and c == 0 else None)
                    loop(pe, FT // MT, gates, 1 if l == 0 else 0)
                    n1, q1 = N0["wd", l], Q0["wd", l]

                    def downs(i):
                        for g in range(2):
                            pair = (q1 + g) % 2
                            pe.wait_ge(acc_free[pair], (q1 + g) // 2 + i + EQ // 2 * e)
                            for s, (k0, nk) in enumerate(KG):
                                pe.wait_ge(acc_free[(q0 + 1) % 2], (q0 + 1) // 2 + (k0 + nk) // MT + EQ // 2 * e)
                                c = g * len(KG) + s
                                products(pe, n1 + c + 2 * len(KG) * i + EN * e, (n1 + c) % 2, pair, s == 0,
                                         s == len(KG) - 1, lambda k, k0=k0: ghi[:, k0 + k, :],
                                         lambda k, k0=k0: glo[:, k0 + k, :], T, nk)
                    with pe.Fori(0, KT // MT // 2) as i:
                        downs(i)

                if l % 2 == 0:
                    expert(0)
                    norm(4 * l + 4)
                    continue
                with pe.If(crowded(pe)):
                    all_tokens(pe, expert)
                with pe.Else():
                    def gather(e, part, k0, k1):
                        if part == 0 and k0 == 0:
                            pe.wait_ge(sem["g_built"], 1 + e)
                            pe.wait_ge(sem["gt_lo"], R3 + FP * e)
                        for k in range(k0, k1):
                            for c in range(3):
                                rows = Q if c < NQ else B
                                ins = pe.matmul(ms[:, 2 * part + k // 4, (k % 4) * P:(k % 4 + 1) * P],
                                                (htokhi, htoklo)[part][0:rows, c, k * P:(k + 1) * P],
                                                pick[0:rows, c, :], start=c == 0, stop=c == 2)
                        if k1 == KT:
                            ins.then_inc(sem[("gathered_hi", "gathered_lo")[part]], 1)

                    for part in range(2):
                        gather(0, part, 0, KT)

                    def turn(b, q, e):
                        pe.wait_ge(sem["gu_done"], R3 + 1 + q + R3 * b + FP * e)
                        pe.wait_ge(sem["gt_lo"], 1 + q + R3 * b + FP * e)
                        for k in range(MT):
                            ins = pe.transpose(ms[:, q % R3, k * P:(k + 1) * P], gus[:, k * P:(k + 1) * P], ident[:, :])
                        ins.then_inc(sem["gu_turned"], 1)

                    def picked(half, two, last):
                        e = 2 * two + half

                        def pair(b, q):
                            peeled = isinstance(b, int)
                            for c in range(2):
                                if c == 0:
                                    pe.wait_ge(sem["gu_done"], 1 + q + R3 * b + FP * e)
                                    if peeled:
                                        pe.wait_ge(sem["scat_added"], 1 + 4 * e)
                                    elif q == 2:
                                        pe.wait_ge(sem["scat_added"], 2 + 4 * e)
                                s = (2 * q + c) % R3
                                pe.wait_ge(sem["lo_ready"], NX + 2 * q + c + 1 + 2 * R3 * b + SN * e)
                                out = acc[:, q % R3, c * CW:(c + 1) * CW]
                                for k in range(KT):
                                    pe.matmul(out, hghi[:, k, :], whi[s][:, k, :], start=k == 0, stop=False)
                                    pe.matmul(out, hghi[:, k, :], wlo[s][:, k, :], start=False, stop=False)
                                    ins = pe.matmul(out, hglo[:, k, :], whi[s][:, k, :], start=False, stop=k == KT - 1)
                                ins.then_inc(sem["w_used"], 1)
                                if c == 0 and not (peeled and q == 0):
                                    turn(b, q - 1, e)
                            if peeled and q == 1:
                                pe.wait_ge(sem["scat_added"], 2 + 4 * e)
                                for c in range(3):
                                    rows = Q if c < NQ else B
                                    pe.transpose(acc[:, 3, c * Q:c * Q + rows], pick[0:rows, c, :].bitcast(F32),
                                                 ident[0:rows, 0:rows])
                                for c in range(3):
                                    rows = Q if c < NQ else B
                                    ins = pe.matmul(acc[:, 3, T:T + 1], pick[0:rows, c, :].bitcast(F32),
                                                    rank[0:rows, c, bass.ds(e, 1)], start=c == 0, stop=c == 2)
                                ins.then_inc(sem["gw_turned"], 1)
                        pe.wait_ge(sem["hg_hi"], 1 + e)
                        pe.wait_ge(sem["hg_lo"], 1 + e)
                        pairs(pe, pair)
                        pe.wait_ge(sem["gw_ready"], 1 + e)
                        for d in range(FD):
                            s = (2 * FP + d) % R3
                            wh, wl = (w[s].rearrange("p k c -> p (k c)") for w in (whi, wlo))
                            pe.wait_ge(sem["lo_ready"], NX + 2 * FP + d + 1 + SN * e)
                            pe.wait_ge(sem["gt_lo"], R3 + 1 + d + FP * e)
                            for k in range(DK):
                                for half in range(2):
                                    cols = slice(k * D + half * 512, k * D + half * 512 + 512)
                                    out = acc[:, 2 + half, :]
                                    hi, lo = gthi[:, DK * d + k, :], gtlo[:, DK * d + k, :]
                                    pe.matmul(out, hi, wh[:, cols], start=d == 0 and k == 0, stop=False)
                                    pe.matmul(out, hi, wl[:, cols], start=False, stop=False)
                                    ins = pe.matmul(out, lo, wh[:, cols], start=False, stop=d == FD - 1 and k == DK - 1)
                            ins.then_inc(sem["w_used"], 1)
                            if d == 0:
                                turn(0, FP - 1, e)
                            if not last and 4 <= d < 8:
                                gather(e + 1, 0, 2 * (d - 4), 2 * (d - 3))
                        if not last:
                            gather(e + 1, 1, 0, KT)
                        pe.wait_ge(sem["ys_ready"], 1 + e)
                        for k in range(KT):
                            if k == 4 or k == 6:
                                pe.wait_ge(sem["scat_added"], 4 * e + 3 + (k - 4) // 2)
                            for y in (yshi, yslo):
                                ins = pe.matmul(acc[:, k % 4, 0:T], y[:, k * P:(k + 1) * P], pickT[:, :],
                                                start=y is yshi, stop=y is yslo)
                            if k % 2:
                                ins.then_inc(sem["scattered"], 1)
                    by_twos(pe, picked)
                norm(4 * l + 4)

            pe.wait_ge(sem["x_ready"], 4 * L)
            for c in range(NQ + 1):
                rows = Q if c < NQ else B
                if c >= 2:
                    pe.wait_ge(sem["y_copied"], c - 1)
                for k in range(KT):
                    ins = pe.transpose(ms[0:rows, 2 * (c % 2) + k // 4, (k % 4) * P:(k % 4 + 1) * P],
                                       x[:, k, c * Q:c * Q + rows], ident[:, :])
                ins.then_inc(sem["y_turned"], 1)

        @block.scalar
        def _(act):
            def norm_sq(v, src):
                for c, ks in enumerate(HALVES):
                    if src is x and v > 1:
                        act.wait_ge(sem["x_ready"], 2 * (v // 2 - 1) + c + 1)
                    act.activation((sq1 if v == 1 else hf)[:, ks, :], src[:, ks, :], ACT.Square) \
                        .then_inc(sem["sq_ready"], 1)

            def norm_rs(v):
                act.wait_ge(sem["ssq_ready"], v)
                act.activation(rs[:, 0, :], ms[:, 3 if v == 1 else 0, 0:T], ACT.Sqrt, bias=eps[:, 0:1],
                               scale=1.0 / D).then_inc(sem["root_ready"], 1)

            def hi_of_x(v, src, ready=None, count=0):
                for c, ks in enumerate(HALVES):
                    if ready:
                        act.wait_ge(ready, 2 * count - 1 + c)
                    act.activation(xhi[:, ks, :], src[:, ks, :], ACT.Copy).then_inc(sem["xs_hi"], 1)

            act.wait_ge(sem["c_in"], 32)
            act.activation(ctok[0:NC, :], ctok[0:NC, :], ACT.Silu).then_inc(sem["c_silu"], 1)
            act.wait_ge(sem["c_turned"], 1)
            act.wait_ge(sem["cst_zero"], 1)
            act.activation(cst[:, :, 0:NC], ms[:, 0, 0:KT * NC].rearrange("p (k c) -> p k c", k=KT), ACT.Copy) \
                .then_inc(sem["c_hi"], 1)

            def mod_rows(m, c):
                act.wait_ge(sem["w_used"], m + 1)
                if not isinstance(m, int) or m >= R3:
                    act.wait_ge(sem["folded"], m - 2)
                act.activation(mtok[0:CL + NC, c, :], acc[0:CL + NC, c, 0:CW], ACT.Copy).then_inc(sem["mt_ready"], 1)

            NM = N0["xbc", 0]

            def mod_body(i, half, last=False):
                first = isinstance(i, int) and i == 0 and half == 0
                for c in range(R3):
                    m = R3 * half + c + 1
                    if not (last and c == R3 - 1):
                        act.wait_ge(raw_full[m % R6], 16 * (m // R6 + 1) + 16 * i)
                        if not (first and c < 2):
                            act.wait_ge(sem["w_used"], m - R3 + 1 + R6 * i)
                        act.activation(whi[m % R3], raw6[m % R6], ACT.Copy).then_inc(sem["hi_ready"], 1)
                    if not (first and c == 0):
                        mod_rows(R6 * i + R3 * half + c - 1, (c - 1) % R3)
            act.wait_ge(raw_full[0], 16)
            act.activation(whi[0], raw[0], ACT.Copy).then_inc(sem["hi_ready"], 1)
            for b in range(MOD_PEEL):
                mod_body(b // 2, b % 2)
                if b == 4:
                    act.wait_ge(sem["sp_in"], 16 * (4 + L))
                    act.activation(expa[:, :], headp[:, 1, :], ACT.Exp).then_inc(sem["a_exp"], 1)
                if b == 5:
                    act.wait_ge(sem["aux_copied"], len(TURNS))
                    norm_sq(1, x)
                if b == 7:
                    norm_rs(1)
            with act.Fori(0, NM // R6 - MOD_PEEL // 2 - 1) as i:
                for half in range(2):
                    mod_body(i + MOD_PEEL // 2, half)
            mod_body(NM // R6 - 1, 0)
            mod_body(NM // R6 - 1, 1, True)
            mod_rows(NM - 1, (NM - 1) % R3)
            for l in range(L):
                if l == 0:
                    split_hi(act, N0["xbc", 0], 0)
                else:
                    norm_sq(4 * l + 1, x)
                    norm_rs(4 * l + 1)
                hi_of_x(5 * l + 1, hf, sem["h_ready"], 2 * l + 1)
                S3 = CK - 1
                act_phase(act, ("xbc", l), IN_CHUNKS["xbc"], lambda i, c, banks: act.activation(
                    xrawv[:, bass.ds(4 * i + 2 * c, 2), S3:S3 + T], banks, ACT.Copy))
                split_hi(act, N0["dt", l] + 1, 0)
                act.wait_ge(sem["dt_abs"], l + 1)
                act.activation(dth[:, 3, :], dth[:, 3, :], ACT.Exp, scale=-1.0).then_inc(sem["dt_exp"], 1)

                def gates(name, dst, fn, after=None):
                    act.preload_act_table(fn)
                    act_phase(act, (name, l), IN_CHUNKS[name], lambda i, c, banks: act.activation(
                        dst[:, bass.ds(4 * i + 2 * c, 2), :], banks, fn), after=after)

                def after_z(c):
                    if c == 0:
                        act.wait_ge(sem["spread_ready"], l + 1)
                        act.activation(spx[:, :, :], ms[:, 3, 0:KT * (2 * B + 1)].rearrange("p (k c) -> p k c", k=KT),
                                       ACT.Copy).then_inc(sem["spread_copied"], 1)
                    if c >= 2:
                        act.wait_ge(sem["conv_part"], 2 * l + c - 1)
                        part = xcv[:, 0:6, 0:S] if c == 2 else xcv[:, 6:10, 0:S]
                        act.activation(part, part, ACT.Silu)
                    if c == 1:
                        act.wait_ge(sem["v_centered"], l + 1)
                        act.activation(hf[:, :, :], vb[:, :, :], ACT.Square).then_inc(sem["v_sq"], 1)

                def outer(b):
                    act.wait_ge(sem["bc_spread"], l * B + b + 1)
                    act.wait_ge(sem["dtx_ready"], l + 1)
                    for k in range(KT):
                        g = k * G // KT
                        ins = act.activation(sprod[b % 2][:, k, :], ms[:, b % 2, g * P:(g + 1) * P], ACT.Copy,
                                             scale=dtx[:, k, b:b + 1])
                    ins.then_inc(sem["outer_ready"], 1)

                def after_ga(c):
                    if c == 0:
                        act.wait_ge(sem["bc_turned"], l + 1)
                        act.activation(bct[:, :], ms[0:B, 2, :], ACT.Copy).then_inc(sem["bc_ready"], 1)
                        outer(0)
                    outer(c + 1)

                def after_gb(c):
                    if B // 2 + c + 1 < B:
                        outer(B // 2 + c + 1)
                gates("v", vb, ACT.Gelu_apprx_tanh)
                act.wait_ge(sem["tail_turned"], l + 1)
                act.activation(tail[0:CK - 1 + B, 0:CD], msf[0:CK - 1 + B, 0:CD], ACT.Copy).then_inc(sem["tail_ready"], 1)
                gates("u", ub, ACT.Gelu_apprx_tanh)
                act.wait_ge(sem["cum_ready"], l + 1)
                act.activation(spin[:, 0:B], dth[:, 2, S:T], ACT.Exp).then_inc(sem["samp_decay"], 1)
                gates("z", zs, ACT.Silu, after_z)
                act.wait_ge(sem["conv_done"], l + 1)
                act.activation(xcv[:, 10:CT, 0:S], xcv[:, 10:CT, 0:S], ACT.Silu)
                act.activation(xcv[:, :, S:T], xcv[:, :, S:T], ACT.Silu).then_inc(sem["xc_ready"], 1)
                gates("ga", sga, ACT.Sigmoid, after_ga)
                act.wait_ge(sem["v_inv"], l + 1)
                act.activation(rs[:, 0, :], rs[:, 0, :], ACT.Sqrt).then_inc(sem["v_rs"], 1)
                gates("gb", sgb, ACT.Sigmoid, after_gb)
                act.wait_ge(sem["vs_turned"], l + 1)
                act.activation(vrow, msf[0:B, 0:D], ACT.Copy).then_inc(sem["vs_copied"], 1)
                for c in range(NQ):
                    act.wait_ge(sem["v_tok"], l * NQ + c + 1)
                    act.activation(vtok[:, c, :], msf[:, 0:D], ACT.Copy).then_inc(sem["v_tok_ready"], 1)
                act.wait_ge(sem["sp_bcast"], l + 1)
                act.activation(spc[:, :, :].rearrange("p a b -> p (a b)"), ms[:, 0, 0:2 * KT], ACT.Copy) \
                    .then_inc(sem["sp_bcast_ready"], 1)
                act.wait_ge(sem["sp_taken"], l + 1)
                act.wait_ge(sem["w_used"], N0["cmlp_out", l])
                hi_of_x(5 * l + 2, ub)
                n = N0["cmlp_out", l]
                for c in range(NQ):
                    v = l * NQ + c
                    act.wait_ge(sem["tok_ready"], v + 1)
                    if c:
                        act.wait_ge(sem["st_part"], v)
                    act.activation(bt[:, :, :], ms[:, 2, 0:G * P].rearrange("p (g n) -> p g n", g=G), ACT.Copy) \
                        .then_inc(sem["bt_ready"], 1)
                    split_hi(act, n + 2 * c + 1, 0)
                    act.wait_ge(sem["wend_arg"], v + 1)
                    act.activation(wend[:, :], wend[:, :], ACT.Exp).then_inc(sem["wend_ready"], 1)
                    act.activation(elast[:, :], lastc[:, :], ACT.Exp).then_inc(sem["last_ready"], 1)
                    for h in range(H // 2, H):
                        ins = act.activation(mix[:, h, :], ms[:, h // 4, (h % 4) * Q:(h % 4 + 1) * Q], ACT.Relu,
                                             bias=tokp[:, 0, h:h + 1], scale=-1.0)
                    ins.then_inc(sem["seg_act"], 1)
                    act.wait_ge(sem["seg_act"], v + 1)
                    act.wait_ge(sem["seg_ready"], v + 1)
                    if c:
                        for s in range(2):
                            act.wait_ge(s_out[s], 8 * (l + 1) * B)
                        act.activation(ce[:, :, :].rearrange("p h q -> p (h q)"), msf, ACT.Exp).then_inc(sem["ce_exp"], 1)
                    act.activation(mix[:, 0:H // 2, :], mix[:, 0:H // 2, :], ACT.Exp)
                    act.activation(mix[:, H // 2:H, :], mix[:, H // 2:H, :], ACT.Exp, scale=-1.0) \
                        .then_inc(sem["mix_exp"], 1)
                    split_hi(act, n + 2 * c + 2, 0)
                    if c == 0:
                        act.wait_ge(sem["st_part"], v + 1)
                        act.activation(hT[:, :], msf[:, 1024:2048], ACT.Copy).then_inc(sem["st_ready"], 1)
                for g, ks in enumerate(HALVES):
                    act.wait_ge(sem["samp_done"], G * l + g + 1)
                    act.activation(zs[:, ks, :], hf[:, ks, :], ACT.Square).then_inc(sem["gate_sq"], 1)
                act.preload_act_table(ACT.Sqrt)
                for g in range(G):
                    act.wait_ge(sem["gate_ssq"], G * l + g + 1)
                    act.activation(rs[:, g, :], ms[:, g, 0:T], ACT.Sqrt, bias=eps[:, 0:1], scale=G / D) \
                        .then_inc(sem["gate_root"], 1)
                act.wait_ge(sem["w_used"], N0["ssd_out", l])
                hi_of_x(5 * l + 3, hf, sem["y_normed"], l + 1)
                act.wait_ge(sem["st_turned"], l + 1)
                act.activation(hst.rearrange("p k n -> p (k n)"), msf[:, 1024:2048], ACT.Copy).then_inc(sem["st_copied"], 1)
                act_phase(act, ("ssd_out", l), KT // MT)
                act.wait_ge(sem["w_used"], N0["w_o", l])
                hi_of_x(5 * l + 4, hf, sem["merged"], l + 1)

                def take_w_o(i, c, banks):
                    ks = bass.ds(4 * i + 2 * c, 2)
                    act.activation(hf[:, ks, :], banks, ACT.Square).then_inc(sem["sq_ready"], 1)
                    return act.activation(zs[:, ks, :], banks, ACT.Copy)
                act_phase(act, ("w_o", l), KT // MT, take_w_o, end=l == L - 1)
                for p in range(2):
                    act.wait_ge(acc_free[p], (Q0["gu", l] + 1 - p) // 2)
                norm_rs(4 * l + 2)
                norm_sq(4 * l + 3, x)
                norm_rs(4 * l + 3)
                hi_of_x(5 * l + 5, hf, sem["h_ready"], 2 * l + 2)
                act.wait_ge(sem["st_out"], 16 * (l + 1))
                if l % 2:
                    def htok_of(c):
                        rows = Q if c < NQ else B
                        act.wait_ge(sem["h_turned"], c + 1)
                        act.activation(htokhi[0:rows, c, :], accf[0:rows, (c % 2) * D:(c % 2 + 1) * D], ACT.Copy) \
                            .then_inc(sem["htok_hi"], 1)
                    act.preload_act_table(ACT.Exp)
                    htok_of(0)
                    htok_of(1)
                    act.wait_ge(sem["route_arg"], 1)
                    act.activation(lg[:, :, :], lg[:, :, :], ACT.Exp).then_inc(sem["route_exp"], 1)
                    htok_of(2)

                def expert(e, pairs_before, last):
                    n0, q0 = N0["gu", l], Q0["gu", l]

                    def gates(i):
                        split_hi(act, n0 + 1, i, 2, e)
                        act.wait_ge(sem["w_used"], n0 + 1 + 2 * i + EN * e)
                        act.wait_ge(sem["gu_ready"], pairs_before + i + FT // MT * e)
                        act.activation(sg[:, :, :], acc[:, 2 * (q0 % 2):2 * (q0 % 2) + 2, 0:T], ACT.Silu) \
                            .then_inc(acc_free[q0 % 2], 1)
                        split_hi(act, n0 + 2, i, 2, e)
                        act.wait_ge(sem["gu_ready"], pairs_before + 1 + i + FT // MT * e)
                        act.activation(ghi[:, bass.ds(2 * i, 2), :], gu[:, :, :], ACT.Copy).then_inc(sem["g_hi"], 1)

                    with act.Fori(0, FT // MT) as i:
                        gates(i)
                    n1 = N0["wd", l]
                    C = 2 * len(KG)

                    def downs(i, last=False):
                        for c in range(C - (1 if last else 0)):
                            split_hi(act, n1 + c + 1, i, C, e)
                    if last:
                        downs(0)
                        downs(1, True)
                    else:
                        with act.Fori(0, KT // MT // 2) as i:
                            downs(i)

                act.preload_act_table(ACT.Silu)
                if l % 2 == 0:
                    expert(0, 1, False)
                    act.wait_ge(acc_free[0], Q0["wd", l] // 2 + KT // MT // 2 + Q0["wd", l] % 2)
                    act.wait_ge(acc_free[1], Q0["wd", l] // 2 + KT // MT // 2)
                else:
                    with act.If(crowded(act)):
                        act.wait_ge(sem["combine_turned"], 1)
                        act.activation(comb[:, :], ms[0:E, 2, 0:T], ACT.Copy).then_inc(sem["combine_ready"], 1)
                        for e in range(E):
                            act.wait_ge(sem["combine_spread"], e + 1)
                            act.activation(cbc[:, e, :], ms[:, e % 4, 0:T], ACT.Copy) \
                                .then_inc(sem["combine_spread_ready"], 1)
                        split_hi(act, NX, 0)
                        act.preload_act_table(ACT.Silu)
                        with act.Fori(0, E - 1) as e:
                            expert(e, 1 + FT // MT, False)
                        expert(E - 1, 1 + FT // MT, True)
                    with act.Else():
                        act.preload_act_table(ACT.Silu)
                        split_hi3(act, 0, 0, 0)
                        split_hi3(act, 1, 0, 0)
                        act.wait_ge(sem["gathered_hi"], 1)
                        act.activation(hghi[:, :, :].rearrange("p k t -> p (k t)"), msf[:, 0:D], ACT.Copy) \
                            .then_inc(sem["hg_hi"], 1)

                        def picked(half, two, last):
                            e = 2 * two + half

                            def turned(b, q):
                                act.wait_ge(sem["gu_turned"], q + 2 + R3 * b + FP * e)
                                act.activation(gthi[:, bass.ds(MT * q + MT * R3 * b, MT), :],
                                               ms[:, q % R3, 0:MT * P].rearrange("p (k t) -> p k t", k=MT), ACT.Copy) \
                                    .then_inc(sem["gt_hi"], 1)

                            def pair(b, q):
                                peeled = isinstance(b, int)
                                split_hi3(act, 2 * q + 2, half, two, b)
                                if not (peeled and q == 0):
                                    turned(b, q - 1)
                                split_hi3(act, 2 * q + 3, half, two, b)
                                act.wait_ge(sem["w_used"], NX + 2 * q + 2 + 2 * R3 * b + SN * e)
                                act.wait_ge(sem["gu_done"], R3 + q + R3 * b + FP * e)
                                act.activation(sgs[:, :], acc[:, q % R3, 0:CW], ACT.Silu).then_inc(sem["gate_ready"], 1)
                                if peeled and q == 1:
                                    act.wait_ge(sem["gw_turned"], 1 + e)
                                    act.activation(pickT[:, :], acc[:, 3, 0:T], ACT.Copy)
                                    act.activation(weight[:, :], acc[:, 3, T:T + 1], ACT.Copy).then_inc(sem["gw_ready"], 1)

                            pairs(act, pair)
                            for d in range(FD):
                                if not (last and d >= FD - 2):
                                    split_hi3(act, 2 * FP + d + 2, half, two)
                                if not last and d == 8:
                                    act.wait_ge(sem["gathered_hi"], 2 + e)
                                    act.activation(hghi[:, :, :].rearrange("p k t -> p (k t)"), msf[:, 0:D], ACT.Copy) \
                                        .then_inc(sem["hg_hi"], 1)
                                if d == 0:
                                    turned(0, FP - 1)
                            act.wait_ge(sem["w_used"], NX + SN + SN * e)
                            act.wait_ge(sem["gw_ready"], 1 + e)
                            act.activation(yshi[:, :].rearrange("p (h c) -> p h c", h=2), acc[:, 2:4, :], ACT.Copy,
                                           scale=weight[:, 0:1]).then_inc(sem["ys_hi"], 1)
                        by_twos(act, picked)
                    act.wait_ge(sem["moe_done"], 1)
                norm_sq(4 * l + 4, facc)
                norm_rs(4 * l + 4)

        @block.vector
        def _(dve):
            steps = 0

            scaled = 0

            def then(ins):
                nonlocal steps
                steps += 1
                ins.then_inc(sem["dve_chain"], 1)
                dve.wait_ge(sem["dve_chain"], steps)

            def mean_inv(out, sums, count, done):
                then(dve.tensor_scalar(out, sums, 1.0 / count, EPS, ALU.mult, ALU.add))
                dve.reciprocal(out, out).then_inc(done, 1)

            def fold_squares(sq, c):
                to, by = (sq[:, HT * c + HT // 2 * k:HT * c + HT // 2 * (k + 1), :] for k in range(2))
                return dve.tensor_tensor(to, to, by, ALU.add)

            def norm_inv(v):
                if v > 1 and v % 4 != 2:
                    for c in range(2):
                        dve.wait_ge(sem["sq_ready"], squares(v) + c + 1)
                        fold_squares(hf, c).then_inc(sem["sq_folded"], 1)
                dve.wait_ge(sem["root_ready"], v)
                then(dve.reciprocal(rs[:, 0, :], rs[:, 0, :]))

            def lo_of_x(v, src):
                for c, ks in enumerate(HALVES):
                    dve.wait_ge(sem["xs_hi"], 2 * v - 1 + c)
                    dve.tensor_tensor(xlo[:, ks, :], src[:, ks, :], xhi[:, ks, :].bitcast(F32), ALU.subtract) \
                        .then_inc(sem["xs_lo"], 1)

            def modulated(l, k, v, hv):
                if v > 1:
                    norm_inv(v)
                sh, sc = mod[:, l, 3 * k * KT:(3 * k + 1) * KT, :], mod[:, l, (3 * k + 1) * KT:(3 * k + 2) * KT, :]
                scaled_x = sq1 if v == 1 else hf
                for ks in HALVES:
                    if v > 1:
                        then(dve.tensor_tensor(hf[:, ks, :], x[:, ks, :], bc(rs[:, 0, :], 1, [P, HT, T]), ALU.mult))
                    hs = hf[:, ks, S:T]
                    dve.tensor_tensor(hs, scaled_x[:, ks, S:T], sc[:, ks, 1:1 + B], ALU.mult) \
                        .then_inc(sem["samp_scaled"], 1)
                    for t in range(KT)[ks]:
                        dve.tensor_scalar(hf[:, t, 0:S], scaled_x[:, t, 0:S], sc[:, t, 0:1], sh[:, t, 0:1], ALU.mult, ALU.add)
                    samples_scaled()
                    dve.tensor_tensor(hs, hs, sh[:, ks, 1:1 + B], ALU.add).then_inc(sem["h_ready"], 1)

            def samples_scaled():
                nonlocal scaled
                scaled += 1
                dve.wait_ge(sem["samp_scaled"], scaled)

            def add_normed(l, k, v, src):
                norm_inv(v)
                g = mod[:, l, (3 * k + 2) * KT:(3 * k + 3) * KT, :]
                for ks in HALVES:
                    then(dve.tensor_tensor(src[:, ks, :], src[:, ks, :], bc(rs[:, 0, :], 1, [P, HT, T]), ALU.mult))
                    dve.tensor_tensor(src[:, ks, S:T], src[:, ks, S:T], g[:, ks, 1:1 + B], ALU.mult) \
                        .then_inc(sem["samp_scaled"], 1)
                    for t in range(KT)[ks]:
                        dve.scalar_tensor_tensor(out=x[:, t, 0:S], in0=src[:, t, 0:S], scalar=g[:, t, 0:1],
                                                 in1=x[:, t, 0:S], op0=ALU.mult, op1=ALU.add)
                    samples_scaled()
                    dve.tensor_tensor(x[:, ks, S:T], x[:, ks, S:T], src[:, ks, S:T], ALU.add) \
                        .then_inc(sem["x_ready"], 1)

            dve.memset(ctok[0:NC, :], 0.0).then_inc(sem["ctok_zero"], 1)
            dve.memset(cst[:, :, :].bitcast(F32), 0.0).then_inc(sem["cst_zero"], 1)
            dve.memset(eps[:, :], EPS)
            then(dve.memset(ones[:, :], 1.0))
            dve.wait_ge(sem["c_hi"], 1)
            dve.tensor_tensor(cst[:, :, CL:CL + NC], ms[:, 0, 0:KT * NC].rearrange("p (k c) -> p k c", k=KT),
                              cst[:, :, 0:NC].bitcast(F32), ALU.subtract).then_inc(sem["c_lo"], 1)

            def turned(p):
                what, c, h = TURNS[p]
                dve.wait_ge(sem["aux_turned"], p + 1)
                bank = turn_bank(p)
                if what == "params":
                    src, dst = bank[:, 0:L * NROW], PT[:, :, :].rearrange("p l r -> p (l r)")
                elif what == "state":
                    src, dst = bank[:, 0:CT * SR], stT[:, c, :, :].rearrange("p c r -> p (c r)")
                elif c < NQ:
                    src, dst = bank.rearrange("p (k t) -> p k t", t=Q), x[:, 4 * h:4 * h + 4, c * Q:(c + 1) * Q]
                else:
                    src, dst = bank[:, 0:KT * B].rearrange("p (k t) -> p k t", t=B), x[:, :, S:T]
                dve.tensor_copy(dst, src).then_inc(sem["aux_copied"], 1)
            NM = N0["xbc", 0]

            def mod_lo(i, m):
                dve.wait_ge(sem["hi_ready"], m + 1 + R6 * i)
                dve.tensor_tensor(wlo[m % R3], raw6[m % R6], whi[m % R3].bitcast(F32), ALU.subtract) \
                    .then_inc(sem["lo_ready"], 1)

            def mod_add(m, s):
                dve.wait_ge(sem["folded"], m + 1)
                c0 = MT * m if isinstance(m, int) else dve.snap(MT * m)
                dve.tensor_copy(modf[:, bass.ds(c0, MT), :], ms[:, s, 0:MT * NC].rearrange("p (j c) -> p j c", j=MT)) \
                    .then_inc(sem["mod_added"], 1)

            def mod_body(i, half, last=False):
                for c in range(R3):
                    m = R3 * half + c
                    if not (last and c == R3 - 1):
                        mod_lo(i, m + 1)
                    if not (isinstance(i, int) and i == 0 and half == 0):
                        mod_add(R6 * i + m - R3, c)
            mod_lo(0, 0)
            for b in range(MOD_PEEL):
                mod_body(b // 2, b % 2)
                for p in TURNS_AFTER.get(b, ()):
                    turned(p)
                if b == 7:
                    norm_inv(1)
                    then(dve.tensor_tensor(sq1, x[:, :, :], bc(rs[:, 0, :], 1, [P, KT, T]), ALU.mult))
            with dve.Fori(0, NM // R6 - MOD_PEEL // 2 - 1) as i:
                for half in range(2):
                    mod_body(i + MOD_PEEL // 2, half)
            mod_body(NM // R6 - 1, 0)
            mod_body(NM // R6 - 1, 1, True)
            for m in range(NM - R3, NM):
                mod_add(m, m % R3)
            dve.wait_ge(sem["mod_added"], NM)
            dve.wait_ge(sem["aux_copied"], len(TURNS))

            def finish_mod(l):
                ml = mod[:, l, :, :]
                then(dve.tensor_tensor(ml, ml, bc(row("b_mod", l), 2, [P, 6 * KT, NC]), ALU.add))
                for k, (pre, post) in enumerate((("mix_pre_g", "mix_post_g"), ("ffn_pre_g", "ffn_post_g"))):
                    sc = mod[:, l, (3 * k + 1) * KT:(3 * k + 2) * KT, :]
                    g = mod[:, l, (3 * k + 2) * KT:(3 * k + 3) * KT, :]
                    dve.scalar_tensor_tensor(out=sc, in0=sc, scalar=1.0, in1=bc(row(pre, l), 2, [P, KT, NC]),
                                             op0=ALU.add, op1=ALU.mult)
                    ins = dve.tensor_tensor(g, g, bc(row(post, l), 2, [P, KT, NC]), ALU.mult)
                ins.then_inc(sem["mod_ready"], 1)
                dve.wait_ge(sem["mod_ready"], l + 1)

            finish_mod(0)
            split_lo(dve, N0["xbc", 0], 0)
            for l in range(L):
                modulated(l, 0, 4 * l + 1, 2 * l + 1)
                lo_of_x(5 * l + 1, hf)
                ins = dve.memset(xrawv[:, :, 0:CK - 1], 0.0)
                then(ins)
                dve_phase(dve, ("xbc", l), IN_CHUNKS["xbc"])
                n, q = N0["dt", l], Q0["dt", l]
                split_lo(dve, n + 1, 0)
                dve.wait_ge(sem["w_used"], n + 1)
                dve.tensor_scalar(dth[:, 1, :], acc[0:H, 2 * (q % 2), 0:T], headp[:, 0, l:l + 1], None, ALU.add) \
                    .then_inc(acc_free[q % 2], 1)
                cum, dt, dta, e_, r_, s2, p_, mx = (dth[:, k, :] for k in range(8))
                dve.wait_ge(acc_free[q % 2], q // 2 + 1)
                dve.scalar_tensor_tensor(out=e_, in0=dt, scalar=-1.0, in1=dt, op0=ALU.mult, op1=ALU.max) \
                    .then_inc(sem["dt_abs"], 1)
                dve.tensor_scalar(mx, dt, 0.0, None, ALU.max)

                def after_v(c):
                    if c == 0:
                        dve.wait_ge(sem["dt_exp"], l + 1)
                        then(dve.tensor_scalar(r_, e_, 2.0, None, ALU.add))
                        then(dve.reciprocal(r_, r_))
                        then(dve.tensor_tensor(r_, e_, r_, ALU.mult))
                    if c == 1:
                        then(dve.tensor_tensor(s2, r_, r_, ALU.mult))
                        then(dve.tensor_scalar(p_, s2, 1.0 / 17, None, ALU.mult))
                        for k in range(15, 9, -2):
                            then(dve.scalar_tensor_tensor(out=p_, in0=p_, scalar=1.0 / k, in1=s2, op0=ALU.add, op1=ALU.mult))
                    if c == 2:
                        for k in range(9, 1, -2):
                            then(dve.scalar_tensor_tensor(out=p_, in0=p_, scalar=1.0 / k, in1=s2, op0=ALU.add, op1=ALU.mult))
                        then(dve.scalar_tensor_tensor(out=p_, in0=p_, scalar=1.0, in1=r_, op0=ALU.add, op1=ALU.mult))
                        then(dve.scalar_tensor_tensor(out=dt, in0=p_, scalar=2.0, in1=mx, op0=ALU.mult, op1=ALU.add))
                    if c == 3:
                        if l + 1 < L:
                            finish_mod(l + 1)
                        dve.wait_ge(sem["a_exp"], 1)
                        then(dve.tensor_scalar(dta, dt, expa[:, l:l + 1], -1.0, ALU.mult, ALU.mult))
                        for k in range(NQ):
                            dve.tensor_tensor_scan(cum[:, k * Q:(k + 1) * Q], ones[0:H, 0:Q], dta[:, k * Q:(k + 1) * Q],
                                                   0.0, ALU.mult, ALU.add)
                        dve.tensor_copy(spin[:, B:2 * B], dt[:, S:T])
                        dve.tensor_copy(spin[:, 2 * B:2 * B + 1], headp[:, 2, l:l + 1]).then_inc(sem["cum_ready"], 1)

                def conv(tiles, done=False):
                    for k in range(CK):
                        for t in tiles:
                            src = xrawv[:, t, k:k + S]
                            if k == 0:
                                ins = dve.tensor_scalar(xcv[:, t, 0:S], src, row("conv_w", l, t), row("conv_b", l, t),
                                                        ALU.mult, ALU.add)
                            else:
                                ins = dve.scalar_tensor_tensor(out=xcv[:, t, 0:S], in0=src,
                                                               scalar=row("conv_w", l, k * CT + t),
                                                               in1=xcv[:, t, 0:S], op0=ALU.mult, op1=ALU.add)
                        if done and k == CK - 1:
                            ins.then_inc(sem["conv_part"], 1)
                        else:
                            then(ins)

                def after_u(c):
                    conv(((0, 1), (2, 3), (4,), (5,))[c], done=c == 3)

                def after_z(c):
                    if c == 0:
                        dve.wait_ge(sem["v_sum"], l + 1)
                        then(dve.tensor_scalar(rs[:, 1, :], ms[:, 0, 0:T], 1.0 / D, None, ALU.mult))
                        dve.tensor_tensor(vb[:, :, :], vb[:, :, :], bc(rs[:, 1, :], 1, [P, KT, T]), ALU.subtract) \
                            .then_inc(sem["v_centered"], 1)
                    else:
                        conv((2 * c + 4, 2 * c + 5), done=c == 2)
                    if c == 3:
                        st = stT[:, l, :, :].rearrange("p c (b k) -> p c b k", k=CK - 1)
                        wk = row("conv_w", l).rearrange("p (k c) -> p k c", k=CK)
                        xs_ = xcv[:, :, S:T]
                        then(dve.tensor_tensor(xs_, xrawv[:, :, CK - 1 + S:CK - 1 + T],
                                               bc(wk[:, CK - 1, :], 2, [P, CT, B]), ALU.mult))
                        for k in range(CK - 1):
                            then(dve.tensor_tensor(tmp[:, :, :], st[:, :, :, k], bc(wk[:, k, :], 2, [P, CT, B]), ALU.mult))
                            then(dve.tensor_tensor(xs_, xs_, tmp[:, :, :], ALU.add))
                        dve.tensor_tensor(xs_, xs_, bc(row("conv_b", l), 2, [P, CT, B]), ALU.add) \
                            .then_inc(sem["conv_done"], 1)

                def sample(b):
                    s = b % 2
                    Sb = sring[:, s]
                    Cb = ms[:, 2 + s, 0:G * P].rearrange("p (g n) -> p g n", g=G)
                    dve.wait_ge(sem["outer_ready"], l * B + b + 1)
                    dve.wait_ge(s_in[s], 16 * (l * B // 2 + b // 2 + 1))
                    for k in range(KT):
                        ins = dve.scalar_tensor_tensor(out=Sb[:, k, :], in0=Sb[:, k, :], scalar=spx[:, k, b:b + 1],
                                                       in1=sprod[s][:, k, :], op0=ALU.mult, op1=ALU.add)
                    ins.then_inc(sem["s_new"], 1)
                    dve.wait_ge(sem["s_new"], l * B + b + 1)
                    for k in range(KT):
                        ins = dve.tensor_tensor_reduce(sprod[s][:, k, :], Sb[:, k, :], Cb[:, k * G // KT, :], 1.0, 0.0,
                                                       ALU.mult, ALU.add, accum_out=ysm[:, k, b:b + 1])
                    ins.then_inc(sem["samp_used"], 1)

                def after_ga(c):
                    if c == 0:
                        dve.wait_ge(sem["xc_ready"], l + 1)
                        dve.wait_ge(sem["spread_copied"], l + 1)
                        dve.tensor_tensor(dtx[:, :, :], xcv[:, 0:KT, S:T], spx[:, :, B:2 * B], ALU.mult) \
                            .then_inc(sem["dtx_ready"], 1)
                    sample(c)

                def after_gb(c):
                    sample(B // 2 + c)
                    if c == 0:
                        dve.wait_ge(sem["v_rs"], l + 1)
                        then(dve.tensor_tensor(vb[:, :, :], vb[:, :, :], bc(rs[:, 0, :], 1, [P, KT, T]), ALU.mult))
                    if c == 1:
                        for t in range(KT):
                            ins = dve.tensor_scalar(vb[:, t, :], vb[:, t, :], row("cmlp_ln_g", l, t),
                                                    row("cmlp_ln_b", l, t), ALU.mult, ALU.add)
                        ins.then_inc(sem["v_normed"], 1)
                dve_phase(dve, ("v", l), IN_CHUNKS["v"], after=after_v)
                for p in range(2):
                    dve.wait_ge(acc_free[p], (Q0["dt", l] + 1 - p) // 2)
                dve_phase(dve, ("u", l), IN_CHUNKS["u"], after=after_u)
                dve_phase(dve, ("z", l), IN_CHUNKS["z"], after=after_z)
                dve.wait_ge(sem["v_ssq"], l + 1)
                mean_inv(rs[:, 0, :], ms[:, 1, 0:T], D, sem["v_inv"])
                dve_phase(dve, ("ga", l), IN_CHUNKS["ga"], after=after_ga)
                dve_phase(dve, ("gb", l), IN_CHUNKS["gb"], after=after_gb)
                dve.wait_ge(sem["sp_in"], 16 * (4 + L))
                dve.tensor_scalar(diag[:, 0, :], ident[0:KT, 0:KT], w00[:, l:l + 1], None, ALU.mult)
                dve.tensor_scalar(diag[:, 1, :], ident[0:KT, 0:KT], spb[:, l, 0:1], None, ALU.mult) \
                    .then_inc(sem["diag_ready"], 1)
                dve.wait_ge(sem["w_turned"], l + 1)
                dve.tensor_tensor(wT, msf[:, 1024:2048].rearrange("p (g q) -> p g q", g=KT),
                                  bc(tri[:, :], 1, [P, KT, Q]), ALU.mult).then_inc(sem["w_ready"], 1)
                dve.wait_ge(sem["v_normed"], l + 1)
                dve.wait_ge(sem["sp_bcast_ready"], l + 1)
                g0 = tmp[:, 0:KT, :]
                then(dve.tensor_tensor(g0, vb[:, :, S:T], bc(spc[:, 0, :], 2, [P, KT, B]), ALU.mult))
                then(dve.tensor_tensor(g0, g0, bc(spc[:, 1, :], 2, [P, KT, B]), ALU.add))
                dve.tensor_tensor(ub[:, :, S:T], ub[:, :, S:T], g0, ALU.mult)
                for c in range(NQ):
                    dve.wait_ge(sem["sp_out"], l * NQ + c + 1)
                    ins = dve.tensor_tensor(ub[:, :, c * Q:(c + 1) * Q], ub[:, :, c * Q:(c + 1) * Q],
                                            msf[:, c * 1024:(c + 1) * 1024].rearrange("p (k q) -> p k q", k=KT), ALU.mult)
                ins.then_inc(sem["sp_taken"], 1)
                lo_of_x(5 * l + 2, ub)

                def cmlp_chunk(c):
                    n, pair = N0["cmlp_out", l] + c, (Q0["cmlp_out", l] + c) % 2
                    dve.wait_ge(sem["w_used"], n + 1)
                    dve.tensor_tensor(sgb[:, 2 * c:2 * c + 2, :], sgb[:, 2 * c:2 * c + 2, :],
                                      acc[:, 2 * pair:2 * pair + 2, 0:T], ALU.mult).then_inc(acc_free[pair], 1)

                for c in range(NQ):
                    v = l * NQ + c
                    toks = slice(c * Q, (c + 1) * Q)
                    dve.wait_ge(sem["b_tok"], v + 1)
                    dve.tensor_copy(tokp[:, :, :].rearrange("p a h -> p (a h)"), ms[:, 2, 2 * P:2 * P + 2 * H]) \
                        .then_inc(sem["tok_ready"], 1)
                    dve.wait_ge(sem["tok_ready"], v + 1)
                    dve.tensor_tensor(xdt[:, :].rearrange("p (h d) -> p h d", h=H),
                                      msf[:, 0:D].rearrange("p (h d) -> p h d", h=H),
                                      bc(tokp[:, 1, :], 2, [P, H, HD]), ALU.mult).then_inc(sem["xdt_ready"], 1)
                    dve.wait_ge(sem["cb_ready"], v + 1)
                    dve.tensor_tensor(cbm[:, :, :], ms[:, 3, 0:G * Q].rearrange("p (g q) -> p g q", g=G),
                                      bc(tri[:, :], 1, [P, G, Q]), ALU.mult).then_inc(sem["cbm_ready"], 1)
                    split_lo(dve, N0["cmlp_out", l] + 2 * c + 1, 0)
                    dve.wait_ge(sem["cumb_ready"], v + 1)
                    last = ms[:, :, :].rearrange("p b (h q) -> p (b h) q", q=Q)[:, :, Q - 1]
                    then(dve.tensor_copy(lastc[:, :], last))
                    dve.tensor_tensor(wend[:, :], lastc[:, :], tokp[:, 0, :], ALU.subtract).then_inc(sem["wend_arg"], 1)
                    for h in range(H // 2):
                        cs = tokp[:, 0, h:h + 1]
                        ins = dve.tensor_scalar(mix[:, h, :], ms[:, h // 4, (h % 4) * Q:(h % 4 + 1) * Q], cs, cs,
                                                ALU.min, ALU.subtract)
                    ins.then_inc(sem["seg_ready"], 1)
                    dve.wait_ge(sem["wend_ready"], v + 1)
                    dve.tensor_tensor(xw[:, :].rearrange("p (h d) -> p h d", h=H),
                                      xdt[:, :].rearrange("p (h d) -> p h d", h=H),
                                      bc(wend[:, :], 2, [P, H, HD]), ALU.mult).then_inc(sem["xw_ready"], 1)
                    cmlp_chunk(2 * c)
                    if c:
                        dve.wait_ge(sem["ce_exp"], l + 1)
                        for g in range(G):
                            ins = dve.tensor_tensor(ce[:, g * R:(g + 1) * R, :], ce[:, g * R:(g + 1) * R, :],
                                                    bc(xcv[:, KT + G + g, toks], 1, [P, R, Q]), ALU.mult)
                        ins.then_inc(sem["ce_ready"], 1)
                    dve.wait_ge(sem["mix_exp"], v + 1)
                    for g in range(G):
                        ins = dve.tensor_tensor(mix[:, g * R:(g + 1) * R, :], mix[:, g * R:(g + 1) * R, :],
                                                bc(cbm[:, g, :], 1, [P, R, Q]), ALU.mult)
                    ins.then_inc(sem["mix_ready"], 1)
                    split_lo(dve, N0["cmlp_out", l] + 2 * c + 2, 0)
                    cmlp_chunk(2 * c + 1)
                    dve.wait_ge(sem["y_part"], v + 1)
                    dve.wait_ge(sem["vs_out"], 16 * (l + 1))
                    for t in range(KT):
                        ins = dve.scalar_tensor_tensor(out=hf[:, t, toks], in0=xcv[:, t, toks],
                                                       scalar=spx[:, t, 2 * B:2 * B + 1],
                                                       in1=ms[:, t // 4, (t % 4) * Q:(t % 4 + 1) * Q],
                                                       op0=ALU.mult, op1=ALU.add)
                    ins.then_inc(sem["y_taken"], 1)

                dve.wait_ge(sem["samp_used"], (l + 1) * B)
                then(dve.tensor_tensor(hf[:, :, S:T], xcv[:, 0:KT, S:T],
                                       spx[:, :, 2 * B:2 * B + 1].to_broadcast([P, KT, B]), ALU.mult))
                then(dve.tensor_tensor(hf[:, :, S:T], hf[:, :, S:T], ysm[:, :, :], ALU.add))
                for ks in HALVES:
                    dve.tensor_tensor(hf[:, ks, :], hf[:, ks, :], zs[:, ks, :], ALU.mult).then_inc(sem["samp_done"], 1)
                for g in range(G):
                    dve.wait_ge(sem["gate_sq"], G * l + g + 1)
                    fold_squares(zs, g).then_inc(sem["gate_folded"], 1)
                dve.wait_ge(sem["last_ready"], (l + 1) * NQ)
                hv = hT[:, :].rearrange("p (h d) -> p h d", h=H)
                then(dve.tensor_tensor(hv, hv, bc(elast[:, :], 2, [P, H, HD]), ALU.mult))
                dve.wait_ge(sem["st_part"], (l + 1) * NQ)
                dve.tensor_tensor(hT[:, :], hT[:, :], msf[:, 1024:2048], ALU.add).then_inc(sem["st_ready"], 1)
                for g, ks in enumerate(HALVES):
                    dve.wait_ge(sem["gate_root"], G * l + g + 1)
                    then(dve.reciprocal(rs[:, g, :], rs[:, g, :]))
                    for t in range(KT)[ks]:
                        ins = dve.scalar_tensor_tensor(out=hf[:, t, :], in0=hf[:, t, :], scalar=row("ssm_norm_g", l, t),
                                                       in1=rs[:, g, :], op0=ALU.mult, op1=ALU.mult)
                    ins.then_inc(sem["y_normed"], 1)
                lo_of_x(5 * l + 3, hf)

                def merge(c):
                    q = Q0["ssd_out", l] + c
                    ks = slice(MT * c, MT * (c + 1))
                    dve.wait_ge(acc_free[q % 2], q // 2 + 1)
                    ins = dve.tensor_tensor(hf[:, ks, :], sga[:, ks, :], sgb[:, ks, :], ALU.add)
                    if c % 2:
                        ins.then_inc(sem["merged"], 1)
                dve_phase(dve, ("ssd_out", l), KT // MT, lambda i, c, banks: dve.tensor_tensor(
                    sga[:, bass.ds(4 * i + 2 * c, 2), :], sga[:, bass.ds(4 * i + 2 * c, 2), :], banks, ALU.mult),
                          after=merge)
                lo_of_x(5 * l + 4, hf)
                dve_phase(dve, ("w_o", l), KT // MT, end=l == L - 1)
                add_normed(l, 0, 4 * l + 2, zs)
                dve.wait_ge(sem["x_ready"], 4 * l + 2)
                modulated(l, 1, 4 * l + 3, 2 * l + 2)
                lo_of_x(5 * l + 5, hf)
                dve.wait_ge(sem["st_out"], 16 * (l + 1))

                if l % 2:
                    dve.memset(sgs[:, :], 0.0).then_inc(sem["gu_done"], R3)
                    dve.memset(gus[:, :], 0.0).then_inc(sem["gt_lo"], R3)
                    dve.memset(weight[:, :], 0.0).then_inc(sem["scat_added"], 2)
                    dve.memset(yslo[:, :].bitcast(F32), 0.0).then_inc(sem["gu_turned"], 1)
                    then(dve.tensor_tensor_scan(count[:, :], ones[:, :], ones[:, :], 0.0, ALU.mult, ALU.add))

                    def build(e):
                        col = bass.ds(e, 1)
                        for c in range(3):
                            rows = Q if c < NQ else B
                            ins = dve.tensor_scalar(pick[0:rows, c, :], count[0:rows, :], place[0:rows, c, col],
                                              sel[0:rows, c, col], ALU.is_equal, ALU.mult)
                        ins.then_inc(sem["g_built"], 1)

                    def htok_of(c):
                        rows = Q if c < NQ else B
                        dve.wait_ge(sem["htok_hi"], c + 1)
                        dve.tensor_tensor(htoklo[0:rows, c, :], accf[0:rows, (c % 2) * D:(c % 2 + 1) * D],
                                          htokhi[0:rows, c, :].bitcast(F32), ALU.subtract).then_inc(sem["htok_lo"], 1)
                    dve.wait_ge(sem["logits_ready"], 1)
                    then(dve.memset(lg[:, :, :], 0.0))
                    then(dve.tensor_copy(lg[:, 0:NQ, :], ms[:, 1:1 + NQ, 0:E]))
                    then(dve.tensor_copy(lg[0:B, NQ, :], ms[0:B, 1 + NQ, 0:E]))
                    for c in range(3):
                        mine, other = bc(lg[:, c, :], 2, [P, E, E]), bc(lg[:, c, :], 1, [P, E, E])
                        dve.tensor_reduce(top[:, c, 0:1], lg[:, c, :], AX.X, ALU.max)
                        then(dve.tensor_tensor(eqm[:, :, :], other, mine, ALU.is_equal))
                        then(dve.tensor_tensor(eqm[:, :, :], eqm[:, :, :], earlier[:, :, :], ALU.mult))
                        then(dve.tensor_tensor(cmp_[:, :, :], other, mine, ALU.is_gt))
                        then(dve.tensor_tensor(cmp_[:, :, :], cmp_[:, :, :], eqm[:, :, :], ALU.add))
                        then(dve.tensor_reduce(rank[:, c, :], cmp_[:, :, :], AX.X, ALU.add))
                    then(dve.tensor_scalar(rank[:, :, :], rank[:, :, :], 1.5, None, ALU.is_lt))
                    then(dve.memset(sel[:, :, :], 0.0))
                    dve.tensor_copy(sel[:, 0:NQ, :], rank[:, 0:NQ, :])
                    dve.tensor_copy(sel[0:B, NQ, :], rank[0:B, NQ, :]).then_inc(sem["sel_ready"], 1)
                    dve.tensor_tensor(lg[:, :, :], lg[:, :, :], top[:, :, 0:1].to_broadcast([P, 3, E]), ALU.subtract) \
                        .then_inc(sem["route_arg"], 1)
                    htok_of(0)
                    htok_of(1)
                    dve.wait_ge(sem["route_exp"], 1)
                    then(dve.tensor_tensor(rank[:, :, :], rank[:, :, :], lg[:, :, :], ALU.mult))
                    then(dve.tensor_reduce(rsum[:, :], rank[:, :, :], AX.X, ALU.add))
                    then(dve.reciprocal(rsum[:, :], rsum[:, :]))
                    dve.tensor_tensor(rank[:, :, :], rank[:, :, :], bc(rsum[:, :], 2, [P, 3, E]), ALU.mult) \
                        .then_inc(sem["route_done"], 1)
                    dve.wait_ge(sem["counted"], 1)
                    then(dve.tensor_copy(place[:, :, :].rearrange("p c e -> p (c e)"), ms[:, 3, 0:4 * E]))
                    then(dve.tensor_reduce(most[:, :], place[:, 3, :], AX.X, ALU.max))
                    dve.tensor_scalar(flag[:, :], most[:, :], float(P), None, ALU.is_gt).then_inc(sem["flag_ready"], 1)
                    build(0)
                    htok_of(2)
                dve.wait_ge(sem["facc_zero"], l + 1)
                if l == 0:
                    dve.memset(gu[:, :, 0:2], 0.0).then_inc(sem["gu_ready"], 1)

                def expert(e, gated, last):
                    n0, q0 = N0["gu", l], Q0["gu", l]
                    gb = 0 if l % 2 == 0 else FT // MT

                    def gates(i):
                        split_lo(dve, n0 + 1, i, 2, e)
                        pair = (q0 + 1) % 2
                        split_lo(dve, n0 + 2, i, 2, e)
                        dve.wait_ge(sem["w_used"], n0 + 2 + 2 * i + EN * e)
                        dve.wait_ge(acc_free[q0 % 2], q0 // 2 + 1 + i + EQ // 2 * e)
                        up = acc[:, 2 * pair:2 * pair + 2, 0:T]
                        if gated:
                            dve.tensor_tensor(sg[:, :, :], sg[:, :, :], cbc[:, bass.ds(e, 1), :].to_broadcast([P, MT, T]),
                                              ALU.mult).then_inc(sem["sg_ready"], 1)
                            dve.wait_ge(sem["sg_ready"], 1 + i + FT // MT * e)
                        dve.tensor_tensor(gu[:, :, :], sg[:, :, :], up, ALU.mult).then_inc(sem["gu_ready"], 1)
                        dve.wait_ge(sem["g_hi"], gb + 1 + i + FT // MT * e)
                        dve.tensor_tensor(glo[:, bass.ds(2 * i, 2), :], gu[:, :, :],
                                          ghi[:, bass.ds(2 * i, 2), :].bitcast(F32), ALU.subtract) \
                            .then_inc(acc_free[pair], 1)
                    with dve.Fori(0, FT // MT) as i:
                        gates(i)
                    n1, q1 = N0["wd", l], Q0["wd", l]
                    C = 2 * len(KG)

                    def downs(i, last=False):
                        for g in range(2):
                            for s in range(len(KG)):
                                c = g * len(KG) + s
                                if not (last and c == C - 1):
                                    split_lo(dve, n1 + c + 1, i, C, e)
                            dve.wait_ge(sem["w_used"], n1 + g * len(KG) + len(KG) + C * i + EN * e)
                            pair = (q1 + g) % 2
                            f = facc[:, bass.ds(4 * i + 2 * g, 2), :]
                            dve.tensor_tensor(f, f, acc[:, 2 * pair:2 * pair + 2, 0:T], ALU.add) \
                                .then_inc(acc_free[pair], 1)
                    if last:
                        downs(0)
                        downs(1, True)
                    else:
                        with dve.Fori(0, KT // MT // 2) as i:
                            downs(i)

                if l % 2 == 0:
                    expert(0, False, False)
                else:
                    crowd = crowded(dve)
                    with dve.If(crowd):
                        dve.wait_ge(sem["combine_spread_ready"], E)
                        split_lo(dve, NX, 0)
                        with dve.Fori(0, E - 1) as e:
                            expert(e, True, False)
                        expert(E - 1, True, True)
                    with dve.Else():
                        def gathered_lo(e):
                            dve.wait_ge(sem["gathered_lo"], 1 + e)
                            dve.tensor_copy(hglo[:, :, :].rearrange("p k t -> p (k t)"), msf[:, D:2 * D]) \
                                .then_inc(sem["hg_lo"], 1)
                        split_lo3(dve, 0, 0, 0)
                        split_lo3(dve, 1, 0, 0)
                        gathered_lo(0)

                        def picked(half, two, last):
                            e = 2 * two + half

                            def turned(b, q):
                                dve.wait_ge(sem["gt_hi"], q + 1 + R3 * b + FP * e)
                                dst = bass.ds(MT * q + MT * R3 * b, MT)
                                dve.tensor_tensor(gtlo[:, dst, :],
                                                  ms[:, q % R3, 0:MT * P].rearrange("p (k t) -> p k t", k=MT),
                                                  gthi[:, dst, :].bitcast(F32), ALU.subtract).then_inc(sem["gt_lo"], 1)

                            def pair(b, q):
                                split_lo3(dve, 2 * q + 2, half, two, b)
                                if not (isinstance(b, int) and q == 0):
                                    turned(b, q - 1)
                                split_lo3(dve, 2 * q + 3, half, two, b)
                                dve.wait_ge(sem["gate_ready"], q + 1 + R3 * b + FP * e)
                                dve.wait_ge(sem["gu_turned"], q + 1 + R3 * b + FP * e)
                                dve.tensor_tensor(gus[:, :], sgs[:, :], acc[:, q % R3, CW:2 * CW], ALU.mult) \
                                    .then_inc(sem["gu_done"], 1)
                            pairs(dve, pair)
                            for d in range(FD):
                                if not (last and d >= FD - 2):
                                    split_lo3(dve, 2 * FP + d + 2, half, two)
                                if d == 0:
                                    turned(0, FP - 1)
                                if d == 2 and not last:
                                    dve.wait_ge(sem["gathered_lo"], 1 + e)
                                    dve.wait_ge(sem["gw_turned"], 1 + e)
                                    build(e + 1)
                            dve.wait_ge(sem["ys_hi"], 1 + e)
                            lo, hi = (b[:, :].rearrange("p (h c) -> p h c", h=2) for b in (yslo, yshi))
                            dve.scalar_tensor_tensor(out=lo, in0=acc[:, 2:4, :], scalar=weight[:, 0:1],
                                                     in1=hi.bitcast(F32), op0=ALU.mult, op1=ALU.subtract) \
                                .then_inc(sem["ys_ready"], 1)
                            if not last:
                                gathered_lo(e + 1)
                            for k in range(4):
                                dve.wait_ge(sem["scattered"], k + 1 + 4 * e)
                                b0 = 2 * (k % 2)
                                f = facc[:, 2 * k:2 * k + 2, :]
                                dve.tensor_tensor(f, f, acc[:, b0:b0 + 2, 0:T], ALU.add).then_inc(sem["scat_added"], 1)
                        by_twos(dve, picked)
                    dve.drain().then_inc(sem["moe_done"], 1)
                add_normed(l, 1, 4 * l + 4, facc)
                dve.wait_ge(sem["x_ready"], 4 * l + 4)

            for c in range(NQ + 1):
                rows = Q if c < NQ else B
                dve.wait_ge(sem["y_turned"], c + 1)
                dve.tensor_copy(xtok[0:rows, c * D:(c + 1) * D], msf[0:rows, (c % 2) * D:(c % 2 + 1) * D]) \
                    .then_inc(sem["y_copied"], 1)


_VECTORS = ["b_mod", "mix_pre_g", "mix_post_g", "ffn_pre_g", "ffn_post_g", "conv_b", "ssm_norm_g", "cmlp_ln_g",
            "cmlp_ln_b"]


def kernel(**inputs):
    import numpy as _np
    import concourse.bacc as _bacc
    from concourse import mybir as _mybir
    from concourse.bass_utils import run_bass_kernel_spmd as _run

    nc = _bacc.Bacc("TRN2", target_bir_lowering=False, num_devices=1)
    arrays, args = {}, {}
    for name, a in inputs.items():
        a = _np.ascontiguousarray(a)
        arrays[f"in_{name}_dram"] = a
        args[name] = nc.dram_tensor(f"in_{name}_dram", a.shape, _mybir.dt.from_np(a.dtype), kind="ExternalInput").ap()
    depth, samples, heads, head_dim, states = inputs["state_ssm"].shape
    _, _, rows, conv_dim = inputs["state_conv"].shape
    batch, seq, width = inputs["x_prompt"].shape
    outs = {
        "y_p": (batch, seq, width), "y_s": tuple(inputs["x_sample"].shape),
        "ssm_p": (depth, batch, heads, head_dim, states), "conv_p": (depth, batch, rows, conv_dim),
        "ssm_s": (depth, samples, heads, head_dim, states), "conv_s": (depth, samples, rows, conv_dim),
        "v_s": (depth, samples, 1, width),
    }
    handles = {name: nc.dram_tensor(f"out_{name}_dram", shape, _mybir.dt.float32, kind="ExternalOutput").ap()
               for name, shape in outs.items()}
    args["vectors"] = {name: args[name] for name in _VECTORS}
    hybrid_ssd_chunkmlp_moe_step(nc, args, handles)
    r = _run(nc, [arrays], core_ids=[0])
    return tuple(r.results[0][f"out_{name}_dram"] for name in outs)
```
